# Optimizing a Trainium2 kernel written in Bass

```python
import math
import numpy as np
import jax
import jax.numpy as jnp
from jax import lax
import jax, jax.numpy as jnp

D_MODEL = 1024
BATCH = 1
SEQ = 256
DEPTH = 1

HEAD_DIM = 64
ROPE_DIM = HEAD_DIM // 4
ROPE_THETA = 500000.0
DIFF_HEADS = 4
DIFF_V_DIM = 2 * HEAD_DIM
NSA_HEADS = 8
NSA_KV_HEADS = 2
NSA_GROUP = NSA_HEADS // NSA_KV_HEADS
N_BRANCH = 3
CMP_BLOCK = 32
CMP_STRIDE = 16
CMP_HIDDEN = 4 * HEAD_DIM
SEL_BLOCK = 64
SEL_TOP_N = 16
WINDOW = 512
D_FF = 2816
Q_BLOCK = 128
SEL_Q_CHUNK = 64
MIX_WIDTH = DIFF_HEADS * DIFF_V_DIM + NSA_HEADS * HEAD_DIM
IN_SIZES = (DIFF_HEADS * 2 * HEAD_DIM, DIFF_HEADS * 2 * HEAD_DIM, DIFF_HEADS * DIFF_V_DIM,
            NSA_HEADS * HEAD_DIM) + (NSA_KV_HEADS * HEAD_DIM,) * 6 + (NSA_HEADS * N_BRANCH,)
IN_WIDTH = sum(IN_SIZES)
EPS = 1e-6
NEG_INF = -1e30
FORCE_SCORE = 1e9


def rms_norm(x, g):
    xf = x.astype(jnp.float32)
    y = xf * lax.rsqrt(jnp.mean(xf * xf, axis=-1, keepdims=True) + EPS)
    return (y * g.astype(jnp.float32)).astype(x.dtype)

def rope_tables(S):
    pos = jnp.arange(S, dtype=jnp.float32)
    inv = ROPE_THETA ** (-jnp.arange(0, ROPE_DIM, 2, dtype=jnp.float32) / ROPE_DIM)
    ang = pos[:, None] * inv[None, :]
    return jnp.cos(ang), jnp.sin(ang)

def partial_rope(x, cos, sin):
    xr = x[..., :ROPE_DIM].astype(jnp.float32)
    x1, x2 = xr[..., :ROPE_DIM // 2], xr[..., ROPE_DIM // 2:]
    rot = jnp.concatenate([x1 * cos - x2 * sin, x2 * cos + x1 * sin], axis=-1)
    return jnp.concatenate([rot.astype(x.dtype), x[..., ROPE_DIM:]], axis=-1)

def swiglu(h, w_gate, w_up, w_down):
    return (jax.nn.silu(h @ w_gate) * (h @ w_up)) @ w_down

def diff_attention(q, k, v, lam, subln_g, lambda_init):
    B, Hd, _, S, dh = q.shape
    nb = S // Q_BLOCK
    scale = dh ** -0.5
    qb = q.reshape(B, Hd, 2, nb, Q_BLOCK, dh).transpose(3, 0, 1, 2, 4, 5)
    kpos = jnp.arange(S)

    def block(args):
        qi, i = args
        s = jnp.einsum('bhmqd,bhmkd->bhmqk', qi, k).astype(jnp.float32) * scale
        qpos = i * Q_BLOCK + jnp.arange(Q_BLOCK)
        s = jnp.where(kpos[None, :] <= qpos[:, None], s, NEG_INF)
        p = jax.nn.softmax(s, axis=-1)
        a = p[:, :, 0] - lam * p[:, :, 1]
        return jnp.einsum('bhqk,bhkd->bhqd', a.astype(v.dtype), v)

    o = lax.map(block, (qb, jnp.arange(nb)))
    o = o.transpose(1, 2, 0, 3, 4).reshape(B, Hd, S, 2 * dh)
    o = rms_norm(o, subln_g) * (1.0 - lambda_init)
    return o.transpose(0, 2, 1, 3).reshape(B, S, Hd * 2 * dh)

def compress(x, pe, w1, w2):
    B, G, S, dh = x.shape
    r = CMP_BLOCK // CMP_STRIDE
    nc = S // CMP_STRIDE - r + 1
    sub = x.reshape(B, G, S // CMP_STRIDE, CMP_STRIDE, dh)
    blocks = jnp.concatenate([sub[:, :, j:j + nc] for j in range(r)], axis=3)
    blocks = (blocks + pe).reshape(B, G, nc, CMP_BLOCK * dh)
    return jax.nn.gelu(blocks @ w1) @ w2

def sel_overlap(nc, n_sel):
    cs = np.arange(nc)[:, None] * CMP_STRIDE
    ss = np.arange(n_sel)[None, :] * SEL_BLOCK
    ov = np.minimum(cs + CMP_BLOCK, ss + SEL_BLOCK) - np.maximum(cs, ss)
    return jnp.asarray(np.clip(ov, 0, None) / CMP_BLOCK, dtype=jnp.float32)

def nsa_attention(q, k_cmp, v_cmp, k_sel, v_sel, k_win, v_win, gates,
                  pe_k, wk1, wk2, pe_v, wv1, wv2):
    B, H, S, dh = q.shape
    G, Hg = NSA_KV_HEADS, NSA_GROUP
    scale = dh ** -0.5
    qg = q.reshape(B, G, Hg, S, dh)
    t = jnp.arange(S)

    kc = compress(k_cmp, pe_k, wk1, wk2)
    vc = compress(v_cmp, pe_v, wv1, wv2)
    nc = kc.shape[2]
    cend = jnp.arange(nc) * CMP_STRIDE + CMP_BLOCK - 1
    cvalid = cend[None, :] <= t[:, None]
    s = jnp.einsum('bghsd,bgcd->bghsc', qg, kc).astype(jnp.float32) * scale
    p_cmp = jnp.where(cvalid, jax.nn.softmax(jnp.where(cvalid, s, NEG_INF), axis=-1), 0.0)
    o_cmp = jnp.einsum('bghsc,bgcd->bghsd', p_cmp.astype(vc.dtype), vc)

    n_sel = S // SEL_BLOCK
    top_n = min(SEL_TOP_N, n_sel)
    imp = jnp.einsum('bghsc,cj->bgsj', p_cmp, sel_overlap(nc, n_sel))
    blk = jnp.arange(n_sel)[None, :]
    cur = (t // SEL_BLOCK)[:, None]
    causal_blk = blk * SEL_BLOCK <= t[:, None]
    forced = (blk == 0) | ((blk <= cur) & (blk >= cur - 1))
    imp = jnp.where(forced, FORCE_SCORE, jnp.where(causal_blk, imp, -1.0))
    _, idx = lax.top_k(imp, top_n)

    kb = k_sel.reshape(B, G, n_sel, SEL_BLOCK, dh)
    vb = v_sel.reshape(B, G, n_sel, SEL_BLOCK, dh)
    C = SEL_Q_CHUNK
    nq = S // C
    q_c = qg.reshape(B, G, Hg, nq, C, dh).transpose(3, 0, 1, 2, 4, 5)
    idx_c = idx.reshape(B, G, nq, C, top_n).transpose(2, 0, 1, 3, 4)
    bi = jnp.arange(B)[:, None, None, None]
    gi = jnp.arange(G)[None, :, None, None]

    def sel_chunk(args):
        qi, ii, c = args
        ks = kb[bi, gi, ii]
        vs = vb[bi, gi, ii]
        s = jnp.einsum('bghqd,bgqnld->bghqnl', qi, ks).astype(jnp.float32) * scale
        kpos = ii[..., None] * SEL_BLOCK + jnp.arange(SEL_BLOCK)
        qpos = c * C + jnp.arange(C)
        mask = kpos <= qpos[None, None, :, None, None]
        s = jnp.where(mask[:, :, None], s, NEG_INF).reshape(B, G, Hg, C, top_n * SEL_BLOCK)
        p = jax.nn.softmax(s, axis=-1).reshape(B, G, Hg, C, top_n, SEL_BLOCK)
        return jnp.einsum('bghqnl,bgqnld->bghqd', p.astype(vs.dtype), vs)

    o_sel = lax.map(sel_chunk, (q_c, idx_c, jnp.arange(nq)))
    o_sel = o_sel.transpose(1, 2, 3, 0, 4, 5).reshape(B, G, Hg, S, dh)

    nb = S // Q_BLOCK
    span = WINDOW + Q_BLOCK
    kp = jnp.pad(k_win, ((0, 0), (0, 0), (WINDOW, 0), (0, 0)))
    vp = jnp.pad(v_win, ((0, 0), (0, 0), (WINDOW, 0), (0, 0)))
    q_w = qg.reshape(B, G, Hg, nb, Q_BLOCK, dh).transpose(3, 0, 1, 2, 4, 5)

    def win_block(args):
        qi, i = args
        start = i * Q_BLOCK
        ks = lax.dynamic_slice_in_dim(kp, start, span, axis=2)
        vs = lax.dynamic_slice_in_dim(vp, start, span, axis=2)
        s = jnp.einsum('bghqd,bgkd->bghqk', qi, ks).astype(jnp.float32) * scale
        qpos = start + jnp.arange(Q_BLOCK)
        kpos = start - WINDOW + jnp.arange(span)
        d = qpos[:, None] - kpos[None, :]
        mask = (d >= 0) & (d < WINDOW) & (kpos[None, :] >= 0)
        p = jax.nn.softmax(jnp.where(mask, s, NEG_INF), axis=-1)
        return jnp.einsum('bghqk,bgkd->bghqd', p.astype(vs.dtype), vs)

    o_win = lax.map(win_block, (q_w, jnp.arange(nb)))
    o_win = o_win.transpose(1, 2, 3, 0, 4, 5).reshape(B, G, Hg, S, dh)

    o = gates[..., 0:1] * o_cmp + gates[..., 1:2] * o_sel + gates[..., 2:3] * o_win
    return o.transpose(0, 3, 1, 2, 4).reshape(B, S, H * dh)

def hybrid_mixer(h, w_in, lambda_q1, lambda_k1, lambda_q2, lambda_k2, diff_subln,
                 cmp_pe_k, cmp_k_w1, cmp_k_w2, cmp_pe_v, cmp_v_w1, cmp_v_w2, w_out, lambda_init):
    B, S, _ = h.shape
    dh = HEAD_DIM
    cos, sin = rope_tables(S)
    pts = [int(v) for v in np.cumsum(IN_SIZES)[:-1]]
    dq, dk, dv, nq, kc, vc, ks, vs, kw, vw, gl = jnp.split(h @ w_in, pts, axis=-1)

    dq = partial_rope(dq.reshape(B, S, DIFF_HEADS, 2, dh).transpose(0, 2, 3, 1, 4), cos, sin)
    dk = partial_rope(dk.reshape(B, S, DIFF_HEADS, 2, dh).transpose(0, 2, 3, 1, 4), cos, sin)
    dv = dv.reshape(B, S, DIFF_HEADS, DIFF_V_DIM).transpose(0, 2, 1, 3)
    lq1, lk1 = lambda_q1.astype(jnp.float32), lambda_k1.astype(jnp.float32)
    lq2, lk2 = lambda_q2.astype(jnp.float32), lambda_k2.astype(jnp.float32)
    lam = jnp.exp(jnp.sum(lq1 * lk1)) - jnp.exp(jnp.sum(lq2 * lk2)) + lambda_init
    o_diff = diff_attention(dq, dk, dv, lam, diff_subln, lambda_init)

    def kv_heads(a):
        return a.reshape(B, S, NSA_KV_HEADS, dh).transpose(0, 2, 1, 3)
    nq = partial_rope(nq.reshape(B, S, NSA_HEADS, dh).transpose(0, 2, 1, 3), cos, sin)
    gates = jax.nn.sigmoid(gl.reshape(B, S, NSA_HEADS, N_BRANCH)).transpose(0, 2, 1, 3)
    gates = gates.reshape(B, NSA_KV_HEADS, NSA_GROUP, S, N_BRANCH)
    o_nsa = nsa_attention(nq, kv_heads(kc), kv_heads(vc),
                          partial_rope(kv_heads(ks), cos, sin), kv_heads(vs),
                          partial_rope(kv_heads(kw), cos, sin), kv_heads(vw), gates,
                          cmp_pe_k, cmp_k_w1, cmp_k_w2, cmp_pe_v, cmp_v_w1, cmp_v_w2)

    return jnp.concatenate([o_diff, o_nsa], axis=-1) @ w_out

def first_inputs(seed: int = 0) -> dict:
    key = jax.random.key(seed)
    ks = jax.random.split(key, 26)
    f32 = jnp.float32
    L = DEPTH

    def w(k, shape, fan_in):
        return jax.random.normal(k, shape, f32) * fan_in ** -0.5

    def gain(k, n):
        return 1.0 + 0.1 * jax.random.normal(k, (L, n), f32)

    return {
        'x': jax.random.normal(ks[0], (BATCH, SEQ, D_MODEL), f32),
        'ff1_norm_pre': gain(ks[1], D_MODEL),
        'ff1_w_gate': w(ks[2], (L, D_MODEL, D_FF), D_MODEL),
        'ff1_w_up': w(ks[3], (L, D_MODEL, D_FF), D_MODEL),
        'ff1_w_down': w(ks[4], (L, D_FF, D_MODEL), D_FF),
        'ff1_norm_post': gain(ks[5], D_MODEL),
        'mix_norm_pre': gain(ks[6], D_MODEL),
        'w_in': w(ks[7], (L, D_MODEL, IN_WIDTH), D_MODEL),
        'lambda_q1': 0.1 * jax.random.normal(ks[8], (L, HEAD_DIM), f32),
        'lambda_k1': 0.1 * jax.random.normal(ks[9], (L, HEAD_DIM), f32),
        'lambda_q2': 0.1 * jax.random.normal(ks[10], (L, HEAD_DIM), f32),
        'lambda_k2': 0.1 * jax.random.normal(ks[11], (L, HEAD_DIM), f32),
        'diff_subln': gain(ks[12], DIFF_V_DIM),
        'cmp_pe_k': 0.1 * jax.random.normal(ks[13], (L, CMP_BLOCK, HEAD_DIM), f32),
        'cmp_k_w1': w(ks[14], (L, CMP_BLOCK * HEAD_DIM, CMP_HIDDEN), CMP_BLOCK * HEAD_DIM),
        'cmp_k_w2': w(ks[15], (L, CMP_HIDDEN, HEAD_DIM), CMP_HIDDEN),
        'cmp_pe_v': 0.1 * jax.random.normal(ks[16], (L, CMP_BLOCK, HEAD_DIM), f32),
        'cmp_v_w1': w(ks[17], (L, CMP_BLOCK * HEAD_DIM, CMP_HIDDEN), CMP_BLOCK * HEAD_DIM),
        'cmp_v_w2': w(ks[18], (L, CMP_HIDDEN, HEAD_DIM), CMP_HIDDEN),
        'w_out': w(ks[19], (L, MIX_WIDTH, D_MODEL), MIX_WIDTH),
        'mix_norm_post': gain(ks[20], D_MODEL),
        'ff2_norm_pre': gain(ks[21], D_MODEL),
        'ff2_w_gate': w(ks[22], (L, D_MODEL, D_FF), D_MODEL),
        'ff2_w_up': w(ks[23], (L, D_MODEL, D_FF), D_MODEL),
        'ff2_w_down': w(ks[24], (L, D_FF, D_MODEL), D_FF),
        'ff2_norm_post': gain(ks[25], D_MODEL),
    }

def first_block(x, ff1_norm_pre, ff1_w_gate, ff1_w_up, ff1_w_down, ff1_norm_post,
              mix_norm_pre, w_in, lambda_q1, lambda_k1, lambda_q2, lambda_k2, diff_subln,
              cmp_pe_k, cmp_k_w1, cmp_k_w2, cmp_pe_v, cmp_v_w1, cmp_v_w2, w_out, mix_norm_post,
              ff2_norm_pre, ff2_w_gate, ff2_w_up, ff2_w_down, ff2_norm_post):
    for l in range(DEPTH):
        lambda_init = 0.8 - 0.6 * math.exp(-0.3 * l)
        h = swiglu(rms_norm(x, ff1_norm_pre[l]), ff1_w_gate[l], ff1_w_up[l], ff1_w_down[l])
        x = x + 0.5 * rms_norm(h, ff1_norm_post[l])
        h = hybrid_mixer(rms_norm(x, mix_norm_pre[l]), w_in[l], lambda_q1[l], lambda_k1[l],
                         lambda_q2[l], lambda_k2[l], diff_subln[l], cmp_pe_k[l], cmp_k_w1[l],
                         cmp_k_w2[l], cmp_pe_v[l], cmp_v_w1[l], cmp_v_w2[l], w_out[l], lambda_init)
        x = x + rms_norm(h, mix_norm_post[l])
        h = swiglu(rms_norm(x, ff2_norm_pre[l]), ff2_w_gate[l], ff2_w_up[l], ff2_w_down[l])
        x = x + 0.5 * rms_norm(h, ff2_norm_post[l])
    return x


DEPTH_2 = 2

ATTN_HEADS = 16
ATTN_KV_HEADS = 4
ATTN_GROUP = ATTN_HEADS // ATTN_KV_HEADS
ATTN_HEAD_DIM = 64
ATTN_Q_DIM = ATTN_HEADS * ATTN_HEAD_DIM
ATTN_KV_DIM = ATTN_KV_HEADS * ATTN_HEAD_DIM
ATTN_IN_DIM = ATTN_Q_DIM + 2 * ATTN_KV_DIM
WINDOW_2 = 128
ATTN_BLOCK = 128
ROPE_DIM_2 = ATTN_HEAD_DIM // 4

GDN_QK_HEADS = 8
GDN_V_HEADS = 16
GDN_HEAD_K = 128
GDN_HEAD_V = 128
GDN_CONV = 4
GDN_CHUNK = 64
GDN_KEY_DIM = GDN_QK_HEADS * GDN_HEAD_K
GDN_VAL_DIM = GDN_V_HEADS * GDN_HEAD_V
GDN_QKV_DIM = 2 * GDN_KEY_DIM + GDN_VAL_DIM
GDN_IN_DIM = GDN_QKV_DIM + GDN_VAL_DIM + 2 * GDN_V_HEADS

D_FF_2 = 3 * D_MODEL
FFN_CONV = 3

N_ATTN_LAYERS = (DEPTH_2 + 1) // 2
N_GDN_LAYERS = DEPTH_2 // 2


def rms_norm_2(x, gain):
    xf = x.astype(jnp.float32)
    y = xf * lax.rsqrt(jnp.mean(xf * xf, axis=-1, keepdims=True) + EPS)
    return (y * gain.astype(jnp.float32)).astype(x.dtype)

def l2_norm(x):
    return x * lax.rsqrt(jnp.sum(x * x, axis=-1, keepdims=True) + EPS)

def causal_dwconv(x, w):
    k = w.shape[0]
    return lax.conv_general_dilated(
        x, w[:, None, :].astype(x.dtype), window_strides=(1,), padding=[(k - 1, 0)],
        dimension_numbers=("NWC", "WIO", "NWC"), feature_group_count=x.shape[-1])

def rope_tables_2(positions):
    inv_freq = ROPE_THETA ** (-jnp.arange(0, ROPE_DIM_2, 2, dtype=jnp.float32) / ROPE_DIM_2)
    ang = positions.astype(jnp.float32)[..., None] * inv_freq
    return jnp.cos(ang)[:, :, None, :], jnp.sin(ang)[:, :, None, :]

def partial_rope_2(x, cos, sin):
    cos = cos.astype(x.dtype)
    sin = sin.astype(x.dtype)
    half = ROPE_DIM_2 // 2
    x1, x2, xp = x[..., :half], x[..., half:ROPE_DIM_2], x[..., ROPE_DIM_2:]
    return jnp.concatenate([x1 * cos - x2 * sin, x2 * cos + x1 * sin, xp], axis=-1)

def swa_sink_attention(u, w_in, q_gain, k_gain, sinks, w_out, cos, sin):
    B, S, _ = u.shape
    nb = S // ATTN_BLOCK
    blk, hkv, g, hd = ATTN_BLOCK, ATTN_KV_HEADS, ATTN_GROUP, ATTN_HEAD_DIM
    qkv = u @ w_in
    q = qkv[..., :ATTN_Q_DIM].reshape(B, S, ATTN_HEADS, hd)
    k = qkv[..., ATTN_Q_DIM:ATTN_Q_DIM + ATTN_KV_DIM].reshape(B, S, hkv, hd)
    v = qkv[..., ATTN_Q_DIM + ATTN_KV_DIM:].reshape(B, S, hkv, hd)
    q = partial_rope_2(rms_norm_2(q, q_gain), cos, sin)
    k = partial_rope_2(rms_norm_2(k, k_gain), cos, sin)
    qb = q.reshape(B, nb, blk, hkv, g, hd)

    def band(t):
        prev = jnp.pad(t, ((0, 0), (blk, 0), (0, 0), (0, 0)))[:, :S]
        return jnp.concatenate([prev.reshape(B, nb, blk, hkv, hd),
                                t.reshape(B, nb, blk, hkv, hd)], axis=2)

    kb, vb = band(k), band(v)
    scores = jnp.einsum("bnqhgd,bnkhd->bnhgqk", qb, kb,
                        preferred_element_type=jnp.float32) * (hd ** -0.5)
    dist = jnp.arange(blk)[:, None] + blk - jnp.arange(2 * blk)[None, :]
    in_window = (dist >= 0) & (dist < WINDOW_2)
    key_pos = jnp.arange(nb)[:, None] * blk - blk + jnp.arange(2 * blk)[None, :]
    mask = in_window[None] & (key_pos >= 0)[:, None, :]
    scores = jnp.where(mask[None, :, None, None], scores, jnp.finfo(jnp.float32).min)
    sink = jnp.broadcast_to(sinks.astype(jnp.float32).reshape(1, 1, hkv, g, 1, 1),
                            scores.shape[:-1] + (1,))
    probs = jax.nn.softmax(jnp.concatenate([scores, sink], axis=-1), axis=-1)[..., :-1]
    out = jnp.einsum("bnhgqk,bnkhd->bnqhgd", probs.astype(vb.dtype), vb)
    return out.reshape(B, S, ATTN_Q_DIM) @ w_out

def chunk_gated_delta_rule(q, k, v, g, beta):
    out_dtype = v.dtype
    B, S, H, DK = q.shape
    DV = v.shape[-1]
    C = GDN_CHUNK
    nc = S // C
    f32 = jnp.float32

    def chunks(t):
        t = t.astype(f32).reshape((B, nc, C, H) + t.shape[3:])
        return jnp.moveaxis(t, 3, 1)

    q, k, v, g, beta = chunks(q), chunks(k), chunks(v), chunks(g), chunks(beta)
    gc = jnp.cumsum(g, axis=-1)
    incl = jnp.tril(jnp.ones((C, C), dtype=bool))
    strict = jnp.tril(jnp.ones((C, C), dtype=bool), k=-1)
    decay = jnp.exp(jnp.where(incl, gc[..., :, None] - gc[..., None, :], -jnp.inf))
    kk = jnp.einsum("bhncd,bhnsd->bhncs", k, k)
    m = jnp.where(strict, beta[..., :, None] * kk * decay, 0.0)
    a = m + jnp.eye(C, dtype=f32)
    rhs = jnp.concatenate([v * beta[..., None], k * (beta * jnp.exp(gc))[..., None]], axis=-1)
    sol = lax.linalg.triangular_solve(a, rhs, left_side=True, lower=True, unit_diagonal=True)
    u, w = sol[..., :DV], sol[..., DV:]
    qk = jnp.where(incl, jnp.einsum("bhncd,bhnsd->bhncs", q, k) * decay, 0.0)
    q_dec = q * jnp.exp(gc)[..., None]
    k_dec = k * jnp.exp(gc[..., -1:] - gc)[..., None]
    g_last = jnp.exp(gc[..., -1])

    def step(state, inp):
        u_c, w_c, qk_c, qd_c, kd_c, gl_c = inp
        v_new = u_c - jnp.einsum("bhcd,bhde->bhce", w_c, state)
        o = jnp.einsum("bhcd,bhde->bhce", qd_c, state) + jnp.einsum("bhcs,bhse->bhce", qk_c, v_new)
        state = state * gl_c[..., None, None] + jnp.einsum("bhcd,bhce->bhde", kd_c, v_new)
        return state, o

    xs = tuple(jnp.moveaxis(t, 2, 0) for t in (u, w, qk, q_dec, k_dec, g_last))
    _, o = lax.scan(step, jnp.zeros((B, H, DK, DV), f32), xs)
    o = jnp.transpose(o, (1, 0, 3, 2, 4)).reshape(B, S, H, DV)
    return o.astype(out_dtype)

def gated_deltanet(u, w_in, conv_w, a_log, dt_bias, norm_gain, w_out):
    B, S, _ = u.shape
    proj = u @ w_in
    qkv = jax.nn.silu(causal_dwconv(proj[..., :GDN_QKV_DIM], conv_w))
    z = proj[..., GDN_QKV_DIM:GDN_QKV_DIM + GDN_VAL_DIM].reshape(B, S, GDN_V_HEADS, GDN_HEAD_V)
    b = proj[..., GDN_QKV_DIM + GDN_VAL_DIM:GDN_QKV_DIM + GDN_VAL_DIM + GDN_V_HEADS]
    a = proj[..., GDN_QKV_DIM + GDN_VAL_DIM + GDN_V_HEADS:]
    rep = GDN_V_HEADS // GDN_QK_HEADS
    q = qkv[..., :GDN_KEY_DIM].reshape(B, S, GDN_QK_HEADS, GDN_HEAD_K).astype(jnp.float32)
    k = qkv[..., GDN_KEY_DIM:2 * GDN_KEY_DIM].reshape(B, S, GDN_QK_HEADS, GDN_HEAD_K).astype(jnp.float32)
    v = qkv[..., 2 * GDN_KEY_DIM:].reshape(B, S, GDN_V_HEADS, GDN_HEAD_V)
    q = jnp.repeat(l2_norm(q) * (GDN_HEAD_K ** -0.5), rep, axis=2)
    k = jnp.repeat(l2_norm(k), rep, axis=2)
    beta = jax.nn.sigmoid(b.astype(jnp.float32))
    g = -jnp.exp(a_log.astype(jnp.float32)) * jax.nn.softplus(
        a.astype(jnp.float32) + dt_bias.astype(jnp.float32))
    o = chunk_gated_delta_rule(q, k, v, g, beta)
    o = rms_norm_2(o, norm_gain) * jax.nn.silu(z)
    return o.reshape(B, S, GDN_VAL_DIM) @ w_out

def conv_glu_ffn(u, w_up, conv_w, conv_b, w_down):
    gu = u @ w_up
    gate = causal_dwconv(gu[..., :D_FF_2], conv_w) + conv_b
    return (jax.nn.silu(gate) * gu[..., D_FF_2:]) @ w_down

def second_inputs(seed: int = 0) -> dict:
    key = jax.random.key(seed)
    ks = jax.random.split(key, 24)
    f32 = jnp.float32

    def nrm(k, shape, scale):
        return jax.random.normal(k, shape, f32) * scale

    x = nrm(ks[0], (BATCH, SEQ, D_MODEL), 1.0)
    start = jax.random.randint(ks[1], (BATCH, 1), 0, 4096, dtype=jnp.int32)
    positions = start + jnp.arange(SEQ, dtype=jnp.int32)[None, :]
    mixer_norm = 1.0 + nrm(ks[2], (DEPTH_2, D_MODEL), 0.05)
    ffn_norm = 1.0 + nrm(ks[3], (DEPTH_2, D_MODEL), 0.05)

    attn_w_in = nrm(ks[4], (N_ATTN_LAYERS, D_MODEL, ATTN_IN_DIM), D_MODEL ** -0.5)
    attn_q_gain = 1.0 + nrm(ks[5], (N_ATTN_LAYERS, ATTN_HEAD_DIM), 0.05)
    attn_k_gain = 1.0 + nrm(ks[6], (N_ATTN_LAYERS, ATTN_HEAD_DIM), 0.05)
    attn_sinks = nrm(ks[7], (N_ATTN_LAYERS, ATTN_HEADS), 1.0)
    attn_w_out = nrm(ks[8], (N_ATTN_LAYERS, ATTN_Q_DIM, D_MODEL), ATTN_Q_DIM ** -0.5)

    gdn_w_in = nrm(ks[9], (N_GDN_LAYERS, D_MODEL, GDN_IN_DIM), D_MODEL ** -0.5)
    gdn_conv = nrm(ks[10], (N_GDN_LAYERS, GDN_CONV, GDN_QKV_DIM), GDN_CONV ** -0.5)
    gdn_a_log = jnp.log(jax.random.uniform(ks[11], (N_GDN_LAYERS, GDN_V_HEADS), f32, 1.0, 16.0))
    dt = jnp.exp(jax.random.uniform(ks[12], (N_GDN_LAYERS, GDN_V_HEADS), f32,
                                    math.log(1e-3), math.log(1e-1)))
    gdn_dt_bias = dt + jnp.log(-jnp.expm1(-dt))
    gdn_norm = 1.0 + nrm(ks[13], (N_GDN_LAYERS, GDN_HEAD_V), 0.05)
    gdn_w_out = nrm(ks[14], (N_GDN_LAYERS, GDN_VAL_DIM, D_MODEL), GDN_VAL_DIM ** -0.5)

    ffn_w_up = nrm(ks[15], (DEPTH_2, D_MODEL, 2 * D_FF_2), D_MODEL ** -0.5)
    ffn_conv = nrm(ks[16], (DEPTH_2, FFN_CONV, D_FF_2), FFN_CONV ** -0.5)
    ffn_conv_b = nrm(ks[17], (DEPTH_2, D_FF_2), 0.02)
    ffn_w_down = nrm(ks[18], (DEPTH_2, D_FF_2, D_MODEL), D_FF_2 ** -0.5)
    return {"x": x, "positions": positions, "mixer_norm": mixer_norm, "ffn_norm": ffn_norm,
            "attn_w_in": attn_w_in, "attn_q_gain": attn_q_gain, "attn_k_gain": attn_k_gain,
            "attn_sinks": attn_sinks, "attn_w_out": attn_w_out,
            "gdn_w_in": gdn_w_in, "gdn_conv": gdn_conv, "gdn_a_log": gdn_a_log,
            "gdn_dt_bias": gdn_dt_bias, "gdn_norm": gdn_norm, "gdn_w_out": gdn_w_out,
            "ffn_w_up": ffn_w_up, "ffn_conv": ffn_conv, "ffn_conv_b": ffn_conv_b,
            "ffn_w_down": ffn_w_down}

def second_block(x, positions, mixer_norm, ffn_norm, attn_w_in, attn_q_gain, attn_k_gain,
              attn_sinks, attn_w_out, gdn_w_in, gdn_conv, gdn_a_log, gdn_dt_bias, gdn_norm,
              gdn_w_out, ffn_w_up, ffn_conv, ffn_conv_b, ffn_w_down):
    cos, sin = rope_tables_2(positions)
    h = x
    for i in range(DEPTH_2):
        j = i // 2
        u = rms_norm_2(h, mixer_norm[i])
        if i % 2 == 0:
            h = h + swa_sink_attention(u, attn_w_in[j], attn_q_gain[j], attn_k_gain[j],
                                       attn_sinks[j], attn_w_out[j], cos, sin)
        else:
            h = h + gated_deltanet(u, gdn_w_in[j], gdn_conv[j], gdn_a_log[j], gdn_dt_bias[j],
                                   gdn_norm[j], gdn_w_out[j])
        u = rms_norm_2(h, ffn_norm[i])
        h = h + conv_glu_ffn(u, ffn_w_up[i], ffn_conv[i], ffn_conv_b[i], ffn_w_down[i])
    return h


def setup_inputs(seed=0):
    out = dict(first_inputs(seed))
    for name, value in second_inputs(seed + 1).items():
        if name != "x":
            out[name + "_2"] = value
    return out


def reference(
    x, ff1_norm_pre, ff1_w_gate, ff1_w_up, ff1_w_down, ff1_norm_post, mix_norm_pre, w_in,
    lambda_q1, lambda_k1, lambda_q2, lambda_k2, diff_subln, cmp_pe_k, cmp_k_w1, cmp_k_w2,
    cmp_pe_v, cmp_v_w1, cmp_v_w2, w_out, mix_norm_post, ff2_norm_pre, ff2_w_gate, ff2_w_up,
    ff2_w_down, ff2_norm_post, positions_2, mixer_norm_2, ffn_norm_2, attn_w_in_2,
    attn_q_gain_2, attn_k_gain_2, attn_sinks_2, attn_w_out_2, gdn_w_in_2, gdn_conv_2,
    gdn_a_log_2, gdn_dt_bias_2, gdn_norm_2, gdn_w_out_2, ffn_w_up_2, ffn_conv_2, ffn_conv_b_2,
    ffn_w_down_2,
):
    x = first_block(
        x, ff1_norm_pre, ff1_w_gate, ff1_w_up, ff1_w_down, ff1_norm_post, mix_norm_pre, w_in,
        lambda_q1, lambda_k1, lambda_q2, lambda_k2, diff_subln, cmp_pe_k, cmp_k_w1, cmp_k_w2,
        cmp_pe_v, cmp_v_w1, cmp_v_w2, w_out, mix_norm_post, ff2_norm_pre, ff2_w_gate, ff2_w_up,
        ff2_w_down, ff2_norm_post,
    )
    return second_block(
        x, positions_2, mixer_norm_2, ffn_norm_2, attn_w_in_2, attn_q_gain_2, attn_k_gain_2,
        attn_sinks_2, attn_w_out_2, gdn_w_in_2, gdn_conv_2, gdn_a_log_2, gdn_dt_bias_2,
        gdn_norm_2, gdn_w_out_2, ffn_w_up_2, ffn_conv_2, ffn_conv_b_2, ffn_w_down_2,
    )


_drawn_inputs = setup_inputs


def setup_inputs(seed=0):
    import zlib

    import numpy as np

    out = dict(_drawn_inputs(seed))
    spreads = {}
    factors = {'lambda_k1': 8.0,
     'lambda_q2': 8.0,
     'cmp_pe_k': 8.0,
     'attn_q_gain_2': 7.648,
     'attn_k_gain_2': 8.0,
     'gdn_norm_2': 3.486,
     'ffn_conv_b_2': 5.572,
     'attn_sinks_2': 8.0}
    for name, (base, spread) in spreads.items():
        noise = np.random.default_rng([zlib.crc32(name.encode()), seed]).standard_normal(out[name].shape)
        drawn = base * np.exp(spread * noise) if base else spread * noise
        out[name] = jnp.asarray(drawn.astype(out[name].dtype))
    for name, factor in factors.items():
        out[name] = (out[name] * factor).astype(out[name].dtype)
    return out
```

```python
from contextlib import ExitStack

import numpy as _np
import concourse.bass as bass
from concourse import mybir

SEQ, D = 256, 1024
ITEM = 2048
EPS = 1e-6
NEG = -1e30
MIX_Q_ORDER = [0, 4, 1, 5, 2, 6, 3, 7]
ATT_Q_ORDER = [8 * p + 4 * a + j for p in range(2) for j in range(4) for a in range(2)]
LEVELS = [1, 2, 4, 8, 16, 32, 64]
PARAMS = {"gains": 56, "subln": 1, "gdn_norm": 1, "gdn_conv": 128, "ffn_conv": 144, "ffn_bias": 48, "pe": 32,
          "w2k": 256, "w2v": 128, "lambdas": 256, "qk_gain": 128, "sinks": 16, "a_log": 16, "dt_bias": 16,
          "small": 448}
CONSTS = {"ident": 128, "causal": 128, "before": 128, "upto": 128, "tril": 128, "levels": 128 * len(LEVELS),
          "cmp_valid": 32, "own_head": 8, "spread": 128, "rope": 32, "inv_freq": 8, "ones": 128}

COUNTS = [("ff1", 33), ("mix_in", 11), ("cmp", 4), ("mix_out", 4), ("ff2", 33), ("att_in", 6), ("att_out", 4),
          ("glu1", 36), ("gdn_qkv", 16), ("gdn_z", 8), ("gdn_out", 8), ("glu2", 36)]
FIRST, N_ITEMS = {}, 0
for _name, _n in COUNTS:
    FIRST[_name] = N_ITEMS
    N_ITEMS += _n
FFNS = {"ff1": (22, False, 0), "ff2": (22, False, 22), "glu1": (24, True, 44), "glu2": (24, True, 68)}
TURNS = ["ff1", "mix_in", "mix_out", "ff2", "att_in", "att_out", "glu1", "gdn_qkv", "gdn_out0", "gdn_out1", "glu2"]
NORMS = ["ff1", "mix_in", "ff2", "att_in", "glu1", "gdn_qkv", "glu2"]
PROJ = {"mix_in": (11, 0), "att_in": (6, 11), "gdn_z": (8, 17)}


def two_blocks(nc, ins, out):
    f32, f32r, bf16 = mybir.dt.float32, mybir.dt.float32r, mybir.dt.bfloat16
    ALU, ACT, AX = mybir.AluOpType, mybir.ActivationFunctionType, mybir.AxisListType
    ctx = ExitStack()
    with ctx:
        def sb(name, shape, dt=f32):
            return ctx.enter_context(nc.sbuf_tensor(name, shape, dt))

        def sem(name):
            return ctx.enter_context(nc.semaphore(name))

        raw = sb("raw", [128, 3, ITEM])
        w_hi = sb("w_hi", [128, 3, ITEM], f32r)
        w_lo = sb("w_lo", [128, 3, ITEM], f32r)
        aT_hi = sb("aT_hi", [128, 16, SEQ], f32r)
        aT_lo = sb("aT_lo", [128, 16, SEQ], f32r)
        x = sb("residual", [128, 2, D])
        xn = sb("xn", [128, 2, D])
        post_gain = sb("post_gain", [128, D])
        par = sb("par", [128, sum(PARAMS.values())])
        con = sb("con", [128, sum(CONSTS.values())])
        ws_hi = sb("ws_hi", [128, 8, 56], f32r)
        ws_lo = sb("ws_lo", [128, 8, 56], f32r)
        arena = sb("arena", [128, 15232])
        stat = sb("stat", [128, 800])

        def columns(buffer, table, name):
            at = 0
            for n, width in table.items():
                if n == name:
                    return buffer[:, at:at + width]
                at += width
            raise KeyError(name)

        def P(name):
            return columns(par, PARAMS, name)

        def C(name):
            return columns(con, CONSTS, name)

        def spread(ap, n, axis=2):
            ap = ap.unsqueeze(axis)
            shape = list(ap.shape)
            shape[axis] = n
            return ap.broadcast_to(tuple(shape))

        ident = C("ident")
        gains = P("gains").rearrange("p (n k) -> p n k", k=8)
        levels = C("levels").rearrange("p (l c) -> p l c", c=128)
        bank = [ctx.enter_context(nc.psum_tensor(f"bank{i}", [128, 512], f32)) for i in range(8)]

        used = [0]

        def room(*shape):
            n = 1
            for s in shape:
                n *= s
            at = used[0]
            used[0] += n
            assert used[0] <= 15232, used[0]
            flat = arena[:, at:at + n]
            if len(shape) == 1:
                return flat
            names = "abcd"[:len(shape)]
            sizes = {c: s for c, s in zip(names[1:], shape[1:])}
            return flat.rearrange(f"p ({' '.join(names)}) -> p {' '.join(names)}", **sizes)

        used[0] = 0
        f_gate = room(2, SEQ)
        f_tanh = room(2, SEQ)
        f_hid = room(2, SEQ)
        used[0] = 0
        proj = room(2, 2816)
        heads = room(14, SEQ)
        expo = room(2, 512)
        expoT = room(2, 512)
        rot = room(4, 224)
        blockT = expo.rearrange("p a (g c) -> p a g c", g=2)
        hidden = room(4, 32)
        hidden2 = room(4, 32)
        kc_diag = room(2, 16)
        v_cmp = room(128)
        v_diag = room(8, 64)
        cmp_s = room(2, 8, 16)
        mixed = room(1024)
        c_expT = room(128)
        c_sums = expoT
        c_mask = room(2, 16)
        used[0] = 0
        qkv = room(2, 4096)
        qkT = room(16, SEQ)
        g_work = room(5, 512)
        g_conv, g_tanh, g_silu = g_work[:, 0, :], g_work[:, 1, :], g_work[:, 2:5, :]
        low_T = [xn[:, t, 0:512] for t in range(2)]
        qk_T = [xn[:, t, 512:1024] for t in range(2)]
        level = [[qkv[:, t, 0:512], qkv[:, t, 512:1024]] for t in range(2)]
        prod = [g_work[:, t, :] for t in range(2)]
        inv_T = [g_work[:, 2 + t, :] for t in range(2)]
        inv = [g_work[:, 4, :], post_gain[:, 0:512]]
        k_decayed = post_gain[:, 512:1024]
        at = [0]

        def small(*shape):
            n = 1
            for s in shape:
                n *= s
            at[0] += n
            assert at[0] <= 800, at[0]
            flat = stat[:, at[0] - n:at[0]]
            return flat if len(shape) == 1 else flat.rearrange("p (a b) -> p a b", b=shape[1])

        half = small(16)
        sumsq = small(4)
        rstd = small(2)
        lam = small(8)
        gates = small(2, 24)
        neg_max = small(2, 32)
        total = small(2, 32)
        coef = small(2, 32)
        r16 = small(2, 20)
        trig = small(4, 16)
        cos_sin = small(4, 8)
        ang = small(2, 8)
        pos = small(2)
        one_s = small(1)
        neg_sinks = small(16)
        ba = small(2, 32)
        soft = small(2, 32)
        beta = small(2, 16)
        decay = small(2, 16)
        decay_sum = small(2, 16)
        decay_exp = small(2, 16)
        decay_rest = small(16)
        beta_decay = small(16)
        rate = small(16)
        masks = sb("masks", [128, 3, 512], bf16)
        ident_b = sb("ident_b", [128, 128], bf16)
        pos_i = sb("pos_i", [128, 2], mybir.dt.int32)

        slot_loaded = [sem(f"slot_loaded{s}") for s in range(3)]
        x_loaded, par_loaded, con_loaded = sem("x_loaded"), sem("par_loaded"), sem("con_loaded")
        post_gain_loaded, stored = sem("post_gain_loaded"), sem("stored")
        w_hi_done, w_lo_done, item_done = sem("w_hi_done"), sem("w_lo_done"), sem("item_done")
        dve_step, act_step, pool_step = sem("dve_step"), sem("act_step"), sem("pool_step")
        x_ready = sem("x_ready")
        squares_ready, variance_ready, rstd_ready = sem("squares_ready"), sem("variance_ready"), sem("rstd_ready")
        rows_ready, turned, turned_hi, turned_lo = sem("rows_ready"), sem("turned"), sem("turned_hi"), sem("turned_lo")
        gate_scaled, gate_conv, gate_tanh = sem("gate_scaled"), sem("gate_conv"), sem("gate_tanh")
        hid_ready, hid_hi, hid_lo = sem("hid_ready"), sem("hid_hi"), sem("hid_lo")
        y_squares, conv_step, silu_step = sem("y_squares"), sem("conv_step"), sem("silu_step")
        setup_hi, setup_done = sem("setup_hi"), sem("setup_done")
        copied = sem("copied")
        heads_ready, heads_turned, heads_copied = sem("heads_ready"), sem("heads_turned"), sem("heads_copied")
        head_squares = sem("head_squares")
        gates_ready, gates_tanh = sem("gates_ready"), sem("gates_tanh")
        scores_ready, neg_max_ready, expo_ready = sem("scores_ready"), sem("neg_max_ready"), sem("expo_ready")
        expo_turned, expoT_ready, pv_done = sem("expo_turned"), sem("expoT_ready"), sem("pv_done")
        out_read, sink_args, sink_expo = sem("out_read"), sem("sink_args"), sem("sink_expo")
        c_twice = sem("c_twice")
        c_turned, c_copied, c_blocks = sem("c_turned"), sem("c_copied"), sem("c_blocks")
        c_gelu_arg, c_tanh, c_hidden = sem("c_gelu_arg"), sem("c_tanh"), sem("c_hidden")
        c_products, c_values, c_spread, c_operands = sem("c_products"), sem("c_values"), sem("c_spread"), sem("c_operands")
        c_scores, c_masked, c_expo, c_probs = sem("c_scores"), sem("c_masked"), sem("c_expo"), sem("c_probs")
        c_probs_turned, c_probsT, c_out, c_out_read = sem("c_probs_turned"), sem("c_probsT"), sem("c_out"), sem("c_out_read")
        g_scaled, g_tap, g_conv_ready, g_tanh_ready = sem("g_scaled"), sem("g_tap"), sem("g_conv_ready"), sem("g_tanh_ready")
        g_silu_ready, g_rows_turned, g_rows_copied = sem("g_silu_ready"), sem("g_rows_turned"), sem("g_rows_copied")
        g_small, g_soft_args, g_soft_done, g_decay = sem("g_small"), sem("g_soft_args"), sem("g_soft_done"), sem("g_decay")
        g_sums, g_sums_read, g_exps = sem("g_sums"), sem("g_sums_read"), sem("g_exps")
        g_squares, g_normed, g_qk_turned, g_qk_copied = sem("g_squares"), sem("g_normed"), sem("g_qk_turned"), sem("g_qk_copied")
        d_rows, d_diff, d_exp, d_masked = sem("d_rows"), sem("d_diff"), sem("d_exp"), sem("d_masked")
        d_mats, d_mats_turned, d_mats_T = sem("d_mats"), sem("d_mats_turned"), sem("d_mats_T")
        d_level, d_first, d_first_turned, d_first_T = sem("d_level"), sem("d_first"), sem("d_first_turned"), sem("d_first_T")
        d_prod, d_prod_copied, d_step, d_applied = sem("d_prod"), sem("d_prod_copied"), sem("d_step"), sem("d_applied")
        r_inputs, r_keys, r_new, r_new_copied = sem("r_inputs"), sem("r_keys"), sem("r_new"), sem("r_new_copied")
        r_state, r_state_copied, r_read, r_rhs = sem("r_state"), sem("r_state_copied"), sem("r_read"), sem("r_rhs")
        r_out, r_out_read, o_squares = sem("r_out"), sem("r_out_read"), sem("o_squares")
        z_tanh, z_step, z_used = sem("z_tanh"), sem("z_step"), sem("z_used")
        lam_args, lam_expo, trig_args, trig_done = sem("lam_args"), sem("lam_expo"), sem("trig_args"), sem("trig_done")

        HEADS = {"mix_in": [], "att_in": []}
        for n in range(8):
            HEADS["mix_in"].append((n % 4, 4 + n % 4, n // 4, 1792 + 128 * (n % 4), 128, n // 4, 128 * (n % 4)))
        for branch in range(2):
            for n in range(8):
                g = n // 4
                HEADS["mix_in"].append((8 + n % 4, 12 + branch, g, 2560 + 128 * branch + 64 * g, 64, 2 + branch, 64 * n))
        for n in range(16):
            HEADS["att_in"].append((4 * (n // 8) + n % 4, 8 + n // 8, n // 4 % 2, 1280 + 64 * (n // 4), 64, n // 8,
                                    64 * (n % 8)))
        HEAD_BANKS = {"mix_in": ([0.125, 0.125, 1.0, 1.0, 0.125, 0.125, 1.0], 0), "att_in": ([0.125] * 4 + [1.0], 7)}
        GROUPS = {n: [(0, 4 * g, 4) for g in range(len(h) // 4)] + [(1, 2 * g, 2) for g in range(len(h) // 2)]
                  for n, h in HEADS.items()}
        GROUPS_BEFORE = {"mix_in": 0, "att_in": len(GROUPS["mix_in"])}
        TILES_BEFORE = {"mix_in": 0, "att_in": 2}

        def c_block(buffer, kv):
            tiles = buffer[:, 8 + 2 * kv:10 + 2 * kv, :].rearrange("p a (b c) -> p (a b) c", c=32)
            return tiles

        def nsa_scale(k):
            return P("subln") if k < 4 else C("ones")[:, 0:1]

        def turn(name):
            return 4 * TURNS.index(name)

        block = ctx.enter_context(nc.Block())

        def rounds(engine, n, body):
            for k in range(min(n, 3)):
                body(k, 0)
            if n >= 6:
                with engine.Fori(1, n // 3) as r:
                    for k in range(3):
                        body(k, r)
            for k in range(max(n // 3, 1) * 3, n):
                body(k, 0)

        def ffn_order(engine, name, tile, down):
            pairs, i0 = FFNS[name][0] // 2, FIRST[name]

            def pair(m, q):
                i = i0 + 2 + 3 * (m - 1)
                tile(2 * m, i, q)
                tile(2 * m + 1, i + 1, q)
                down(m - 1, i + 2, q)

            tile(0, i0, 0)
            tile(1, i0 + 1, 0)
            pair(1, 0)
            looped = (pairs - 2) // 2 - (name == "glu2")
            with engine.Fori(0, looped) as q:
                pair(2, q)
                pair(3, q)
            for m in range(2 + 2 * looped, pairs):
                pair(m, 0)
            down(pairs - 1, i0 + 3 * pairs - 1, 0)

        @block.sync
        def _(sp):
            for t in range(2):
                sp.dma_start(x[:, t, :], ins["x"][128 * t:128 * t + 128, :]).then_inc(x_loaded, 16)
            sp.dma_start(con[:, :], ins["consts"]).then_inc(con_loaded, 16)
            sp.dma_start(par[:, :], ins["params"]).then_inc(par_loaded, 16)
            sp.dma_start(pos_i[:, :], ins["positions"]).then_inc(par_loaded, 16)
            for s in range(3):
                sp.dma_start(raw[:, s, :], ins["weights"][s]).then_inc(slot_loaded[s], 16)
            with sp.Fori(1, N_ITEMS // 3) as r:
                for s in range(3):
                    sp.wait_ge(w_lo_done, 3 * r + s - 2)
                    item = ins["weights"][bass.ds(3 * r + s, 1), :, :]
                    sp.dma_start(raw[:, s, :], item.rearrange("a p n -> p (a n)")).then_inc(slot_loaded[s], 16)
            for i in range(N_ITEMS // 3 * 3, N_ITEMS):
                sp.wait_ge(w_lo_done, i - 2)
                sp.dma_start(raw[:, i % 3, :], ins["weights"][i]).then_inc(slot_loaded[i % 3], 16)
            for t in range(2):
                sp.wait_ge(x_ready, 2 * len(NORMS) + t + 1)
                sp.dma_start(out[128 * t:128 * t + 128, :], x[:, t, :]).then_inc(stored, 16)
            sp.wait_ge(stored, 32)

        @block.tensor
        def _(pe):
            def exact(to, w, left, start, stop, moving_w=False):
                w_parts, l_parts = w, left
                pairs = [(w_parts[0], l_parts[0]), (w_parts[0], l_parts[1]), (w_parts[1], l_parts[0])]
                for n, (a, b) in enumerate(pairs):
                    lhsT, rhs = (b, a) if moving_w else (a, b)
                    last = nc.tensor.matmul(to, lhsT, rhs, start=start and n == 0, stop=stop and n == 2)
                return last

            def weights(i, a, b):
                return w_hi[:, i % 3, a:b], w_lo[:, i % 3, a:b]

            def left(k, a=0, b=SEQ):
                return aT_hi[:, k, a:b], aT_lo[:, k, a:b]

            def turn_rows(name, source, ready=None):
                n = TURNS.index(name)
                for t in range(2):
                    pe.wait_ge(rows_ready, 2 * n + t + 1)
                    for k in range(8):
                        to = bank[4 + k // 2][:, 256 * (k % 2) + 128 * t:256 * (k % 2) + 128 * t + 128]
                        last = nc.tensor.transpose(to, source[:, t, 128 * k:128 * k + 128], ident)
                        if t == 1 and k % 2:
                            last.then_inc(turned, 1)

            def aT_ready(name):
                pe.wait_ge(turned_lo, turn(name) + 4)

            def ffn(name):
                n_tiles, conv, f0 = FFNS[name]
                turn_rows(name, xn)
                aT_ready(name)

                def tile(f, i, q):
                    pe.wait_ge(w_lo_done, i + 1 + 6 * q)
                    if f0 + f >= 4:
                        pe.wait_ge(hid_ready, f0 + f - 3 + 4 * q)
                    to = bank[4 + f % 4]
                    for part in range(2):
                        for k in range(8):
                            at = 1024 * part + 128 * k
                            last = exact(to[:, 256 * part:256 * part + 256], weights(i, at, at + 128), left(k),
                                         k == 0, k == 7)
                    last.then_inc(item_done, 1)

                def down(m, i, q):
                    pe.wait_ge(w_lo_done, i + 1 + 6 * q)
                    pe.wait_ge(hid_lo, f0 + 2 * m + 2 + 4 * q)
                    for j in range(2):
                        f = 2 * m + j
                        for y in range(4):
                            t, h = y // 2, y % 2
                            last = exact(bank[y][:, :], weights(i, 1024 * j + 512 * h, 1024 * j + 512 * h + 512),
                                         left(8 + f % 4, 128 * t, 128 * t + 128), f == 0, f == n_tiles - 1, True)
                    last.then_inc(item_done, 1)

                ffn_order(pe, name, tile, down)

            def project_rows(name):
                n, before = PROJ[name]

                def body(k, r):
                    i = FIRST[name] + k
                    pe.wait_ge(w_lo_done, i + 1 + 3 * r)
                    if k >= 3 or not isinstance(r, int) or r > 0:
                        pe.wait_ge(copied, before + k - 2 + 3 * r)
                    for t in range(2):
                        for kk in range(8):
                            last = exact(bank[4 + k % 3][:, 256 * t:256 * t + 256],
                                         weights(i, 256 * kk, 256 * kk + 256), left(kk, 128 * t, 128 * t + 128),
                                         kk == 0, kk == 7, True)
                    last.then_inc(item_done, 1)

                rounds(pe, n, body)

            def project_small(a, b, done):
                for t in range(2):
                    for kk in range(8):
                        last = exact(bank[7][:, 64 * t:64 * t + b - a], (ws_hi[:, kk, a:b], ws_lo[:, kk, a:b]),
                                     left(kk, 128 * t, 128 * t + 128), kk == 0, kk == 7, True)
                last.then_inc(done, 1)

            def project_out(name, halves=1):
                for c in range(4):
                    for h in range(halves):
                        i = FIRST[name] + halves * c + h
                        pe.wait_ge(w_lo_done, i + 1)
                        for t in range(2):
                            for kk in range(8):
                                last = exact(bank[2 * t + c // 2][:, 256 * (c % 2):256 * (c % 2) + 256],
                                             weights(i, 256 * kk, 256 * kk + 256),
                                             left(8 * h + kk, 128 * t, 128 * t + 128),
                                             h == 0 and kk == 0, h == halves - 1 and kk == 7, True)
                        last.then_inc(item_done, 1)

            def turn_heads(layer):
                scales, before = HEAD_BANKS[layer]
                pe.wait_ge(heads_ready, 1 + (layer == "att_in"))
                for b in range(len(scales)):
                    if b >= 4:
                        pe.wait_ge(heads_copied, before + b - 3)
                    for j in range(2):
                        for t in range(2):
                            at = 128 * (2 * b + j)
                            last = nc.tensor.transpose(bank[4 + b % 4][:, 256 * j + 128 * t:256 * j + 128 * t + 128],
                                                       proj[:, t, at:at + 128], ident)
                    last.then_inc(heads_turned, 1)
                pe.wait_ge(heads_copied, before + len(scales))

            def attention(layer):
                groups, base = GROUPS[layer], GROUPS_BEFORE[layer]

                def scores(n):
                    t, h0, count = groups[n]
                    width = 512 // count
                    to = bank[4 + n % 2]
                    if n >= 2:
                        pe.wait_ge(expo_ready, base + n - 1)
                    mask = 0 if t == 0 else (2 if layer == "att_in" else 1)
                    nc.tensor.matmul(to[:, :], ident_b[:, :], masks[:, mask, :], start=True, stop=False)
                    for c in range(count):
                        q, k, half_of, _, _, _, _ = HEADS[layer][h0 + c]
                        rows = slice(64 * half_of, 64 * half_of + 64)
                        last = nc.tensor.matmul(to[:, width * c:width * c + width],
                                                heads[rows, q, 128 * t:128 * t + 128], heads[rows, k, 0:width],
                                                start=False, stop=c == count - 1)
                    last.then_inc(scores_ready, 1)

                def turn_expo(n):
                    pe.wait_ge(expo_ready, base + n + 1)
                    if n >= 2:
                        pe.wait_ge(expoT_ready, base + n - 1)
                    for b in range(4):
                        last = nc.tensor.transpose(bank[6 + n % 2][:, 128 * b:128 * b + 128],
                                                   expo[:, n % 2, 128 * b:128 * b + 128], ident)
                    last.then_inc(expo_turned, 1)

                def values(n):
                    t, h0, count = groups[n]
                    pe.wait_ge(expoT_ready, base + n + 1)
                    if t == 1 and h0 == 0:
                        pe.wait_ge(out_read, TILES_BEFORE[layer] + 1)
                    for c in range(count):
                        _, _, _, v, width, b, at = HEADS[layer][h0 + c]
                        for kt in range(t + 1):
                            s = 128 * ((t + 1) * c + kt)
                            last = nc.tensor.matmul(bank[b][:, at:at + width], expoT[:, n % 2, s:s + 128],
                                                    proj[:, kt, v:v + width], start=kt == 0, stop=kt == t)
                    last.then_inc(pv_done, 1)

                scores(0)
                scores(1)
                for n in range(len(groups)):
                    turn_expo(n)
                    if n + 2 < len(groups):
                        scores(n + 2)
                    if n >= 1:
                        values(n - 1)
                values(len(groups) - 1)

            def compressed():
                pe.wait_ge(copied, 11)
                pe.wait_ge(c_twice, 1)
                for kv in range(2):
                    for g in range(2):
                        for t in range(2):
                            at = 512 * t + 256 * kv + 128 * g
                            last = nc.tensor.transpose(bank[4 + kv][:, 256 * g + 128 * t:256 * g + 128 * t + 128],
                                                       mixed[:, at:at + 128], ident)
                    last.then_inc(c_turned, 1)
                pe.wait_ge(c_blocks, 2)
                for kv in range(2):
                    for part in range(2):
                        i = FIRST["cmp"] + 2 * kv + part
                        pe.wait_ge(w_lo_done, i + 1)
                        for k in range(8):
                            for h in range(2):
                                at = 256 * k + 128 * h
                                last = exact(bank[2 * kv + h][:, 0:30], weights(i, at, at + 128),
                                             (c_block(aT_hi, kv)[:, 8 * part + k, 0:30],
                                              c_block(aT_lo, kv)[:, 8 * part + k, 0:30]),
                                             part == 0 and k == 0, part == 1 and k == 7)
                        last.then_inc(item_done, 1)

            def compressed_operands():
                pe.wait_ge(c_hidden, 1)
                w2k = P("w2k").rearrange("p (h c) -> p h c", h=2)
                w2v = P("w2v").rearrange("p (h c) -> p h c", h=2)
                for h in range(2):
                    nc.tensor.matmul(bank[0][:, 0:30], w2k[:, h, :], hidden2[:, h, 0:30], start=h == 0, stop=h == 1)
                for g in range(2):
                    for h in range(2):
                        last = nc.tensor.matmul(bank[1][0:15, 64 * g:64 * g + 64], hidden2[:, 2 + h, 15 * g:15 * g + 15],
                                                w2v[:, h, :], start=h == 0, stop=h == 1)
                last.then_inc(c_products, 1)
                pe.wait_ge(c_values, 1)
                nc.tensor.matmul(bank[2][:, 0:128], C("spread")[0:15, :], v_cmp[0:15, :], start=True, stop=True)                    .then_inc(c_spread, 1)
                pe.wait_ge(c_operands, 1)
                for t in range(2):
                    for j in range(4):
                        last = nc.tensor.matmul(bank[t][:, 32 * j:32 * j + 32], heads[:, 8 + j, 128 * t:128 * t + 128],
                                                kc_diag.rearrange("p g c -> p (g c)"), start=True, stop=True)
                    last.then_inc(c_scores, 1)

            def compressed_out():
                for t in range(2):
                    pe.wait_ge(c_probs, t + 1)
                    nc.tensor.transpose(bank[2][:, 128 * t:128 * t + 128], cmp_s[:, t].rearrange("p h c -> p (h c)"),
                                        ident).then_inc(c_probs_turned, 1)
                    pe.wait_ge(c_probsT, t + 1)
                    if t == 1:
                        pe.wait_ge(c_out_read, 1)
                    nc.tensor.matmul(bank[3][:, :], c_expT, v_diag.rearrange("p h c -> p (h c)"),
                                     start=True, stop=True).then_inc(c_out, 1)
                pe.wait_ge(c_out_read, 2)

            def convolved():
                def to_rows(k, r):
                    pe.wait_ge(g_silu_ready, k + 1 + 3 * r)
                    if k >= 3 or not isinstance(r, int):
                        pe.wait_ge(g_rows_copied, k - 2 + 3 * r)
                    for t in range(2):
                        for n in range(2):
                            last = nc.tensor.transpose(bank[k % 3][:, 256 * t + 128 * n:256 * t + 128 * n + 128],
                                                       g_silu[:, k % 3, 256 * n + 128 * t:256 * n + 128 * t + 128],
                                                       ident)
                    last.then_inc(g_rows_turned, 1)

                def body(k, r):
                    pe.wait_ge(w_lo_done, FIRST["gdn_qkv"] + k + 1 + 3 * r)
                    if k >= 3 or not isinstance(r, int):
                        pe.wait_ge(g_silu_ready, k - 2 + 3 * r)
                    for n in range(2):
                        for kk in range(8):
                            at = 256 * kk + 128 * n
                            last = exact(bank[4 + k % 3][:, 256 * n:256 * n + 256],
                                         weights(FIRST["gdn_qkv"] + k, at, at + 128), left(kk), kk == 0, kk == 7)
                    last.then_inc(item_done, 1)
                    if k or not isinstance(r, int):
                        to_rows(k - 1, r)

                rounds(pe, 16, body)
                to_rows(15, 0)

            def delta_setup():
                pe.wait_ge(g_decay, 1)
                for t in range(2):
                    nc.tensor.matmul(bank[7][:, 16 * t:16 * t + 16], C("upto"), decay[:, t, :], start=True, stop=True)
                nc.tensor.matmul(bank[7][:, 32:48], C("ones"), decay[:, 0, :], start=True, stop=True)\
                    .then_inc(g_sums, 1)
                pe.wait_ge(g_sums_read, 1)
                pe.wait_ge(g_normed, 2)
                for b in range(8):
                    if b >= 4:
                        pe.wait_ge(g_qk_copied, b - 3)
                    for j in range(2):
                        for t in range(2):
                            at = 128 * (2 * b + j)
                            last = nc.tensor.transpose(bank[4 + b % 4][:, 256 * j + 128 * t:256 * j + 128 * t + 128],
                                                       qkv[:, t, at:at + 128], ident)
                    last.then_inc(g_qk_turned, 1)
                pe.wait_ge(g_qk_copied, 8)

            def delta(b):
                tok = [slice(0, 128), slice(128, 256)]
                col = [slice(128 * c, 128 * c + 128) for c in range(4)]
                if b:
                    pe.wait_ge(r_out_read, 2 * b)
                for t in range(2):
                    rows, prods = bank[4 * t], bank[4 * t + 1]
                    for c in range(4):
                        g_row = decay[:, t, 4 * b + c:4 * b + c + 1].broadcast_to((128, 128))
                        nc.tensor.matmul(rows[:, col[c]], g_row, C("upto"), start=True, stop=True)
                    for c in range(2):
                        key, query = qkT[:, 8 + 2 * b + c, tok[t]], qkT[:, 2 * b + c, tok[t]]
                        nc.tensor.matmul(prods[:, col[c]], key, key, start=True, stop=True)
                        last = nc.tensor.matmul(prods[:, col[2 + c]], query, key, start=True, stop=True)
                    last.then_inc(d_rows, 1)
                for t in range(2):
                    pe.wait_ge(d_mats, 2 * b + t + 1)
                    for c in range(4):
                        nc.tensor.transpose(bank[4 * t + 2][:, col[c]], prod[t][:, col[c]], ident)
                    for c in range(4):
                        last = nc.tensor.transpose(bank[4 * t + 3][:, col[c]], inv[t][:, col[c]], ident)
                    last.then_inc(d_mats_turned, 1)
                for t in range(2):
                    pe.wait_ge(d_first, 2 * b + t + 1)
                    for c in range(4):
                        last = nc.tensor.transpose(bank[4 * t][:, col[c]], inv_T[t][:, col[c]], ident)
                    last.then_inc(d_first_turned, 1)
                for n in range(1, len(LEVELS)):
                    for t in range(2):
                        at = 12 * b + 2 * (n - 1) + t
                        pe.wait_ge(d_level, 14 * b + 2 * n + t + 1)
                        if n == 1:
                            pe.wait_ge(d_first_T, 2 * b + t + 1)
                        else:
                            pe.wait_ge(d_applied, at - 1)
                        for c in range(4):
                            last = nc.tensor.matmul(bank[4 * t][:, col[c]], level[t][n % 2][:, col[c]],
                                                    inv[t][:, col[c]], start=True, stop=True)
                        last.then_inc(d_prod, 1)
                    for t in range(2):
                        pe.wait_ge(d_prod_copied, 12 * b + 2 * (n - 1) + t + 1)
                        for c in range(4):
                            last = nc.tensor.matmul(bank[4 * t + 1][:, col[c]], prod[t][:, col[c]],
                                                    inv_T[t][:, col[c]], start=True, stop=True)
                        if n < len(LEVELS) - 1:
                            for c in range(4):
                                last = nc.tensor.matmul(bank[4 * t + 2][:, col[c]], inv_T[t][:, col[c]],
                                                        prod[t][:, col[c]], start=True, stop=True)
                        last.then_inc(d_step, 1)
                pe.wait_ge(d_applied, 12 * b + 12)
                pe.wait_ge(r_inputs, b + 1)
                v = [qkv[:, t, 2048 + 512 * b:2560 + 512 * b] for t in range(2)]
                new = [level[0][0], level[0][1]]
                state = level[1][0]
                for c in range(4):
                    last = nc.tensor.matmul(bank[3][:, col[c]], inv_T[0][:, col[c]], v[0][:, col[c]],
                                            start=True, stop=True)
                last.then_inc(r_new, 1)
                pe.wait_ge(r_new_copied, 2 * b + 1)
                pe.wait_ge(r_keys, b + 1)
                for c in range(4):
                    last = nc.tensor.matmul(bank[0][:, col[c]], k_decayed[:, col[c]], new[0][:, col[c]],
                                            start=True, stop=True)
                last.then_inc(r_state, 1)
                for c in range(4):
                    last = nc.tensor.matmul(bank[1][:, col[c]], qk_T[0][:, col[c]], new[0][:, col[c]],
                                            start=True, stop=True)
                last.then_inc(r_out, 1)
                pe.wait_ge(r_state_copied, b + 1)
                for to, first in ((4, 8), (5, 0)):
                    for c in range(4):
                        last = nc.tensor.matmul(bank[to][:, col[c]], qkT[:, first + 2 * b + c // 2, tok[1]],
                                                state[:, col[c]], start=True, stop=True)
                last.then_inc(r_read, 1)
                pe.wait_ge(r_rhs, b + 1)
                for c in range(4):
                    last = nc.tensor.matmul(bank[6][:, col[c]], inv_T[1][:, col[c]], v[1][:, col[c]],
                                            start=True, stop=True)
                last.then_inc(r_new, 1)
                pe.wait_ge(r_new_copied, 2 * b + 2)
                for c in range(4):
                    last = nc.tensor.matmul(bank[7][:, col[c]], qk_T[1][:, col[c]], new[1][:, col[c]],
                                            start=True, stop=True)
                last.then_inc(r_out, 1)

            pe.wait_ge(con_loaded, 16)
            pe.wait_ge(setup_done, 3)
            ffn("ff1")
            turn_rows("mix_in", xn)
            aT_ready("mix_in")
            project_rows("mix_in")
            project_small(0, 24, gates_ready)
            compressed()
            turn_heads("mix_in")
            compressed_operands()
            compressed_out()
            attention("mix_in")
            turn_rows("mix_out", xn)
            aT_ready("mix_out")
            project_out("mix_out")
            ffn("ff2")
            turn_rows("att_in", xn)
            aT_ready("att_in")
            project_rows("att_in")
            turn_heads("att_in")
            attention("att_in")
            turn_rows("att_out", xn)
            aT_ready("att_out")
            project_out("att_out")
            ffn("glu1")
            turn_rows("gdn_qkv", xn)
            aT_ready("gdn_qkv")
            convolved()
            project_small(24, 56, g_small)
            delta_setup()
            for b in range(4):
                delta(b)
            pe.wait_ge(r_out_read, 8)
            project_rows("gdn_z")
            pe.wait_ge(z_used, 8)
            turn_rows("gdn_out0", qkv[:, :, 2048:3072])
            pe.wait_ge(turned_lo, turn("gdn_out0") + 4)
            turn_rows("gdn_out1", qkv[:, :, 3072:4096])
            aT_ready("gdn_out1")
            project_out("gdn_out", 2)
            ffn("glu2")

        @block.scalar
        def _(act):
            done = [0]

            def link(instruction):
                done[0] += 1
                instruction.then_inc(act_step, 1)
                act.wait_ge(act_step, done[0])

            def split(i, r=0):
                if i >= N_ITEMS:
                    return
                act.wait_ge(slot_loaded[i % 3], 16 * (i // 3 + 1) + 16 * r)
                if i >= 3:
                    act.wait_ge(item_done, i - 2 + 3 * r)
                nc.scalar.activation(w_hi[:, i % 3, :], raw[:, i % 3, :], ACT.Copy).then_inc(w_hi_done, 1)

            def turn_out(name, scale):
                n = TURNS.index(name)
                base = 8 if name == "gdn_out1" else 0
                for j in range(4):
                    act.wait_ge(turned, 4 * n + j + 1)
                    for k in range(2):
                        last = nc.scalar.activation(aT_hi[:, base + 2 * j + k, :], bank[4 + j][:, 256 * k:256 * k + 256],
                                                    ACT.Copy, scale=scale(2 * j + k))
                    last.then_inc(turned_hi, 1)

            def norm_squares(name):
                n = NORMS.index(name)
                for t in range(2):
                    act.wait_ge(x_ready, 2 * n + t + 1)
                    nc.scalar.activation(xn[:, t, :], x[:, t, :], ACT.Square, accum_out=sumsq[:, t:t + 1])\
                        .then_inc(squares_ready, 1)

            def pre_norm(name):
                norm_squares(name)
                n = NORMS.index(name)
                turn_out(name, lambda k: gains[:, n, k:k + 1])

            def ffn(name):
                n_tiles, conv, f0 = FFNS[name]
                pre_norm(name)

                def tile(f, i, q):
                    gate = bank[4 + f % 4][:, 0:256]
                    act.wait_ge(item_done, i + 1 + 6 * q)
                    tanh_of = gate
                    if conv:
                        tap = P("ffn_conv")[:, 72 * (name == "glu2"):72 * (name == "glu2") + 72]
                        bias = P("ffn_bias")[:, 24 * (name == "glu2"):24 * (name == "glu2") + 24]
                        tap, bias = tap.rearrange("p (f t) -> p f t", t=3), bias
                        nc.scalar.activation(f_gate[:, f % 2, :], gate, ACT.Identity,
                                             scale=at_tile(tap, f, q, 2), bias=at_tile(bias, f, q))\
                            .then_inc(gate_scaled, 1)
                        act.wait_ge(gate_conv, f0 - 44 + f + 1 + 4 * q)
                        tanh_of = f_gate[:, f % 2, :]
                    nc.scalar.activation(f_tanh[:, f % 2, :], tanh_of, ACT.Tanh, scale=0.5).then_inc(gate_tanh, 1)
                    split(i + 3, 2 * q)
                    act.wait_ge(hid_ready, f0 + f + 1 + 4 * q)
                    nc.scalar.activation(aT_hi[:, 8 + f % 4, :], f_hid[:, f % 2, :], ACT.Copy).then_inc(hid_hi, 1)

                def down(m, i, q):
                    split(i + 3, 2 * q)

                ffn_order(act, name, tile, down)

            def at_tile(table, f, q, tap=None):
                if tap is None:
                    return table[:, bass.ds(f + 4 * q, 1)]
                return table[:, bass.ds(f + 4 * q, 1), tap:tap + 1].rearrange("p a b -> p (a b)")

            def post_squares(name):
                act.wait_ge(item_done, FIRST[name] + dict(COUNTS)[name])
                for y in range(4):
                    nc.scalar.activation(xn[:, y // 2, 512 * (y % 2):512 * (y % 2) + 512], bank[y][:, :], ACT.Square,
                                         accum_out=sumsq[:, y:y + 1]).then_inc(y_squares, 1)

            def copy_out(name, extra):
                n, before = PROJ[name]

                def body(k, r):
                    act.wait_ge(item_done, FIRST[name] + k + 1 + 3 * r)
                    extra(k, r)
                    split(FIRST[name] + k + 3, r)

                rounds(act, n, body)

            def copy_rows(k, r):
                to = proj[:, :, bass.ds(256 * k + 768 * r, 256)]
                nc.scalar.activation(to, bank[4 + k % 3][:, :].rearrange("p (t c) -> p t c", t=2), ACT.Copy)\
                    .then_inc(copied, 1)

            def splits(first, n):
                for i in range(first, first + n):
                    split(i + 3)

            def turn_heads(layer):
                scales, before = HEAD_BANKS[layer]
                for b, scale in enumerate(scales):
                    act.wait_ge(heads_turned, before + b + 1)
                    nc.scalar.activation(heads[:, 2 * b:2 * b + 2, :],
                                         bank[4 + b % 4][:, :].rearrange("p (j c) -> p j c", j=2),
                                         ACT.Copy, scale=scale).then_inc(heads_copied, 1)

            def attention(layer):
                for n, (t, h0, count) in enumerate(GROUPS[layer]):
                    base, width = GROUPS_BEFORE[layer], 512 // count
                    act.wait_ge(neg_max_ready, base + n + 1)
                    if n >= 2:
                        act.wait_ge(expo_turned, base + n - 1)
                    for c in range(count):
                        cols = slice(width * c, width * c + width)
                        last = nc.scalar.activation(expo[:, n % 2, cols], bank[4 + n % 2][:, cols], ACT.Exp,
                                                    bias=neg_max[:, t, h0 + c:h0 + c + 1],
                                                    accum_out=total[:, t, h0 + c:h0 + c + 1])
                    last.then_inc(expo_ready, 1)
                    if layer == "att_in" and n in (len(GROUPS[layer]) // 3, len(GROUPS[layer]) - 1):
                        tile = int(n > len(GROUPS[layer]) // 3)
                        act.wait_ge(sink_args, tile + 1)
                        nc.scalar.activation(coef[:, tile, 16:32], coef[:, tile, 16:32], ACT.Exp)\
                            .then_inc(sink_expo, 1)

            def convolved():
                taps = P("gdn_conv").rearrange("p (f t) -> p f t", t=4)

                def rows(k, r):
                    act.wait_ge(g_rows_turned, k + 1 + 3 * r)
                    nc.scalar.activation(qkv[:, :, bass.ds(256 * k + 768 * r, 256)],
                                         bank[k % 3][:, :].rearrange("p (t c) -> p t c", t=2), ACT.Copy, scale=0.5)\
                        .then_inc(g_rows_copied, 1)

                def body(k, r):
                    act.wait_ge(item_done, FIRST["gdn_qkv"] + k + 1 + 3 * r)
                    if k or not isinstance(r, int):
                        act.wait_ge(g_silu_ready, k + 3 * r)
                    for n in range(2):
                        tap = taps[:, bass.ds(2 * k + n + 6 * r, 1), 3:4].rearrange("p a b -> p (a b)")
                        last = nc.scalar.activation(g_conv[:, 256 * n:256 * n + 256],
                                                    bank[4 + k % 3][:, 256 * n:256 * n + 256], ACT.Copy, scale=tap)
                    last.then_inc(g_scaled, 1)
                    split(FIRST["gdn_qkv"] + k + 3, r)
                    act.wait_ge(g_conv_ready, k + 1 + 3 * r)
                    nc.scalar.activation(g_tanh, g_conv, ACT.Tanh, scale=0.5).then_inc(g_tanh_ready, 1)
                    if k or not isinstance(r, int):
                        rows(k - 1, r)

                rounds(act, 16, body)
                rows(15, 0)

            def delta_setup():
                act.wait_ge(g_rows_copied, 16)
                nc.scalar.activation(xn[:, :, :].rearrange("p t c -> p (t c)"), qkv[:, 0, 0:2048], ACT.Square)\
                    .then_inc(g_squares, 1)
                act.wait_ge(g_soft_args, 1)
                link(nc.scalar.activation(soft[:, :, 0:16], soft[:, :, 0:16], ACT.Exp))
                nc.scalar.activation(soft[:, :, 16:32], ba[:, :, 0:16], ACT.Tanh, scale=0.5)
                nc.scalar.activation(rate, P("a_log"), ACT.Exp)
                nc.scalar.activation(soft[:, :, 0:16], soft[:, :, 0:16], ACT.Ln, bias=1.0).then_inc(g_soft_done, 1)
                act.wait_ge(g_normed, 1)
                nc.scalar.activation(xn[:, :, :].rearrange("p t c -> p (t c)"), qkv[:, 1, 0:2048], ACT.Square)\
                    .then_inc(g_squares, 1)
                for b in range(8):
                    act.wait_ge(g_qk_turned, b + 1)
                    nc.scalar.activation(qkT[:, 2 * b:2 * b + 2, :],
                                         bank[4 + b % 4][:, :].rearrange("p (j c) -> p j c", j=2), ACT.Copy)\
                        .then_inc(g_qk_copied, 1)
                act.wait_ge(g_sums_read, 1)
                nc.scalar.activation(decay_exp, decay_sum, ACT.Exp)
                nc.scalar.activation(decay_rest, decay_rest, ACT.Exp).then_inc(g_exps, 1)

            def delta(b):
                for t in range(2):
                    act.wait_ge(d_diff, 2 * b + t + 1)
                    nc.scalar.activation(level[t][0], level[t][0], ACT.Exp, scale=-1.0).then_inc(d_exp, 1)
                for t in range(2):
                    act.wait_ge(d_mats_turned, 2 * b + t + 1)
                    nc.scalar.activation(low_T[t], bank[4 * t + 2][:, :], ACT.Copy)
                    nc.scalar.activation(qk_T[t], bank[4 * t + 3][:, :], ACT.Copy).then_inc(d_mats_T, 1)
                for t in range(2):
                    act.wait_ge(d_first_turned, 2 * b + t + 1)
                    nc.scalar.activation(inv[t], bank[4 * t][:, :], ACT.Copy).then_inc(d_first_T, 1)
                for n in range(1, len(LEVELS)):
                    for t in range(2):
                        act.wait_ge(d_prod, 12 * b + 2 * (n - 1) + t + 1)
                        nc.scalar.activation(prod[t], bank[4 * t][:, :], ACT.Copy).then_inc(d_prod_copied, 1)
                for t in range(2):
                    act.wait_ge(r_new, 2 * b + t + 1)
                    nc.scalar.activation(level[0][t], bank[3 + 3 * t][:, :], ACT.Copy).then_inc(r_new_copied, 1)
                    if t == 0:
                        act.wait_ge(r_state, b + 1)
                        nc.scalar.activation(level[1][0], bank[0][:, :], ACT.Copy).then_inc(r_state_copied, 1)

            def gated():
                for t in range(2):
                    act.wait_ge(r_out_read, 8)
                    if t:
                        act.wait_ge(g_normed, 3)
                    nc.scalar.activation(xn[:, :, :].rearrange("p t c -> p (t c)"), qkv[:, t, 2048:4096],
                                         ACT.Square).then_inc(o_squares, 1)

                def gate(k, r):
                    if k >= 3 or not isinstance(r, int):
                        act.wait_ge(z_used, k - 2 + 3 * r)
                    nc.scalar.activation(g_work[:, k % 3, :], bank[4 + k % 3][:, :], ACT.Tanh, scale=0.5)\
                        .then_inc(z_tanh, 1)

                copy_out("gdn_z", gate)

            act.wait_ge(par_loaded, 32)
            nc.scalar.activation(ws_hi[:, :, :], P("small").rearrange("p (k c) -> p k c", c=56), ACT.Copy)\
                .then_inc(setup_hi, 1)
            for i in range(3):
                split(i)
            act.wait_ge(lam_args, 1)
            nc.scalar.activation(lam[:, 2:4], lam[:, 0:2], ACT.Exp).then_inc(lam_expo, 1)
            act.wait_ge(trig_args, 1)
            nc.scalar.activation(trig[:, 1, :], trig[:, 0, :], ACT.Sin)
            nc.scalar.activation(trig[:, 2, :], trig[:, 0, :], ACT.Sin, scale=0.5).then_inc(trig_done, 1)
            ffn("ff1")
            post_squares("ff1")
            pre_norm("mix_in")
            copy_out("mix_in", copy_rows)
            act.wait_ge(gates_ready, 1)
            nc.scalar.activation(gates, bank[7][:, 0:128].rearrange("p (t c) -> p t c", t=2)[:, :, 0:24], ACT.Tanh,
                                 scale=0.5).then_inc(gates_tanh, 1)
            for kv in range(2):
                act.wait_ge(c_turned, kv + 1)
                rows = bank[4 + kv][:, :].rearrange("p (g c) -> p g c", g=2)
                nc.scalar.activation(blockT[0:64, kv, :, :], rows[0:64, :, :], ACT.Copy)
                nc.scalar.activation(blockT[64:128, kv, :, 0:255], rows[64:128, :, 1:256], ACT.Copy).then_inc(c_copied, 1)
            splits(FIRST["cmp"], 3)
            turn_heads("mix_in")
            splits(FIRST["cmp"] + 3, 1)
            act.wait_ge(c_gelu_arg, 1)
            nc.scalar.activation(hidden2[:, :, 0:30], hidden2[:, :, 0:30], ACT.Tanh, scale=0.7978845608028654)\
                .then_inc(c_tanh, 1)
            for t in range(2):
                act.wait_ge(c_masked, t + 1)
                nc.scalar.activation(cmp_s[:, t], cmp_s[:, t], ACT.Exp).then_inc(c_expo, 1)
            attention("mix_in")
            scales = nsa_scale
            turn_out("mix_out", scales)
            splits(FIRST["mix_out"], 4)
            post_squares("mix_out")
            ffn("ff2")
            post_squares("ff2")
            pre_norm("att_in")
            copy_out("att_in", copy_rows)
            act.wait_ge(copied, 17)
            for t in range(2):
                nc.scalar.activation(proj[:, t, 1536:2816], proj[:, t, 0:1280], ACT.Square).then_inc(head_squares, 1)
            turn_heads("att_in")
            attention("att_in")
            turn_out("att_out", lambda k: 1.0)
            splits(FIRST["att_out"], 4)
            ffn("glu1")
            pre_norm("gdn_qkv")
            convolved()
            delta_setup()
            for b in range(4):
                delta(b)
            gated()
            turn_out("gdn_out0", lambda k: P("gdn_norm"))
            turn_out("gdn_out1", lambda k: P("gdn_norm"))
            splits(FIRST["gdn_out"], 8)
            ffn("glu2")

        @block.gpsimd
        def _(pool):
            steps = [0]

            def link(instruction):
                steps[0] += 1
                instruction.then_inc(pool_step, 1)
                pool.wait_ge(pool_step, steps[0])

            def power(n, value, result):
                pool.wait_ge(variance_ready, n + 1)
                nc.gpsimd.tensor_tensor(result, value, half[:, 0:1].broadcast_to(result.shape), ALU.pow)\
                    .then_inc(rstd_ready, 1)

            def load_post_gain(n):
                if n:
                    pool.wait_ge(x_ready, 2 * n + 2)
                pool.dma_start(post_gain[:, :], ins["post_gains"][n:n + 1, :].broadcast_to((128, D)))\
                    .then_inc(post_gain_loaded, 16)

            link(nc.gpsimd.memset(half, -0.5))
            load_post_gain(0)
            powers = [0]

            def power_of(value, result):
                power(powers[0], value, result)
                powers[0] += 1

            def pre_norm():
                for t in range(2):
                    power_of(rstd[:, t:t + 1], rstd[:, t:t + 1])

            def post_norm():
                power_of(rstd[:, 0:2], rstd[:, 0:2])
            pre_norm()
            post_norm()
            pre_norm()
            load_post_gain(1)
            for t in range(2):
                power_of(r16[:, t, 0:4], r16[:, t, 0:4])
            post_norm()
            load_post_gain(2)
            pre_norm()
            post_norm()
            pre_norm()
            for t in range(2):
                power_of(r16[:, t, 0:20], r16[:, t, 0:20])
            pre_norm()
            pre_norm()
            for t in range(2):
                power_of(r16[:, t, 0:16], r16[:, t, 0:16])
            for b in range(4):
                for t in range(2):
                    pool.wait_ge(d_exp, 2 * b + t + 1)
                    four = level[t][0].rearrange("p (h d) -> p h d", h=4)
                    nc.gpsimd.tensor_tensor(four, four, spread(C("tril"), 4, 1), ALU.mult).then_inc(d_masked, 1)
                for n in range(len(LEVELS)):
                    for t in range(2):
                        if n == 0:
                            pool.wait_ge(d_mats_T, 2 * b + t + 1)
                        if n == 2:
                            pool.wait_ge(d_first, 2 * b + t + 1)
                        if n > 2:
                            pool.wait_ge(d_prod, 12 * b + 2 * (n - 3) + t + 1)
                        nc.gpsimd.tensor_tensor(level[t][n % 2].rearrange("p (h d) -> p h d", h=4),
                                                low_T[t].rearrange("p (h d) -> p h d", h=4), spread(levels[:, n, :], 4, 1),
                                                ALU.mult).then_inc(d_level, 1)
                if b == 0:
                    pool.wait_ge(g_exps, 1)
                else:
                    pool.wait_ge(r_state, b)
                nc.gpsimd.tensor_tensor(k_decayed.rearrange("p (k m c) -> p k m c", k=2, m=2),
                                        spread(qkv[:, 0, 1024 + 256 * b:1280 + 256 * b].rearrange("p (k c) -> p k c", k=2), 2),
                                        spread(decay_rest[:, 4 * b:4 * b + 4].rearrange("p (k m) -> p k m", k=2), 128, 3),
                                        ALU.mult).then_inc(r_keys, 1)
            for t in range(2):
                power_of(r16[:, t, 0:16], r16[:, t, 0:16])
            pre_norm()

        @block.vector
        def _(dve):
            chain = [0]

            def link(instruction):
                chain[0] += 1
                instruction.then_inc(dve_step, 1)
                dve.wait_ge(dve_step, chain[0])

            def split(i, r=0):
                if i >= N_ITEMS:
                    return
                dve.wait_ge(w_hi_done, i + 1 + 3 * r)
                nc.vector.tensor_tensor(w_lo[:, i % 3, :], raw[:, i % 3, :], w_hi[:, i % 3, :].bitcast(f32),
                                        ALU.subtract).then_inc(w_lo_done, 1)

            powers = [0]

            def power_of(instruction):
                powers[0] += 1
                instruction.then_inc(variance_ready, 1)
                dve.wait_ge(rstd_ready, powers[0])

            def turn_out(name, scale):
                n = TURNS.index(name)
                base = 8 if name == "gdn_out1" else 0
                for j in range(4):
                    dve.wait_ge(turned_hi, 4 * n + j + 1)
                    for k in range(2):
                        kk = base + 2 * j + k
                        last = nc.vector.scalar_tensor_tensor(aT_lo[:, kk, :], bank[4 + j][:, 256 * k:256 * k + 256],
                                                              scale(2 * j + k), aT_hi[:, kk, :].bitcast(f32),
                                                              ALU.mult, ALU.subtract)
                    last.then_inc(turned_lo, 1)

            def pre_norm(name):
                n = NORMS.index(name)
                for t in range(2):
                    dve.wait_ge(squares_ready, 2 * n + t + 1)
                    power_of(nc.vector.tensor_scalar(rstd[:, t:t + 1], sumsq[:, t:t + 1], 1.0 / D, EPS,
                                                     ALU.mult, ALU.add))
                    nc.vector.tensor_scalar(xn[:, t, :], x[:, t, :], rstd[:, t:t + 1], None, ALU.mult)\
                        .then_inc(rows_ready, 1)
                turn_out(name, lambda k: gains[:, n, k:k + 1])

            def post_norm(layer, n, factor):
                y0 = {"ff1": 0, "mix_out": 4, "ff2": 8}[layer]
                dve.wait_ge(y_squares, y0 + 4)
                pairs = sumsq[:, 0:4].rearrange("p (t h) -> p t h", h=2)
                link(nc.vector.tensor_tensor(rstd[:, 0:2], pairs[:, :, 0], pairs[:, :, 1], ALU.add))
                power_of(nc.vector.tensor_scalar(rstd[:, 0:2], rstd[:, 0:2], 1.0 / D, EPS, ALU.mult, ALU.add))
                link(nc.vector.tensor_scalar(rstd[:, 0:2], rstd[:, 0:2], factor, None, ALU.mult))
                dve.wait_ge(post_gain_loaded, 16 * (n + 1))
                for t in range(2):
                    for h in range(2):
                        c = slice(512 * h, 512 * h + 512)
                        nc.vector.scalar_tensor_tensor(xn[:, t, c], bank[2 * t + h][:, :], rstd[:, t:t + 1],
                                                       post_gain[:, c], ALU.mult, ALU.mult)\
                            .then_inc(dve_step, 1)
                        chain[0] += 1
                    dve.wait_ge(dve_step, chain[0])
                    nc.vector.tensor_tensor(x[:, t, :], x[:, t, :], xn[:, t, :], ALU.add).then_inc(x_ready, 1)

            def plain_sum(name):
                dve.wait_ge(item_done, FIRST[name] + dict(COUNTS)[name])
                for t in range(2):
                    nc.vector.tensor_tensor(x[:, t, 0:512], x[:, t, 0:512], bank[2 * t][:, :], ALU.add)
                    nc.vector.tensor_tensor(x[:, t, 512:1024], x[:, t, 512:1024], bank[2 * t + 1][:, :], ALU.add)\
                        .then_inc(x_ready, 1)

            def at_tile(table, f, q, tap):
                return table[:, bass.ds(f + 4 * q, 1), tap:tap + 1].rearrange("p a b -> p (a b)")

            def ffn(name):
                n_tiles, conv, f0 = FFNS[name]
                pre_norm(name)
                tap = P("ffn_conv")[:, 72 * (name == "glu2"):72 * (name == "glu2") + 72]
                tap = tap.rearrange("p (f t) -> p f t", t=3)

                def tile(f, i, q):
                    gate, up = bank[4 + f % 4][:, 0:256], bank[4 + f % 4][:, 256:512]
                    g = f_gate[:, f % 2, :]
                    if conv:
                        dve.wait_ge(gate_scaled, f0 - 44 + f + 1 + 4 * q)
                        c0 = 2 * (f0 - 44 + f)
                        nc.vector.scalar_tensor_tensor(g[:, 1:256], gate[:, 0:255], at_tile(tap, f, q, 1),
                                                       g[:, 1:256], ALU.mult, ALU.add).then_inc(conv_step, 1)
                        dve.wait_ge(conv_step, f0 - 44 + f + 1 + 4 * q)
                        nc.vector.scalar_tensor_tensor(g[:, 2:256], gate[:, 0:254], at_tile(tap, f, q, 0),
                                                       g[:, 2:256], ALU.mult, ALU.add).then_inc(gate_conv, 1)
                        gate = g
                    dve.wait_ge(gate_tanh, f0 + f + 1 + 4 * q)
                    nc.vector.scalar_tensor_tensor(f_tanh[:, f % 2, :], f_tanh[:, f % 2, :], 1.0, gate,
                                                   ALU.add, ALU.mult).then_inc(silu_step, 1)
                    dve.wait_ge(silu_step, f0 + f + 1 + 4 * q)
                    nc.vector.scalar_tensor_tensor(f_hid[:, f % 2, :], f_tanh[:, f % 2, :], 0.5, up,
                                                   ALU.mult, ALU.mult).then_inc(hid_ready, 1)
                    split(i + 3, 2 * q)
                    dve.wait_ge(hid_hi, f0 + f + 1 + 4 * q)
                    nc.vector.tensor_tensor(aT_lo[:, 8 + f % 4, :], f_hid[:, f % 2, :],
                                            aT_hi[:, 8 + f % 4, :].bitcast(f32), ALU.subtract).then_inc(hid_lo, 1)

                def down(m, i, q):
                    split(i + 3, 2 * q)

                ffn_order(dve, name, tile, down)

            def rope(t, n, cos, sin):
                v = proj[:, t, 0:64 * n].rearrange("p (h d) -> p h d", d=64)
                x1, x2 = v[:, :, 0:8], v[:, :, 8:16]
                parts = [rot[:, a, 0:8 * n].rearrange("p (h d) -> p h d", d=8) for a in range(4)]
                cos, sin = spread(cos, n, 1), spread(sin, n, 1)
                for to, a, b in zip(parts, (x1, x2, x2, x1), (cos, sin, cos, sin)):
                    last = nc.vector.tensor_tensor(to, a, b, ALU.mult)
                link(last)
                nc.vector.tensor_tensor(x1, parts[0], parts[1], ALU.subtract)
                return nc.vector.tensor_tensor(x2, parts[2], parts[3], ALU.add)

            def attention(layer, finish):
                groups, base = GROUPS[layer], GROUPS_BEFORE[layer]

                def maximum(n):
                    t, h0, count = groups[n]
                    dve.wait_ge(scores_ready, base + n + 1)
                    to = neg_max[:, t, h0:h0 + count]
                    last = nc.vector.tensor_reduce(to, bank[4 + n % 2][:, :].rearrange("p (h c) -> p h c", h=count),
                                                   AX.X, ALU.max, negate=True)
                    if layer == "att_in":
                        link(last)
                        last = nc.vector.tensor_tensor(to, to, neg_sinks[:, h0:h0 + count], ALU.min)
                    last.then_inc(neg_max_ready, 1)

                maximum(0)
                for n, (t, h0, count) in enumerate(groups):
                    if n + 1 < len(groups):
                        maximum(n + 1)
                    dve.wait_ge(expo_turned, base + n + 1)
                    if n >= 2:
                        dve.wait_ge(pv_done, base + n - 1)
                    nc.vector.tensor_copy(expoT[:, n % 2, :], bank[6 + n % 2][:, :]).then_inc(expoT_ready, 1)
                    if n == len(groups) // 3:
                        finish(0, base + len(groups) // 3)
                finish(1, base + len(groups))

            def mix_finish(t, groups):
                dve.wait_ge(pv_done, groups)
                c = coef[:, t, :]
                link(nc.vector.reciprocal(c[:, 0:24], total[:, t, 0:24]))
                g = gates[:, t, :].rearrange("p (h b) -> p h b", b=3)
                nc.vector.tensor_scalar(c[:, 4:8], c[:, 4:8], lam[:, 5:6], None, ALU.mult)
                nc.vector.tensor_tensor(c[:, 8:16], c[:, 8:16], g[:, :, 1], ALU.mult)
                link(nc.vector.tensor_tensor(c[:, 16:24], c[:, 16:24], g[:, :, 2], ALU.mult))
                for b in range(2):
                    last = nc.vector.tensor_tensor(mixed[:, 512 * b:512 * b + 512].rearrange("p (h d) -> p h d", h=4),
                                                   bank[b][:, :].rearrange("p (h d) -> p h d", h=4),
                                                   spread(c[:, 4 * b:4 * b + 4], 128), ALU.mult)
                link(last)
                o = xn[:, t, 0:512].rearrange("p (h d) -> p h d", h=4)
                link(nc.vector.tensor_tensor(xn[:, t, 0:512], mixed[:, 0:512], mixed[:, 512:1024], ALU.add))
                for b in range(2):
                    last = nc.vector.tensor_tensor(mixed[:, 512 * b:512 * b + 512].rearrange("p (h d) -> p h d", h=8),
                                                   bank[2 + b][:, :].rearrange("p (h d) -> p h d", h=8),
                                                   spread(c[:, 8 + 8 * b:16 + 8 * b], 64), ALU.mult)
                last.then_inc(out_read, 1)
                dve.wait_ge(out_read, t + 1)
                for b in range(2):
                    link(nc.vector.tensor_tensor(xn[:, t, 512:1024], xn[:, t, 512:1024],
                                                 mixed[:, 512 * b:512 * b + 512], ALU.add))
                link(nc.vector.tensor_tensor(mixed[:, 0:512], xn[:, t, 0:512], xn[:, t, 0:512], ALU.mult))
                r = r16[:, t, 0:4]
                link(nc.vector.tensor_reduce(r, mixed[:, 0:512].rearrange("p (h d) -> p h d", h=4), AX.X, ALU.add))
                power_of(nc.vector.tensor_scalar(r, r, 1.0 / 128, EPS, ALU.mult, ALU.add))
                link(nc.vector.tensor_scalar(r, r, 0.8, None, ALU.mult))
                nc.vector.tensor_tensor(o, o, spread(r, 128), ALU.mult).then_inc(rows_ready, 1)

            def att_finish(t, groups):
                dve.wait_ge(pv_done, groups)
                nc.vector.tensor_tensor(coef[:, t, 16:32], P("sinks"), neg_max[:, t, 0:16], ALU.add)\
                    .then_inc(sink_args, 1)
                dve.wait_ge(sink_expo, t + 1)
                link(nc.vector.tensor_tensor(coef[:, t, 0:16], total[:, t, 0:16], coef[:, t, 16:32], ALU.add))
                link(nc.vector.reciprocal(coef[:, t, 0:16], coef[:, t, 0:16]))
                for b in range(2):
                    last = nc.vector.tensor_tensor(xn[:, t, 512 * b:512 * b + 512].rearrange("p (h d) -> p h d", h=8),
                                                   bank[b][:, :].rearrange("p (h d) -> p h d", h=8),
                                                   spread(coef[:, t, 8 * b:8 * b + 8], 64), ALU.mult)
                last.then_inc(out_read, 1)
                dve.wait_ge(out_read, 2 + t + 1)
                nc.vector.memset(one_s, 1.0).then_inc(rows_ready, 1)

            def compressed_blocks():
                pe_terms = P("pe").rearrange("p (v l) -> p v l", v=2)
                for kv in range(2):
                    dve.wait_ge(c_copied, kv + 1)
                    sums = c_sums[:, kv, :].rearrange("p (l c) -> p l c", c=32)
                    for g in range(2):
                        view = blockT[:, kv, g, :].rearrange("p (c l) -> p l c", l=16)[:, 0:16:2, :]
                        for part in range(2):
                            term = spread(pe_terms[:, kv, 8 * part:8 * part + 8], 15)
                            last = nc.vector.tensor_tensor(sums[:, 8 * part:8 * part + 8, 15 * g:15 * g + 15],
                                                           view[:, :, part:part + 15], term, ALU.add)
                    link(last)
                    link(nc.vector.tensor_copy(c_block(aT_hi, kv)[:, :, 0:30], sums[:, :, 0:30]))
                    nc.vector.tensor_tensor(c_block(aT_lo, kv)[:, :, 0:30], sums[:, :, 0:30],
                                            c_block(aT_hi, kv)[:, :, 0:30].bitcast(f32), ALU.subtract)                        .then_inc(c_blocks, 1)

            def compressed_hidden():
                dve.wait_ge(item_done, FIRST["cmp"] + 4)
                for b in range(4):
                    last = nc.vector.tensor_copy(hidden[:, b, 0:30], bank[b][:, 0:30])
                link(last)
                x_, y_ = hidden[:, :, 0:30], hidden2[:, :, 0:30]
                link(nc.vector.tensor_tensor(y_, x_, x_, ALU.mult))
                link(nc.vector.tensor_scalar(y_, y_, 0.044715, 1.0, ALU.mult, ALU.add))
                nc.vector.tensor_tensor(y_, y_, x_, ALU.mult).then_inc(c_gelu_arg, 1)
                dve.wait_ge(c_tanh, 1)
                link(nc.vector.scalar_tensor_tensor(y_, y_, 1.0, x_, ALU.add, ALU.mult))
                nc.vector.tensor_scalar(y_, y_, 0.5, None, ALU.mult).then_inc(c_hidden, 1)
                link(nc.vector.memset(kc_diag, 0.0))
                dve.wait_ge(c_products, 1)
                nc.vector.tensor_copy(v_cmp[0:15, :], bank[1][0:15, 0:128]).then_inc(c_values, 1)
                nc.vector.tensor_copy(kc_diag[0:64, 0, 0:15], bank[0][0:64, 0:15])
                nc.vector.tensor_copy(kc_diag[64:128, 1, 0:15], bank[0][64:128, 15:30])
                dve.wait_ge(c_spread, 1)
                nc.vector.tensor_tensor(v_diag.rearrange("p (g j) d -> p g j d", g=2),
                                        spread(bank[2][:, 0:128].rearrange("p (g d) -> p g d", g=2), 4),
                                        spread(C("own_head").rearrange("p (g j) -> p g j", g=2), 64, 3), ALU.mult)                    .then_inc(c_operands, 1)
                valid = C("cmp_valid").rearrange("p (t c) -> p t c", t=2)
                link(nc.vector.tensor_scalar(c_mask, valid, -NEG, NEG, ALU.mult, ALU.add))
                for t in range(2):
                    s = cmp_s[:, t]
                    dve.wait_ge(c_scores, t + 1)
                    link(nc.vector.tensor_tensor(s, bank[t][:, 0:128].rearrange("p (h c) -> p h c", h=8),
                                                 spread(c_mask[:, t, :], 8, 1), ALU.add))
                    m = neg_max[:, t, 24:32]
                    link(nc.vector.tensor_reduce(m, s, AX.X, ALU.max, negate=True))
                    nc.vector.tensor_tensor(s, s, spread(m, 16), ALU.add).then_inc(c_masked, 1)
                for t in range(2):
                    s = cmp_s[:, t]
                    dve.wait_ge(c_expo, t + 1)
                    link(nc.vector.tensor_reduce(total[:, t, 24:32], s, AX.X, ALU.add))
                    nc.vector.tensor_tensor(s, s, spread(valid[:, t, :], 8, 1), ALU.mult).then_inc(c_probs, 1)
                    link(nc.vector.reciprocal(coef[:, t, 24:32], total[:, t, 24:32]))
                    g = gates[:, t, :].rearrange("p (g j b) -> p g j b", g=2, j=4)
                    c = coef[:, t, 0:8].rearrange("p (g j) -> p g j", g=2)
                    link(nc.vector.tensor_tensor(c, coef[:, t, 24:32].rearrange("p (j g) -> p g j", j=4),
                                                 g[:, :, :, 0], ALU.mult))
                    dve.wait_ge(c_probs_turned, t + 1)
                    nc.vector.tensor_copy(c_expT, bank[2][:, 128 * t:128 * t + 128]).then_inc(c_probsT, 1)
                    dve.wait_ge(c_out, t + 1)
                    nc.vector.tensor_tensor(xn[:, t, 512:1024].rearrange("p (h d) -> p h d", h=8),
                                            bank[3][:, :].rearrange("p (h d) -> p h d", h=8),
                                            spread(coef[:, t, 0:8], 64), ALU.mult).then_inc(c_out_read, 1)

            def convolved():
                taps = P("gdn_conv").rearrange("p (f t) -> p f t", t=4)

                def body(k, r):
                    dve.wait_ge(g_scaled, k + 1 + 3 * r)
                    for back in (1, 2, 3):
                        for n in range(2):
                            tap = taps[:, bass.ds(2 * k + n + 6 * r, 1), 3 - back:4 - back].rearrange("p a b -> p (a b)")
                            to = g_conv[:, 256 * n + back:256 * n + 256]
                            last = nc.vector.scalar_tensor_tensor(to, bank[4 + k % 3][:, 256 * n:256 * n + 256 - back],
                                                                  tap, to, ALU.mult, ALU.add)
                        if back < 3:
                            last.then_inc(g_tap, 1)
                            dve.wait_ge(g_tap, 2 * k + back + 6 * r)
                    last.then_inc(g_conv_ready, 1)
                    split(FIRST["gdn_qkv"] + k + 3, r)
                    dve.wait_ge(g_tanh_ready, k + 1 + 3 * r)
                    if k >= 3 or not isinstance(r, int):
                        dve.wait_ge(g_rows_turned, k - 2 + 3 * r)
                    nc.vector.scalar_tensor_tensor(g_silu[:, k % 3, :], g_tanh, 1.0, g_conv, ALU.add, ALU.mult)\
                        .then_inc(g_silu_ready, 1)

                rounds(dve, 16, body)

            def delta_setup():
                dve.wait_ge(g_small, 1)
                link(nc.vector.tensor_copy(ba, bank[7][:, 0:128].rearrange("p (t c) -> p t c", t=2)[:, :, 0:32]))
                link(nc.vector.tensor_tensor(ba[:, :, 16:32], ba[:, :, 16:32], spread(P("dt_bias"), 2, 1), ALU.add))
                link(nc.vector.tensor_scalar(soft[:, :, 0:16], ba[:, :, 16:32], -1.0, None, ALU.mult))
                nc.vector.tensor_tensor(soft[:, :, 0:16], soft[:, :, 0:16], ba[:, :, 16:32], ALU.min)\
                    .then_inc(g_soft_args, 1)
                link(nc.vector.tensor_scalar(ba[:, :, 16:32], ba[:, :, 16:32], 0.0, None, ALU.max))
                dve.wait_ge(g_soft_done, 1)
                nc.vector.tensor_scalar(beta, soft[:, :, 16:32], 0.5, 0.5, ALU.mult, ALU.add)
                link(nc.vector.tensor_tensor(decay, ba[:, :, 16:32], soft[:, :, 0:16], ALU.add))
                nc.vector.scalar_tensor_tensor(decay, decay, -1.0, spread(rate, 2, 1), ALU.mult, ALU.mult)\
                    .then_inc(g_decay, 1)
                dve.wait_ge(g_sums, 1)
                link(nc.vector.tensor_copy(decay_sum, bank[7][:, 0:32].rearrange("p (t h) -> p t h", t=2)))
                nc.vector.tensor_tensor(decay_rest, bank[7][:, 32:48], decay_sum[:, 0, :], ALU.subtract)\
                    .then_inc(g_sums_read, 1)
                for t in range(2):
                    dve.wait_ge(g_squares, t + 1)
                    r = r16[:, t, 0:16]
                    link(nc.vector.tensor_reduce(r, xn[:, :, :].rearrange("p t (h d) -> p (t h) d", d=128), AX.X,
                                                 ALU.add))
                    power_of(nc.vector.tensor_scalar(r, r, EPS, None, ALU.add))
                    link(nc.vector.tensor_scalar(r16[:, t, 0:8], r16[:, t, 0:8], 128 ** -0.5, None, ALU.mult))
                    v = qkv[:, t, 0:2048].rearrange("p (h d) -> p h d", d=128)
                    nc.vector.tensor_tensor(v, v, spread(r, 128), ALU.mult).then_inc(g_normed, 1)
                dve.wait_ge(g_exps, 1)
                link(nc.vector.tensor_tensor(beta_decay, beta[:, 1, :], decay_exp[:, 1, :], ALU.mult))

            def delta(b):
                h = 4 * b
                col = [slice(128 * c, 128 * c + 128) for c in range(4)]

                def four(ap):
                    return ap.rearrange("p (h d) -> p h d", h=4)

                v = [qkv[:, t, 2048 + 512 * b:2560 + 512 * b] for t in range(2)]
                dve.wait_ge(g_qk_copied, 8)
                for t in range(2):
                    dve.wait_ge(d_rows, 2 * b + t + 1)
                    for c in range(4):
                        last = nc.vector.tensor_scalar(level[t][0][:, col[c]], bank[4 * t][:, col[c]],
                                                       decay_sum[:, t, h + c:h + c + 1], 0.0, ALU.subtract, ALU.max)
                    last.then_inc(d_diff, 1)
                for t in range(2):
                    dve.wait_ge(d_masked, 2 * b + t + 1)
                    prods = bank[4 * t + 1]
                    for c in range(4):
                        nc.vector.scalar_tensor_tensor(prod[t][:, col[c]], prods[:, col[c // 2]],
                                                       beta[:, t, h + c:h + c + 1], level[t][0][:, col[c]],
                                                       ALU.mult, ALU.mult)
                    pairs = prods[:, 256:512].rearrange("p (k c) -> p k c", k=2)
                    nc.vector.tensor_tensor(inv[t].rearrange("p (k m c) -> p k m c", k=2, m=2), spread(pairs, 2),
                                            level[t][0].rearrange("p (k m c) -> p k m c", k=2, m=2), ALU.mult)\
                        .then_inc(d_mats, 1)
                for t in range(2):
                    last = nc.vector.tensor_tensor(four(v[t]), four(v[t]), spread(beta[:, t, h:h + 4], 128), ALU.mult)
                last.then_inc(r_inputs, 1)
                for t in range(2):
                    dve.wait_ge(d_level, 14 * b + t + 1)
                    nc.vector.tensor_tensor(four(inv_T[t]), spread(ident, 4, 1), four(level[t][0]), ALU.subtract)\
                        .then_inc(d_first, 1)
                for n in range(1, len(LEVELS)):
                    for t in range(2):
                        dve.wait_ge(d_step, 12 * b + 2 * (n - 1) + t + 1)
                        last = nc.vector.tensor_tensor(inv_T[t], inv_T[t], bank[4 * t + 1][:, :], ALU.subtract)
                        if n < len(LEVELS) - 1:
                            if n == 1:
                                dve.wait_ge(d_first_T, 2 * b + t + 1)
                            last = nc.vector.tensor_tensor(inv[t], inv[t], bank[4 * t + 2][:, :], ALU.subtract)
                        last.then_inc(d_applied, 1)
                dve.wait_ge(r_out, 2 * b + 1)
                nc.vector.tensor_copy(v[0], bank[1][:, :]).then_inc(r_out_read, 1)
                dve.wait_ge(r_read, b + 1)
                link(nc.vector.tensor_tensor(four(prod[1]), four(bank[4][:, :]), spread(beta_decay[:, h:h + 4], 128),
                                             ALU.mult))
                nc.vector.tensor_tensor(v[1], v[1], prod[1], ALU.subtract).then_inc(r_rhs, 1)
                link(nc.vector.tensor_tensor(four(inv[1]), four(bank[5][:, :]), spread(decay_exp[:, 1, h:h + 4], 128),
                                             ALU.mult))
                dve.wait_ge(r_out, 2 * b + 2)
                nc.vector.tensor_tensor(v[1], inv[1], bank[7][:, :], ALU.add).then_inc(r_out_read, 1)

            def gated():
                for t in range(2):
                    dve.wait_ge(o_squares, t + 1)
                    r = r16[:, t, 0:16]
                    link(nc.vector.tensor_reduce(r, xn[:, :, :].rearrange("p t (h d) -> p (t h) d", d=128), AX.X,
                                                 ALU.add))
                    power_of(nc.vector.tensor_scalar(r, r, 1.0 / 128, EPS, ALU.mult, ALU.add))
                    v = qkv[:, t, 2048:4096].rearrange("p (h d) -> p h d", d=128)
                    nc.vector.tensor_tensor(v, v, spread(r, 128), ALU.mult).then_inc(g_normed, 1)
                dve.wait_ge(g_normed, 4)

                def body(k, r):
                    s = g_work[:, k % 3, :]
                    dve.wait_ge(z_tanh, k + 1 + 3 * r)
                    nc.vector.scalar_tensor_tensor(s, s, 1.0, bank[4 + k % 3][:, :], ALU.add, ALU.mult)\
                        .then_inc(copied, 1)
                    dve.wait_ge(copied, 17 + k + 1 + 3 * r)
                    o = qkv[:, :, bass.ds(2048 + 256 * k + 768 * r, 256)]
                    nc.vector.scalar_tensor_tensor(o, s.rearrange("p (t c) -> p t c", t=2), 0.5, o,
                                                   ALU.mult, ALU.mult).then_inc(z_used, 1)
                    split(FIRST["gdn_z"] + k + 3, r)

                rounds(dve, 8, body)

            dve.wait_ge(x_loaded, 32)
            nc.vector.memset(one_s, 1.0).then_inc(x_ready, 2)
            dve.wait_ge(setup_hi, 1)
            nc.vector.tensor_tensor(ws_lo[:, :, :], P("small").rearrange("p (k c) -> p k c", c=56),
                                    ws_hi[:, :, :].bitcast(f32), ALU.subtract).then_inc(setup_done, 1)
            dve.wait_ge(con_loaded, 16)
            link(nc.vector.memset(masks[:, :, :], 0.0))
            nc.vector.tensor_copy(ident_b[:, :], ident)
            nc.vector.tensor_copy(masks[:, 0, :].rearrange("p (h c) -> p h c", h=4), spread(C("causal"), 4, 1))
            for m in (1, 2):
                rows = masks[:, m, :].rearrange("p (h a c) -> p h a c", h=2, a=2)
                if m == 2:
                    nc.vector.tensor_copy(rows[:, :, 0, :], spread(C("before"), 2, 1))
                nc.vector.tensor_copy(rows[:, :, 1, :], spread(C("causal"), 2, 1)).then_inc(setup_done, 1)
            for i in range(3):
                split(i)
            dve.wait_ge(par_loaded, 32)
            pairs = P("lambdas").rearrange("p (a b c) -> p a b c", a=2, b=2)
            link(nc.vector.tensor_tensor(mixed[:, 0:128].rearrange("p (a c) -> p a c", a=2), pairs[:, :, 0, :],
                                         pairs[:, :, 1, :], ALU.mult))
            nc.vector.tensor_reduce(lam[:, 0:2], mixed[:, 0:128].rearrange("p (a c) -> p a c", a=2), AX.X, ALU.add)\
                .then_inc(lam_args, 1)
            link(nc.vector.tensor_copy(pos, pos_i[:, :]))
            for t in range(2):
                last = nc.vector.tensor_scalar(ang[:, t, 0:8], C("inv_freq"), pos[:, t:t + 1], None, ALU.mult)
            link(last)
            link(nc.vector.tensor_scalar(trig[:, 3, :].rearrange("p (t c) -> p t c", t=2), ang[:, :, 0:8],
                                         0.15915494309189535, 12582912.0, ALU.mult, ALU.add))
            link(nc.vector.tensor_scalar(trig[:, 3, :], trig[:, 3, :], 12582912.0, None, ALU.subtract))
            rest = trig[:, 0, :]
            link(nc.vector.tensor_copy(rest.rearrange("p (t c) -> p t c", t=2), ang[:, :, 0:8]))
            for part in (6.28125, 0.0019350051879882812, 3.019916e-07):
                link(nc.vector.scalar_tensor_tensor(rest, trig[:, 3, :], -part, rest, ALU.mult, ALU.add))
            nc.vector.tensor_scalar(rest, rest, 3.1415925, -3.1415925, ALU.min, ALU.max).then_inc(trig_args, 1)
            dve.wait_ge(lam_expo, 1)
            link(nc.vector.tensor_tensor(lam[:, 4:5], lam[:, 2:3], lam[:, 3:4], ALU.subtract))
            nc.vector.tensor_scalar(lam[:, 5:6], lam[:, 4:5], -1.0, -0.2, ALU.mult, ALU.add)
            dve.wait_ge(trig_done, 1)
            nc.vector.tensor_copy(cos_sin[:, 2:4, :].rearrange("p a b -> p (a b)"), trig[:, 1, :])
            link(nc.vector.tensor_tensor(trig[:, 3, :], trig[:, 2, :], trig[:, 2, :], ALU.mult))
            nc.vector.tensor_scalar(cos_sin[:, 0:2, :].rearrange("p a b -> p (a b)"), trig[:, 3, :], -2.0, 1.0,
                                    ALU.mult, ALU.add)
            link(nc.vector.tensor_scalar(neg_sinks, P("sinks"), -1.0, None, ALU.mult))
            ffn("ff1")
            post_norm("ff1", 0, 0.5)
            pre_norm("mix_in")
            rounds(dve, 9, lambda k, r: split(FIRST["mix_in"] + k + 3, r))
            split(FIRST["mix_in"] + 12)
            split(FIRST["mix_in"] + 13)
            dve.wait_ge(copied, 10)
            for t in range(2):
                last = nc.vector.tensor_copy(mixed[:, 512 * t:512 * t + 512].rearrange("p (a m d) -> p a m d", a=4, m=2),
                                             spread(proj[:, t, 2304:2560].rearrange("p (a d) -> p a d", a=4), 2))
            last.then_inc(c_twice, 1)
            table = C("rope").rearrange("p (f t c) -> p f t c", f=2, t=2)
            rope(0, 28, table[:, 0, 0, :], table[:, 1, 0, :]).then_inc(dve_step, 1)
            chain[0] += 1
            dve.wait_ge(dve_step, chain[0])
            rope(1, 28, table[:, 0, 1, :], table[:, 1, 1, :]).then_inc(heads_ready, 1)
            dve.wait_ge(gates_tanh, 1)
            link(nc.vector.tensor_scalar(gates, gates, 0.5, 0.5, ALU.mult, ALU.add))
            compressed_blocks()
            for i in range(FIRST["cmp"], FIRST["cmp"] + 4):
                split(i + 3)
            compressed_hidden()
            attention("mix_in", mix_finish)
            turn_out("mix_out", nsa_scale)
            for i in range(FIRST["mix_out"], FIRST["mix_out"] + 4):
                split(i + 3)
            post_norm("mix_out", 1, 1.0)
            ffn("ff2")
            post_norm("ff2", 2, 0.5)
            pre_norm("att_in")
            rounds(dve, 6, lambda k, r: split(FIRST["att_in"] + k + 3, r))
            dve.wait_ge(copied, 17)
            gain = P("qk_gain")
            for t in range(2):
                dve.wait_ge(head_squares, t + 1)
                r = r16[:, t, 0:20]
                v = proj[:, t, 0:1280].rearrange("p (h d) -> p h d", d=64)
                link(nc.vector.tensor_reduce(r, proj[:, t, 1536:2816].rearrange("p (h d) -> p h d", d=64), AX.X, ALU.add))
                power_of(nc.vector.tensor_scalar(r, r, 1.0 / 64, EPS, ALU.mult, ALU.add))
                link(nc.vector.tensor_tensor(v, v, spread(r, 64), ALU.mult))
                nc.vector.tensor_tensor(v[:, 0:16, :], v[:, 0:16, :], spread(gain[:, 0:64], 16, 1), ALU.mult)
                link(nc.vector.tensor_tensor(v[:, 16:20, :], v[:, 16:20, :], spread(gain[:, 64:128], 4, 1), ALU.mult))
                link(rope(t, 20, cos_sin[:, t, :], cos_sin[:, 2 + t, :]))
            nc.vector.memset(one_s, 1.0).then_inc(heads_ready, 1)
            attention("att_in", att_finish)
            turn_out("att_out", lambda k: 1.0)
            for i in range(FIRST["att_out"], FIRST["att_out"] + 4):
                split(i + 3)
            plain_sum("att_out")
            ffn("glu1")
            plain_sum("glu1")
            pre_norm("gdn_qkv")
            convolved()
            delta_setup()
            for b in range(4):
                delta(b)
            gated()
            dve.wait_ge(z_used, 8)
            nc.vector.memset(one_s, 1.0).then_inc(rows_ready, 4)
            turn_out("gdn_out0", lambda k: P("gdn_norm"))
            turn_out("gdn_out1", lambda k: P("gdn_norm"))
            for i in range(FIRST["gdn_out"], FIRST["gdn_out"] + 8):
                split(i + 3)
            plain_sum("gdn_out")
            ffn("glu2")
            plain_sum("glu2")


def _pack_columns(w, blocks):
    k = w.shape[0] // 128
    return w.reshape(k, 128, w.shape[1] // blocks, blocks).transpose(2, 1, 0, 3)


def _ffn_items(w_gate, w_up, w_down):
    gate = _pack_columns(w_gate, 128)
    up = _pack_columns(w_up, 128)
    n = gate.shape[0]
    tiles = [_np.stack([gate[f], up[f]], 1).reshape(128, ITEM) for f in range(n)]
    down = w_down.reshape(n // 2, 2, 128, D).transpose(0, 2, 1, 3).reshape(n // 2, 128, ITEM)
    order = [tiles[0], tiles[1]]
    for m in range(1, n // 2):
        order += [tiles[2 * m], tiles[2 * m + 1], down[m - 1]]
    return order + [down[n // 2 - 1]]


def _column_items(w):
    out = []
    for block in _pack_columns(w, 256):
        for h in range(block.shape[1] // 8):
            out.append(block[:, 8 * h:8 * h + 8].reshape(128, ITEM))
    return out


def _heads(cols, order, size=64):
    return _np.concatenate([cols[:, size * h:size * h + size] for h in order], 1)


def _column(v, n):
    return v.reshape(n, 128).T


def _stream(a):
    w = a["w_in"][0]
    cut = _np.split(w, _np.cumsum([512, 512, 512, 512] + [128] * 6), axis=1)
    dq, dk, dv, nq, kc, vc, ks, vs, kw, vw, gl = cut
    mix = _np.concatenate([dq, dk, _heads(nq, MIX_Q_ORDER), ks, kw, dv, kc, vc, vs, vw], 1)
    att = a["attn_w_in_2"][0]
    att = _np.concatenate([_heads(att[:, :1024], ATT_Q_ORDER), att[:, 1024:]], 1)
    gdn = a["gdn_w_in_2"][0]
    up0, up1 = a["ffn_w_up_2"]
    items = _ffn_items(a["ff1_w_gate"][0], a["ff1_w_up"][0], a["ff1_w_down"][0])
    items += _column_items(mix)
    items += _column_items(a["cmp_k_w1"][0]) + _column_items(a["cmp_v_w1"][0])
    items += _column_items(a["w_out"][0])
    items += _ffn_items(a["ff2_w_gate"][0], a["ff2_w_up"][0], a["ff2_w_down"][0])
    items += _column_items(att) + _column_items(a["attn_w_out_2"][0])
    items += _ffn_items(up0[:, :3072], up0[:, 3072:], a["ffn_w_down_2"][0])
    items += _column_items(gdn[:, :6144]) + _column_items(a["gdn_w_out_2"][0])
    items += _ffn_items(up1[:, :3072], up1[:, 3072:], a["ffn_w_down_2"][1])
    small = _np.concatenate([gl, gdn[:, 6144:]], 1).reshape(8, 128, 56).transpose(1, 0, 2)
    return _np.stack(items), small.reshape(128, 448)


def _parameters(a, small):
    def rows(v):
        return _np.broadcast_to(v.reshape(1, -1), (128, v.size))

    def taps(w):
        return w.reshape(w.shape[0], -1, 128).transpose(2, 1, 0).reshape(128, -1)

    def pe(v):
        return v.reshape(16, 128).T

    gains = [a["ff1_norm_pre"][0], a["mix_norm_pre"][0], a["ff2_norm_pre"][0], a["mixer_norm_2"][0],
             a["ffn_norm_2"][0], a["mixer_norm_2"][1], a["ffn_norm_2"][1]]
    w2k = a["cmp_k_w2"][0].reshape(2, 128, 1, 64).transpose(1, 0, 2, 3)
    p = {
        "gains": _np.concatenate([_column(g, 8) for g in gains], 1),
        "subln": a["diff_subln"][0].reshape(128, 1),
        "gdn_norm": a["gdn_norm_2"][0].reshape(128, 1),
        "gdn_conv": taps(a["gdn_conv_2"][0]),
        "ffn_conv": _np.concatenate([taps(a["ffn_conv_2"][0]), taps(a["ffn_conv_2"][1])], 1),
        "ffn_bias": _np.concatenate([_column(a["ffn_conv_b_2"][0], 24), _column(a["ffn_conv_b_2"][1], 24)], 1),
        "pe": _np.concatenate([pe(a["cmp_pe_k"][0]), pe(a["cmp_pe_v"][0])], 1),
        "w2k": _np.broadcast_to(w2k, (128, 2, 2, 64)).reshape(128, 256),
        "w2v": a["cmp_v_w2"][0].reshape(2, 128, 64).transpose(1, 0, 2).reshape(128, 128),
        "lambdas": rows(_np.concatenate([a["lambda_q1"], a["lambda_k1"], a["lambda_q2"], a["lambda_k2"]], 1)),
        "qk_gain": rows(_np.concatenate([a["attn_q_gain_2"], a["attn_k_gain_2"]], 1)),
        "sinks": rows(a["attn_sinks_2"]),
        "a_log": rows(a["gdn_a_log_2"]),
        "dt_bias": rows(a["gdn_dt_bias_2"]),
        "small": small,
    }
    assert list(p) == list(PARAMS) and all(p[n].shape == (128, PARAMS[n]) for n in p)
    return _np.concatenate(list(p.values()), 1)


def _constants():
    i, j = _np.arange(128)[:, None], _np.arange(128)[None, :]
    f = lambda m: m.astype(_np.float32)
    block = [(i // s != j // s) & (i // (2 * s) == j // (2 * s)) & (i < j) for s in LEVELS]
    t = _np.arange(256).reshape(2, 128).T[:, :, None]
    valid = (_np.arange(16) < 15) & (_np.arange(16) * 16 + 31 <= t)
    inv = 500000.0 ** (-_np.arange(0, 16, 2, dtype=_np.float32) / 16)
    inv = inv.astype(_np.float32)
    angle = t.astype(_np.float32) * inv
    c = {
        "ident": f(i == j),
        "causal": NEG * f(j > i),
        "before": NEG * f(j <= i),
        "upto": f(i <= j),
        "tril": f(j <= i),
        "levels": _np.concatenate([f(b) for b in block], 1),
        "cmp_valid": f(valid).reshape(128, 32),
        "own_head": f(i // 16 == _np.array([2 * (h % 4) + h // 4 for h in range(8)])[None, :]),
        "spread": f((i == j % 16) & (i < 15)),
        "rope": _np.stack([_np.cos(angle), _np.sin(angle)], 1).reshape(128, 32),
        "inv_freq": _np.broadcast_to(inv, (128, 8)),
        "ones": _np.ones((128, 128)),
    }
    assert list(c) == list(CONSTS) and all(c[n].shape == (128, CONSTS[n]) for n in c)
    return _np.concatenate([v.astype(_np.float32) for v in c.values()], 1)


def kernel(**inputs):
    import concourse.bacc as _bacc
    from concourse.bass_utils import run_bass_kernel_spmd as _run

    a = {k: _np.asarray(v) for k, v in inputs.items()}
    stream, small = _stream(a)
    arrays = {
        "weights": stream,
        "params": _parameters(a, small),
        "consts": _constants(),
        "x": a["x"].reshape(SEQ, D),
        "post_gains": _np.concatenate([a["ff1_norm_post"], a["mix_norm_post"], a["ff2_norm_post"]], 0),
        "positions": a["positions_2"].reshape(2, 128).T,
    }
    arrays = {k: _np.ascontiguousarray(v) for k, v in arrays.items()}
    nc = _bacc.Bacc("TRN2", target_bir_lowering=False, num_devices=1)
    ins = {k: nc.dram_tensor(k, v.shape, mybir.dt.from_np(v.dtype), kind="ExternalInput").ap()
           for k, v in arrays.items()}
    out = nc.dram_tensor("out", (SEQ, D), mybir.dt.float32, kind="ExternalOutput").ap()
    two_blocks(nc, ins, out)
    r = _run(nc, [arrays], core_ids=[0])
    return r.results[0]["out"].reshape(1, SEQ, D)
```

```python
from contextlib import ExitStack

import numpy as _np
import concourse.bass as bass
from concourse import mybir

SEQ, D = 256, 1024
ITEM = 2048
EPS = 1e-6
NEG = -1e30
MIX_Q_ORDER = [0, 4, 1, 5, 2, 6, 3, 7]
ATT_Q_ORDER = [8 * p + 4 * a + j for p in range(2) for j in range(4) for a in range(2)]
ATT_HEADS = [4 * g + h for g in range(4) for h in (0, 2, 1, 3)]
LEVELS = [1, 2, 4, 8, 16, 32, 64]
PARAMS = {"gains": 56, "subln": 1, "gdn_norm": 1, "gdn_conv": 128, "ffn_conv": 144, "ffn_bias": 48, "pe": 32,
          "w2k": 256, "w2v": 128, "lambdas": 256, "qk_gain": 128, "sinks": 16, "a_log": 16, "dt_bias": 16,
          "small": 448}
CONSTS = {"ident": 128, "causal": 128, "before": 128, "upto": 128, "tril": 128, "levels": 128 * len(LEVELS),
          "cmp_valid": 32, "own_head": 8, "spread": 128, "rope": 32, "inv_freq": 8, "ones": 128}

COUNTS = [("ff1", 33), ("mix_in", 15), ("mix_out", 4), ("ff2", 33), ("att_in", 6), ("att_out", 4),
          ("glu1", 36), ("gdn_qkv", 16), ("gdn_z", 8), ("gdn_out", 8), ("glu2", 36)]
FIRST, N_ITEMS = {}, 0
for _name, _n in COUNTS:
    FIRST[_name] = N_ITEMS
    N_ITEMS += _n
FFNS = {"ff1": (22, False, 0), "ff2": (22, False, 22), "glu1": (24, True, 44), "glu2": (24, True, 68)}
TURNS = ["ff1", "mix_in", "mix_out", "ff2", "att_in", "att_out", "glu1", "gdn_qkv", "gdn_out0", "gdn_out1", "glu2"]
NORMS = ["ff1", "mix_in", "ff2", "att_in", "glu1", "gdn_qkv", "glu2"]
RESULTS = ["ff1", "mix_out", "ff2", "att_out", "glu1", "gdn_out", "glu2"]
MIX_ORDER = [9, 0, 1, 2, 3, 11, 12, 13, 14, 4, 5, 6, 7, 8, 10]
TURN_AT = [3, 4, 5, 6, 10, 11, 12]


def two_blocks(nc, ins, out):
    f32, f32r, bf16 = mybir.dt.float32, mybir.dt.float32r, mybir.dt.bfloat16
    ALU, ACT, AX = mybir.AluOpType, mybir.ActivationFunctionType, mybir.AxisListType
    ctx = ExitStack()
    with ctx:
        def sb(name, shape, dt=f32):
            return ctx.enter_context(nc.sbuf_tensor(name, shape, dt))

        def sem(name):
            return ctx.enter_context(nc.semaphore(name))

        raw = sb("raw", [128, 3, ITEM])
        w_hi = sb("w_hi", [128, 3, ITEM], f32r)
        w_lo = sb("w_lo", [128, 3, ITEM], f32r)
        aT_hi = sb("aT_hi", [128, 8, SEQ], f32r)
        aT_lo = sb("aT_lo", [128, 8, SEQ], f32r)
        with nc.sbuf_tensor("z_silu", [128, 8, 512], f32) as z_silu:
            pass
        hT_hi = sb("hT_hi", [128, 8, SEQ], f32r)
        hT_lo = sb("hT_lo", [128, 8, SEQ], f32r)
        x = sb("residual", [128, 2, D])
        xn = sb("xn", [128, 2, D])
        post_gain = sb("post_gain", [128, D])
        par = sb("par", [128, sum(PARAMS.values())])
        con = sb("con", [128, sum(CONSTS.values())])
        ws_hi = sb("ws_hi", [128, 8, 56], f32r)
        ws_lo = sb("ws_lo", [128, 8, 56], f32r)
        arena = sb("arena", [128, 15232])
        stat = sb("stat", [128, 800])

        def columns(buffer, table, name):
            at = 0
            for n, width in table.items():
                if n == name:
                    return buffer[:, at:at + width]
                at += width
            raise KeyError(name)

        def P(name):
            return columns(par, PARAMS, name)

        def C(name):
            return columns(con, CONSTS, name)

        def spread(ap, n, axis=2):
            ap = ap.unsqueeze(axis)
            shape = list(ap.shape)
            shape[axis] = n
            return ap.broadcast_to(tuple(shape))

        ident = C("ident")
        gains = P("gains").rearrange("p (n k) -> p n k", k=8)
        levels = C("levels").rearrange("p (l c) -> p l c", c=128)
        bank = [ctx.enter_context(nc.psum_tensor(f"bank{i}", [128, 512], f32)) for i in range(8)]

        used = [0]

        def room(*shape):
            n = 1
            for s in shape:
                n *= s
            at = used[0]
            used[0] += n
            assert used[0] <= 15232, used[0]
            flat = arena[:, at:at + n]
            if len(shape) == 1:
                return flat
            names = "abcd"[:len(shape)]
            sizes = {c: s for c, s in zip(names[1:], shape[1:])}
            return flat.rearrange(f"p ({' '.join(names)}) -> p {' '.join(names)}", **sizes)

        used[0] = 0
        f_gate = room(2, SEQ)
        f_tanh = room(2, SEQ)
        f_hid = room(2, SEQ)
        used[0] = 0
        proj = room(2, 2816)
        heads = room(14, SEQ)
        expo = room(2, 512)
        expoT = room(2, 512)
        rot = room(4, 224)
        blockT = expo.rearrange("p a (g c) -> p a g c", g=2)
        hidden = room(4, 32)
        hidden2 = room(4, 32)
        window_part = rot.rearrange("p a b -> p (a b)")[:, 0:512]
        kc_diag = room(2, 16)
        v_cmp = room(128)
        v_diag = room(8, 64)
        cmp_s = room(2, 8, 16)
        mixed = room(1024)
        c_expT = room(2, 128)
        c_sums = expoT
        c_mask = room(2, 16)
        used[0] = 0
        qkv = room(2, 4096)
        qkT = room(16, SEQ)
        g_work = room(5, 512)
        g_conv, g_tanh = [g_work[:, c, :] for c in range(3)], [g_work[:, 3 + c, :] for c in range(2)]
        low_T = [xn[:, t, 0:512] for t in range(2)]
        qk_T = [xn[:, t, 512:1024] for t in range(2)]
        level = [[qkv[:, t, 0:512], qkv[:, t, 512:1024]] for t in range(2)]
        prod = [g_work[:, t, :] for t in range(2)]
        inv_T = [g_work[:, 2 + t, :] for t in range(2)]
        inv = [g_work[:, 4, :], post_gain[:, 0:512]]
        k_decayed = post_gain[:, 512:1024]
        small_T = xn[0:32, 1, 768:1024]
        at = [0]

        def small(*shape):
            n = 1
            for s in shape:
                n *= s
            at[0] += n
            assert at[0] <= 800, at[0]
            flat = stat[:, at[0] - n:at[0]]
            return flat if len(shape) == 1 else flat.rearrange("p (a b) -> p a b", b=shape[1])

        half = small(16)
        sumsq = small(4)
        rstd = small(2)
        lam = small(8)
        gates = small(2, 24)
        neg_max = small(2, 32)
        total = small(2, 32)
        coef = small(2, 32)
        r16 = small(2, 20)
        trig = small(4, 16)
        cos_sin = small(4, 8)
        ang = small(2, 8)
        pos = small(2)
        one_s = small(1)
        neg_sinks = small(16)
        ba = small(2, 32)
        soft = small(2, 32)
        beta = small(2, 16)
        head_rstd = small(40)
        qk_rstd = head_rstd[:, 0:32]
        decay = small(2, 16)
        decay_sum = small(2, 16)
        decay_exp = small(2, 16)
        decay_rest = small(16)
        beta_decay = small(16)
        rate = small(16)
        masks = sb("masks", [128, 3, 512], bf16)
        ident_b = sb("ident_b", [128, 128], bf16)
        pos_i = sb("pos_i", [128, 2], mybir.dt.int32)

        slot_loaded = [sem(f"slot_loaded{s}") for s in range(3)]
        x_loaded = [sem(f"x_loaded{t}") for t in range(2)]
        par_loaded, con_loaded = sem("par_loaded"), sem("con_loaded")
        post_gain_loaded, stored = sem("post_gain_loaded"), sem("stored")
        w_hi_done, w_lo_done, item_done = sem("w_hi_done"), sem("w_lo_done"), sem("item_done")
        dve_step, act_step, pool_step = sem("dve_step"), sem("act_step"), sem("pool_step")
        x_ready = sem("x_ready")
        squares_ready, variance_ready, rstd_ready = sem("squares_ready"), sem("variance_ready"), sem("rstd_ready")
        rows_ready, turned, turned_hi, turned_lo = sem("rows_ready"), sem("turned"), sem("turned_hi"), sem("turned_lo")
        gate_scaled, gate_conv, gate_tanh = sem("gate_scaled"), sem("gate_conv"), sem("gate_tanh")
        hid_ready, hid_hi, hid_lo = sem("hid_ready"), sem("hid_hi"), sem("hid_lo")
        y_done = sem("y_done")
        y_squares, conv_step, silu_step = sem("y_squares"), sem("conv_step"), sem("silu_step")
        setup_hi, setup_done = sem("setup_hi"), sem("setup_done")
        copied = sem("copied")
        heads_ready, heads_turned, heads_copied = sem("heads_ready"), sem("heads_turned"), sem("heads_copied")
        head_squares, head_sums, head_normed = sem("head_squares"), sem("head_sums"), sem("head_normed")
        small_product, small_copied = sem("small_product"), sem("small_copied")
        gates_ready, gates_tanh = sem("gates_ready"), sem("gates_tanh")
        scores_ready, neg_max_ready, expo_ready = sem("scores_ready"), sem("neg_max_ready"), sem("expo_ready")
        expo_turned, expoT_ready, pv_done = sem("expo_turned"), sem("expoT_ready"), sem("pv_done")
        expo_normed = sem("expo_normed")
        out_read, sink_args, sink_expo = sem("out_read"), sem("sink_args"), sem("sink_expo")
        mix_sum, mix_squares = sem("mix_sum"), sem("mix_squares")
        c_twice, c_rows, c_rows_turned = sem("c_twice"), sem("c_rows"), sem("c_rows_turned")
        c_turned, c_copied, c_blocks = sem("c_turned"), sem("c_copied"), sem("c_blocks")
        c_gelu_arg, c_tanh, c_hidden = sem("c_gelu_arg"), sem("c_tanh"), sem("c_hidden")
        c_products, c_values, c_spread, c_operands = sem("c_products"), sem("c_values"), sem("c_spread"), sem("c_operands")
        c_scores, c_masked, c_expo, c_probs = sem("c_scores"), sem("c_masked"), sem("c_expo"), sem("c_probs")
        c_probs_turned, c_probsT, c_out, c_out_read = sem("c_probs_turned"), sem("c_probsT"), sem("c_out"), sem("c_out_read")
        g_scaled, g_tap, g_conv_ready, g_tanh_ready = sem("g_scaled"), sem("g_tap"), sem("g_conv_ready"), sem("g_tanh_ready")
        g_silu_ready, g_rows_turned, g_rows_copied = sem("g_silu_ready"), sem("g_rows_turned"), sem("g_rows_copied")
        g_soft_args, g_soft_done, g_decay = sem("g_soft_args"), sem("g_soft_done"), sem("g_decay")
        g_sums, g_sums_read, g_exps = sem("g_sums"), sem("g_sums_read"), sem("g_exps")
        g_variance = sem("g_variance")
        g_squares, g_normed, g_qk_turned, g_qk_copied = sem("g_squares"), sem("g_normed"), sem("g_qk_turned"), sem("g_qk_copied")
        d_rows, d_diff, d_exp, d_masked = sem("d_rows"), sem("d_diff"), sem("d_exp"), sem("d_masked")
        d_mats, d_mats_turned, d_mats_T = sem("d_mats"), sem("d_mats_turned"), sem("d_mats_T")
        d_level, d_first, d_first_turned, d_first_T = sem("d_level"), sem("d_first"), sem("d_first_turned"), sem("d_first_T")
        d_prod, d_prod_copied, d_step, d_applied = sem("d_prod"), sem("d_prod_copied"), sem("d_step"), sem("d_applied")
        d_inv_step, d_inv = sem("d_inv_step"), sem("d_inv")
        r_inputs, r_keys, r_new, r_new_copied = sem("r_inputs"), sem("r_keys"), sem("r_new"), sem("r_new_copied")
        r_state, r_state_copied, r_read, r_rhs = sem("r_state"), sem("r_state_copied"), sem("r_read"), sem("r_rhs")
        r_out, r_out_read = sem("r_out"), sem("r_out_read")
        z_tanh, z_used = sem("z_tanh"), sem("z_used")
        o_squares, o_variance, o_rstd, o_normed = sem("o_squares"), sem("o_variance"), sem("o_rstd"), sem("o_normed")
        lam_args, lam_expo, trig_args, trig_done = sem("lam_args"), sem("lam_expo"), sem("trig_args"), sem("trig_done")

        HEADS = {"mix_in": [], "att_in": []}
        for n in range(8):
            HEADS["mix_in"].append((n % 4, 4 + n % 4, n // 4, 1792 + 128 * (n % 4), 128, n // 4, 128 * (n % 4)))
        for branch in range(2):
            for n in range(8):
                g = n // 4
                HEADS["mix_in"].append((8 + n % 4, 12 + branch, g, 2560 + 128 * branch + 64 * g, 64, 2 + branch, 64 * n))
        for n in ATT_HEADS:
            HEADS["att_in"].append((4 * (n // 8) + n % 4, 8 + n // 8, n // 4 % 2, 1280 + 64 * (n // 4), 64, n // 4,
                                    n % 4))
        HEAD_BANKS = {"mix_in": ([0.125, 0.125, 1.0, 1.0, 0.125, 0.125, 1.0], 0), "att_in": ([0.125] * 4 + [1.0], 7)}
        GROUPS = {n: [(0, 4 * g, 4) for g in range(len(h) // 4)] + [(1, 2 * g, 2) for g in range(len(h) // 2)]
                  for n, h in HEADS.items()}
        GROUPS_BEFORE = {"mix_in": 0, "att_in": len(GROUPS["mix_in"])}
        TILES_BEFORE = {"mix_in": 0, "att_in": 2}

        def block_at(p):
            return MIX_ORDER[p] if MIX_ORDER[p] < 11 else None

        def projections(p):
            return sum(b < 11 for b in MIX_ORDER[:p])

        def c_block(buffer, kv):
            tiles = buffer[:, 2 * kv:2 * kv + 2, :].rearrange("p a (b c) -> p (a b) c", c=32)
            return tiles

        def nsa_scale(k):
            return P("subln") if k < 4 else C("ones")[:, 0:1]

        def squares_of(p):
            return mixed[:, 512 * (p % 2):512 * (p % 2) + 512].rearrange("p (t c) -> p t c", t=2)

        turns_before = {name: n for n, name in enumerate(t for t in TURNS if t != "att_out")}

        def heads_squared(t):
            return proj[:, t, 0:512]

        def turn(name):
            return 4 * TURNS.index(name)

        block = ctx.enter_context(nc.Block())

        def rounds(engine, n, body):
            for k in range(min(n, 3)):
                body(k, 0)
            if n >= 6:
                with engine.Fori(1, n // 3) as r:
                    for k in range(3):
                        body(k, r)
            for k in range(max(n // 3, 1) * 3, n):
                body(k, 0)

        def ffn_order(engine, name, tile, down):
            pairs, i0 = FFNS[name][0] // 2, FIRST[name]

            def pair(m, q):
                i = i0 + 2 + 3 * (m - 1)
                tile(2 * m, i, q)
                tile(2 * m + 1, i + 1, q)
                down(m - 1, i + 2, q)

            tile(0, i0, 0)
            tile(1, i0 + 1, 0)
            pair(1, 0)
            looped = (pairs - 2) // 2 - (name == "glu2")
            with engine.Fori(0, looped) as q:
                pair(2, q)
                pair(3, q)
            for m in range(2 + 2 * looped, pairs):
                pair(m, 0)
            down(pairs - 1, i0 + 3 * pairs - 1, 0)

        @block.sync
        def _(sp):
            sp.dma_start(x[:, 0, :], ins["x"][0:128, :]).then_inc(x_loaded[0], 16)
            sp.dma_start(x[:, 1, :], ins["x"][128:256, :]).then_inc(x_loaded[1], 16)
            sp.dma_start(con[:, 0:128], ins["consts"][:, 0:128]).then_inc(con_loaded, 16)
            sp.dma_start(par[:, :], ins["params"]).then_inc(par_loaded, 16)
            sp.dma_start(pos_i[:, :], ins["positions"]).then_inc(par_loaded, 16)
            for s in range(3):
                sp.dma_start(raw[:, s, :], ins["weights"][s]).then_inc(slot_loaded[s], 16)
            sp.wait_ge(con_loaded, 16)
            sp.dma_start(con[:, 128:], ins["consts"][:, 128:]).then_inc(con_loaded, 16)
            with sp.Fori(1, N_ITEMS // 3) as r:
                for s in range(3):
                    sp.wait_ge(w_lo_done, 3 * r + s - 2)
                    item = ins["weights"][bass.ds(3 * r + s, 1), :, :]
                    sp.dma_start(raw[:, s, :], item.rearrange("a p n -> p (a n)")).then_inc(slot_loaded[s], 16)
            for i in range(N_ITEMS // 3 * 3, N_ITEMS):
                sp.wait_ge(w_lo_done, i - 2)
                sp.dma_start(raw[:, i % 3, :], ins["weights"][i]).then_inc(slot_loaded[i % 3], 16)
            for t in range(2):
                sp.wait_ge(x_ready, 2 * len(NORMS) + t - 1)
                sp.dma_start(out[128 * t:128 * t + 128, :], x[:, t, :]).then_inc(stored, 16)
            sp.wait_ge(stored, 32)

        @block.tensor
        def _(pe):
            def exact(to, w, left, start, stop, moving_w=False):
                w_parts, l_parts = w, left
                pairs = [(w_parts[0], l_parts[0]), (w_parts[0], l_parts[1]), (w_parts[1], l_parts[0])]
                for n, (a, b) in enumerate(pairs):
                    lhsT, rhs = (b, a) if moving_w else (a, b)
                    last = nc.tensor.matmul(to, lhsT, rhs, start=start and n == 0, stop=stop and n == 2)
                return last

            def weights(i, a, b):
                return w_hi[:, i % 3, a:b], w_lo[:, i % 3, a:b]

            def left(k, a=0, b=SEQ):
                if k >= 8:
                    return hT_hi[:, k - 8, a:b], hT_lo[:, k - 8, a:b]
                return aT_hi[:, k, a:b], aT_lo[:, k, a:b]

            def turn_rows(name, source, ready=None):
                for t in range(2):
                    pe.wait_ge(rows_ready, 2 * turns_before[name] + t + 1)
                    for k in range(8):
                        to = bank[4 + k // 2][:, 256 * (k % 2) + 128 * t:256 * (k % 2) + 128 * t + 128]
                        last = nc.tensor.transpose(to, source[:, t, 128 * k:128 * k + 128], ident)
                        if t == 1 and k % 2:
                            last.then_inc(turned, 1)

            def aT_ready(name):
                pe.wait_ge(turned_lo, turn(name) + 4)

            def ffn(name):
                n_tiles, conv, f0 = FFNS[name]
                turn_rows(name, xn)

                def tile(f, i, q):
                    pe.wait_ge(w_lo_done, i + 1 + 6 * q)
                    if f0 + f >= 4:
                        pe.wait_ge(hid_ready, f0 + f - 3 + 4 * q)
                    to = bank[4 + f % 4]
                    for part in range(2):
                        for k in range(8):
                            at = 1024 * part + 128 * k
                            if f == 0 and part == 0 and k % 2 == 0:
                                pe.wait_ge(turned_lo, turn(name) + k // 2 + 1)
                            last = exact(to[:, 256 * part:256 * part + 256], weights(i, at, at + 128), left(k),
                                         k == 0, k == 7)
                    last.then_inc(item_done, 1)

                def down(m, i, q):
                    pe.wait_ge(w_lo_done, i + 1 + 6 * q)
                    pe.wait_ge(hid_lo, f0 + 2 * m + 2 + 4 * q)
                    for y in range(4):
                        t, h = y // 2, y % 2
                        for j in range(2):
                            f = 2 * m + j
                            last = exact(bank[y][:, :], weights(i, 1024 * j + 512 * h, 1024 * j + 512 * h + 512),
                                         left(8 + f % 4, 128 * t, 128 * t + 128), f == 0, f == n_tiles - 1, True)
                        if f == n_tiles - 1 and y == 1:
                            last.then_inc(y_done, 1)
                    last.then_inc(item_done, 1)

                ffn_order(pe, name, tile, down)

            def first_use(i, kk, first):
                for name in ("mix_in", "att_in", "gdn_qkv"):
                    if i == FIRST[name] and first and kk % 2 == 0:
                        pe.wait_ge(turned_lo, turn(name) + kk // 2 + 1)

            def project_small(a, b):
                for kk in range(8):
                    last = exact(bank[7][0:b - a, 0:SEQ], (ws_hi[:, kk, a:b], ws_lo[:, kk, a:b]), left(kk),
                                 kk == 0, kk == 7)
                last.then_inc(small_product, 1)

            def turn_small(n, use):
                pe.wait_ge(small_copied, use + 1)
                for t in range(2):
                    last = nc.tensor.transpose(bank[7][:, 32 * t:32 * t + n], small_T[0:n, 128 * t:128 * t + 128],
                                               ident[0:n, 0:n])
                last.then_inc(gates_ready, 1)

            def project_out(name, halves=1):
                for c in range(4):
                    for h in range(halves):
                        i = FIRST[name] + halves * c + h
                        pe.wait_ge(w_lo_done, i + 1)
                        for t in range(2):
                            for kk in range(8):
                                last = exact(bank[2 * t + c // 2][:, 256 * (c % 2):256 * (c % 2) + 256],
                                             weights(i, 256 * kk, 256 * kk + 256),
                                             left(8 * h + kk, 128 * t, 128 * t + 128),
                                             h == 0 and kk == 0, h == halves - 1 and kk == 7, True)
                            if t == 0 and c == 3 and h == halves - 1:
                                last.then_inc(y_done, 1)
                        last.then_inc(item_done, 1)

            def turn_heads(layer, b, to):
                before = HEAD_BANKS[layer][1]
                pe.wait_ge(heads_ready, before + b + 1)
                if b >= len(to):
                    pe.wait_ge(heads_copied, before + b + 1 - len(to))
                for j in range(2):
                    for t in range(2):
                        at = 128 * (2 * b + j)
                        last = nc.tensor.transpose(bank[to[b % len(to)]][:, 256 * j + 128 * t:256 * j + 128 * t + 128],
                                                   proj[:, t, at:at + 128], ident)
                last.then_inc(heads_turned, 1)

            def project_block(i, n, count_before):
                pe.wait_ge(w_lo_done, i + 1)
                if n >= 3:
                    pe.wait_ge(copied, count_before + n - 2)
                for t in range(2):
                    for kk in range(8):
                        first_use(i, kk, t == 0)
                        last = exact(bank[4 + n % 3][:, 256 * t:256 * t + 256],
                                     weights(i, 256 * kk, 256 * kk + 256), left(kk, 128 * t, 128 * t + 128),
                                     kk == 0, kk == 7, True)
                last.then_inc(item_done, 1)

            def attention(layer):
                groups, base = GROUPS[layer], GROUPS_BEFORE[layer]

                def scores(n):
                    t, h0, count = groups[n]
                    width = 512 // count
                    to = bank[4 + n % 2]
                    if n >= 2:
                        pe.wait_ge(expo_ready, base + n - 1)
                    mask = 0 if t == 0 else (2 if layer == "att_in" else 1)
                    nc.tensor.matmul(to[:, :], ident_b[:, :], masks[:, mask, :], start=True, stop=False)
                    for c in range(count):
                        q, k, half_of, _, _, _, _ = HEADS[layer][h0 + c]
                        rows = slice(64 * half_of, 64 * half_of + 64)
                        last = nc.tensor.matmul(to[:, width * c:width * c + width],
                                                heads[rows, q, 128 * t:128 * t + 128], heads[rows, k, 0:width],
                                                start=False, stop=c == count - 1)
                    last.then_inc(scores_ready, 1)

                def turn_expo(n):
                    if layer == "att_in":
                        pe.wait_ge(expo_normed, n + 1)
                    else:
                        pe.wait_ge(expo_ready, base + n + 1)
                    if n >= 2:
                        pe.wait_ge(expoT_ready, base + n - 1)
                    for b in range(4):
                        last = nc.tensor.transpose(bank[6 + n % 2][:, 128 * b:128 * b + 128],
                                                   expo[:, n % 2, 128 * b:128 * b + 128], ident)
                    last.then_inc(expo_turned, 1)

                def values(n):
                    t, h0, count = groups[n]
                    pe.wait_ge(expoT_ready, base + n + 1)
                    if n == 0 and layer == "mix_in":
                        pe.wait_ge(c_out_read, 2)
                    if t == 1 and h0 == 0 and layer == "mix_in":
                        pe.wait_ge(out_read, TILES_BEFORE[layer] + 1)
                    if layer == "att_in":
                        for c in range(0, count, 2):
                            _, _, _, v, width, b, head = HEADS[layer][h0 + c]
                            rows = slice(64 * (head % 2), 64 * (head % 2) + 64)
                            to = bank[b][rows, :].rearrange("p (k c) -> p k c", k=2)[:, :, 128 * t:128 * t + 128]
                            both = expoT[:, n % 2, 512 // count * c:512 // count * (c + 2)]
                            both = both.rearrange("p (k a c) -> p k a c", k=2, c=128)
                            for kt in range(t + 1):
                                last = nc.tensor.matmul(to, proj[:, kt, v:v + width], both[:, :, kt, :],
                                                        start=kt == 0, stop=kt == t)
                        last.then_inc(pv_done, 1)
                        return
                    for c in range(count):
                        _, _, _, v, width, b, at = HEADS[layer][h0 + c]
                        for kt in range(t + 1):
                            s = 128 * ((t + 1) * c + kt)
                            last = nc.tensor.matmul(bank[b][:, at:at + width], expoT[:, n % 2, s:s + 128],
                                                    proj[:, kt, v:v + width], start=kt == 0, stop=kt == t)
                    last.then_inc(pv_done, 1)

                scores(0)
                scores(1)
                for n in range(len(groups)):
                    turn_expo(n)
                    if n + 2 < len(groups):
                        scores(n + 2)
                    if n >= 1:
                        values(n - 1)
                values(len(groups) - 1)

            def mixer_projection():
                for p, b in enumerate(MIX_ORDER):
                    i = FIRST["mix_in"] + p
                    if b < 11:
                        project_block(i, projections(p), 0)
                    else:
                        kv, part = (b - 11) // 2, (b - 11) % 2
                        pe.wait_ge(w_lo_done, i + 1)
                        pe.wait_ge(c_blocks, kv + 1)
                        for k in range(8):
                            last = exact(bank[kv][0:30, 0:256], weights(i, 256 * k, 256 * k + 256),
                                         (c_block(hT_hi, kv)[:, 8 * part + k, 0:30],
                                          c_block(hT_lo, kv)[:, 8 * part + k, 0:30]),
                                         part == 0 and k == 0, part == 1 and k == 7, True)
                        last.then_inc(item_done, 1)
                    if p == 1:
                        project_small(0, 24)
                        pe.wait_ge(c_twice, 1)
                        for kv in range(2):
                            for g in range(2):
                                for t in range(2):
                                    at = 512 * t + 256 * kv + 128 * g
                                    last = nc.tensor.transpose(
                                        bank[kv][:, 256 * g + 128 * t:256 * g + 128 * t + 128],
                                        mixed[:, at:at + 128], ident)
                            last.then_inc(c_turned, 1)
                    if p == 2:
                        turn_small(24, 0)
                    if p == 3:
                        pe.wait_ge(gates_tanh, 1)
                    if p in TURN_AT:
                        turn_heads("mix_in", TURN_AT.index(p), [7])
                    if p == 9:
                        pe.wait_ge(c_rows, 2)
                        for kv in range(2):
                            for h in range(2):
                                at = 512 + 256 * kv + 128 * h
                                last = nc.tensor.transpose(bank[2][:, 64 * kv + 32 * h:64 * kv + 32 * h + 30],
                                                           mixed[0:30, at:at + 128], ident[0:30, 0:30])
                        last.then_inc(c_rows_turned, 1)
                    if p == 10:
                        compressed_products()
                    if p == 11:
                        pe.wait_ge(c_values, 1)
                        nc.tensor.matmul(bank[2][:, 0:128], C("spread")[0:15, :], v_cmp[0:15, :],
                                         start=True, stop=True).then_inc(c_spread, 1)
                    if p == 12:
                        pe.wait_ge(c_operands, 1)
                        pe.wait_ge(heads_copied, 6)
                        for t in range(2):
                            for j in range(4):
                                last = nc.tensor.matmul(bank[t][:, 32 * j:32 * j + 32],
                                                        heads[:, 8 + j, 128 * t:128 * t + 128],
                                                        kc_diag.rearrange("p g c -> p (g c)"), start=True, stop=True)
                            last.then_inc(c_scores, 1)
                    if p == 14:
                        for t in range(2):
                            pe.wait_ge(c_probs, t + 1)
                            last = nc.tensor.transpose(bank[2][:, 128 * t:128 * t + 128],
                                                       cmp_s[:, t].rearrange("p h c -> p (h c)"), ident)
                        last.then_inc(c_probs_turned, 1)
                pe.wait_ge(c_probsT, 1)
                for t in range(2):
                    nc.tensor.matmul(bank[(3, 0)[t]][:, :], c_expT[:, t, :], v_diag.rearrange("p h c -> p (h c)"),
                                     start=True, stop=True).then_inc(c_out, 1)
                pe.wait_ge(heads_copied, 7)
                pe.wait_ge(copied, 11)

            def compressed_products():
                pe.wait_ge(c_hidden, 1)
                w2k = P("w2k").rearrange("p (h c) -> p h c", h=2)
                w2v = P("w2v").rearrange("p (h c) -> p h c", h=2)
                for h in range(2):
                    nc.tensor.matmul(bank[0][:, 0:30], w2k[:, h, :], hidden2[:, h, 0:30], start=h == 0, stop=h == 1)
                for g in range(2):
                    for h in range(2):
                        last = nc.tensor.matmul(bank[1][0:15, 64 * g:64 * g + 64],
                                                hidden2[:, 2 + h, 15 * g:15 * g + 15], w2v[:, h, :],
                                                start=h == 0, stop=h == 1)
                last.then_inc(c_products, 1)

            def attention_projection():
                for p in range(6):
                    project_block(FIRST["att_in"] + p, p, 11)
                    if p >= 2:
                        turn_heads("att_in", p - 2, [3, 7])
                turn_heads("att_in", 4, [3, 7])
                pe.wait_ge(heads_copied, 12)
                pe.wait_ge(copied, 17)

            def convolved():
                def rows(j):
                    pe.wait_ge(g_silu_ready, j + 1)
                    if j >= 3:
                        pe.wait_ge(g_rows_copied, j - 2)
                    for t in range(2):
                        for n in range(2):
                            last = nc.tensor.transpose(bank[j % 3][:, 256 * t + 128 * n:256 * t + 128 * n + 128],
                                                       g_conv[j % 3][:, 256 * n + 128 * t:256 * n + 128 * t + 128],
                                                       ident)
                    last.then_inc(g_rows_turned, 1)

                def back(j):
                    pe.wait_ge(g_normed, j + 1)
                    if j >= 2:
                        pe.wait_ge(g_qk_copied, j - 1)
                    for n in range(2):
                        for t in range(2):
                            at = 128 * (2 * j + n)
                            last = nc.tensor.transpose(
                                bank[3 + 4 * (j % 2)][:, 256 * n + 128 * t:256 * n + 128 * t + 128],
                                qkv[:, t, at:at + 128], ident)
                    last.then_inc(g_qk_turned, 1)

                for k in range(16):
                    pe.wait_ge(w_lo_done, FIRST["gdn_qkv"] + k + 1)
                    if k >= 3:
                        pe.wait_ge(g_conv_ready, k - 2)
                    for n in range(2):
                        for kk in range(8):
                            at = 256 * kk + 128 * n
                            first_use(FIRST["gdn_qkv"] + k, kk, n == 0)
                            last = exact(bank[4 + k % 3][:, 256 * n:256 * n + 256],
                                         weights(FIRST["gdn_qkv"] + k, at, at + 128), left(kk), kk == 0, kk == 7)
                    last.then_inc(item_done, 1)
                    if k == 0:
                        project_small(24, 56)
                    if k == 1:
                        turn_small(32, 1)
                    if k == 3:
                        pe.wait_ge(g_decay, 1)
                        for t in range(2):
                            nc.tensor.matmul(bank[7][:, 16 * t:16 * t + 16], C("upto"), decay[:, t, :],
                                             start=True, stop=True)
                        nc.tensor.matmul(bank[7][:, 32:48], C("ones"), decay[:, 0, :], start=True, stop=True)\
                            .then_inc(g_sums, 1)
                    if k >= 2:
                        rows(k - 2)
                    if k == 6:
                        pe.wait_ge(g_sums_read, 1)
                    if 6 <= k < 14:
                        back(k - 6)
                rows(14)
                rows(15)

            def z_part(b, first, last_one):
                for c in range(first, last_one):
                    i, t, kk = 2 * b + c // 16, c % 16 // 8, c % 8
                    if c % 16 == 0:
                        pe.wait_ge(w_lo_done, FIRST["gdn_z"] + i + 1)
                        if i >= 2:
                            pe.wait_ge(z_used, i - 1)
                    last = exact(bank[3 + 4 * (i % 2)][:, 256 * t:256 * t + 256],
                                 weights(FIRST["gdn_z"] + i, 256 * kk, 256 * kk + 256),
                                 left(kk, 128 * t, 128 * t + 128), kk == 0, kk == 7, True)
                    if c % 16 == 15:
                        last.then_inc(item_done, 1)

            def delta(b):
                tok = [slice(0, 128), slice(128, 256)]
                col = [slice(128 * c, 128 * c + 128) for c in range(4)]
                if b:
                    pe.wait_ge(r_out_read, 2 * b)
                else:
                    pe.wait_ge(g_qk_copied, 8)
                    pe.wait_ge(g_rows_copied, 16)
                for t in range(2):
                    rows, prods = bank[4 * t], bank[4 * t + 1]
                    for c in range(4):
                        g_row = decay[:, t, 4 * b + c:4 * b + c + 1].broadcast_to((128, 128))
                        nc.tensor.matmul(rows[:, col[c]], g_row, C("upto"), start=True, stop=True)
                    for c in range(2):
                        key, query = qkT[:, 8 + 2 * b + c, tok[t]], qkT[:, 2 * b + c, tok[t]]
                        nc.tensor.matmul(prods[:, col[c]], key, key, start=True, stop=True)
                        last = nc.tensor.matmul(prods[:, col[2 + c]], query, key, start=True, stop=True)
                    last.then_inc(d_rows, 1)
                z_part(b, 0, 12)
                for t in range(2):
                    pe.wait_ge(d_mats, 2 * b + t + 1)
                    for c in range(4):
                        nc.tensor.transpose(bank[4 * t + 2][:, col[c]], prod[t][:, col[c]], ident)
                    for c in range(4):
                        last = nc.tensor.transpose(bank[4 * t][:, col[c]], inv[t][:, col[c]], ident)
                    last.then_inc(d_mats_turned, 1)
                z_part(b, 12, 20)
                for t in range(2):
                    pe.wait_ge(d_first, 2 * b + t + 1)
                    for c in range(4):
                        last = nc.tensor.transpose(bank[4 * t][:, col[c]], inv_T[t][:, col[c]], ident)
                    last.then_inc(d_first_turned, 1)
                z_part(b, 20, 22)
                for n in range(1, len(LEVELS)):
                    for t in range(2):
                        at = 12 * b + 2 * (n - 1) + t
                        pe.wait_ge(d_level, 14 * b + 2 * n + t + 1)
                        if n == 1:
                            pe.wait_ge(d_first_T, 2 * b + t + 1)
                        else:
                            pe.wait_ge(d_inv, 10 * b + 2 * (n - 2) + t + 1)
                        for c in range(4):
                            last = nc.tensor.matmul(bank[4 * t][:, col[c]], level[t][n % 2][:, col[c]],
                                                    inv[t][:, col[c]], start=True, stop=True)
                        last.then_inc(d_prod, 1)
                    for t in range(2):
                        pe.wait_ge(d_prod_copied, 12 * b + 2 * (n - 1) + t + 1)
                        if n > 1:
                            pe.wait_ge(d_applied, 12 * b + 2 * (n - 2) + t + 1)
                        if n < len(LEVELS) - 1:
                            for c in range(4):
                                last = nc.tensor.matmul(bank[4 * t + 2][:, col[c]], inv_T[t][:, col[c]],
                                                        prod[t][:, col[c]], start=True, stop=True)
                            last.then_inc(d_inv_step, 1)
                        for c in range(4):
                            last = nc.tensor.matmul(bank[4 * t + 1][:, col[c]], prod[t][:, col[c]],
                                                    inv_T[t][:, col[c]], start=True, stop=True)
                        last.then_inc(d_step, 1)
                pe.wait_ge(d_applied, 12 * b + 12)
                pe.wait_ge(r_inputs, b + 1)
                v = [qkv[:, t, 2048 + 512 * b:2560 + 512 * b] for t in range(2)]
                new = [level[0][0], level[0][1]]
                state = level[1][0]
                for c in range(4):
                    last = nc.tensor.matmul(bank[2][:, col[c]], inv_T[0][:, col[c]], v[0][:, col[c]],
                                            start=True, stop=True)
                last.then_inc(r_new, 1)
                z_part(b, 22, 24)
                pe.wait_ge(r_new_copied, 2 * b + 1)
                pe.wait_ge(r_keys, b + 1)
                for c in range(4):
                    last = nc.tensor.matmul(bank[0][:, col[c]], k_decayed[:, col[c]], new[0][:, col[c]],
                                            start=True, stop=True)
                last.then_inc(r_state, 1)
                for c in range(4):
                    last = nc.tensor.matmul(bank[1][:, col[c]], qk_T[0][:, col[c]], new[0][:, col[c]],
                                            start=True, stop=True)
                last.then_inc(r_out, 1)
                pe.wait_ge(r_state_copied, b + 1)
                for to, first in ((4, 8), (5, 0)):
                    for c in range(2):
                        two = slice(256 * c, 256 * c + 256)
                        last = nc.tensor.matmul(bank[to][:, two], qkT[:, first + 2 * b + c, tok[1]], state[:, two],
                                                start=True, stop=True)
                last.then_inc(r_read, 1)
                z_part(b, 24, 29)
                pe.wait_ge(r_rhs, b + 1)
                for c in range(4):
                    last = nc.tensor.matmul(bank[6][:, col[c]], inv_T[1][:, col[c]], v[1][:, col[c]],
                                            start=True, stop=True)
                last.then_inc(r_new, 1)
                z_part(b, 29, 31)
                pe.wait_ge(r_new_copied, 2 * b + 2)
                for c in range(4):
                    last = nc.tensor.matmul(bank[0][:, col[c]], qk_T[1][:, col[c]], new[1][:, col[c]],
                                            start=True, stop=True)
                last.then_inc(r_out, 1)
                z_part(b, 31, 32)

            pe.wait_ge(con_loaded, 16)
            ffn("ff1")
            turn_rows("mix_in", xn)
            pe.wait_ge(setup_done, 3)
            mixer_projection()
            attention("mix_in")
            turn_rows("mix_out", xn)
            aT_ready("mix_out")
            project_out("mix_out")
            ffn("ff2")
            turn_rows("att_in", xn)
            attention_projection()
            attention("att_in")
            aT_ready("att_out")
            project_out("att_out")
            ffn("glu1")
            turn_rows("gdn_qkv", xn)
            convolved()
            for b in range(4):
                delta(b)
            turn_rows("gdn_out0", qkv[:, :, 2048:3072])
            pe.wait_ge(turned_lo, turn("gdn_out0") + 4)
            turn_rows("gdn_out1", qkv[:, :, 3072:4096])
            aT_ready("gdn_out1")
            project_out("gdn_out", 2)
            ffn("glu2")

        @block.scalar
        def _(act):
            done = [0]

            def link(instruction):
                done[0] += 1
                instruction.then_inc(act_step, 1)
                act.wait_ge(act_step, done[0])

            def split(i, r=0):
                if i >= N_ITEMS:
                    return
                act.wait_ge(slot_loaded[i % 3], 16 * (i // 3 + 1) + 16 * r)
                if i >= 3:
                    act.wait_ge(item_done, i - 2 + 3 * r)
                nc.scalar.activation(w_hi[:, i % 3, :], raw[:, i % 3, :], ACT.Copy).then_inc(w_hi_done, 1)

            def turn_out(name, scale):
                n = TURNS.index(name)
                hi = hT_hi if name == "gdn_out1" else aT_hi
                for j in range(4):
                    source = bank[4 + j]
                    if name == "att_out":
                        source = bank[j]
                        act.wait_ge(pv_done, GROUPS_BEFORE["att_in"] + 4 + 2 * (j + 1))
                    else:
                        act.wait_ge(turned, 4 * turns_before[name] + j + 1)
                    for k in range(2):
                        last = nc.scalar.activation(hi[:, 2 * j + k, :], source[:, 256 * k:256 * k + 256],
                                                    ACT.Copy, scale=scale(2 * j + k))
                    last.then_inc(turned_hi, 1)

            def norm_squares(name):
                n = NORMS.index(name)
                for t in range(2):
                    if n == 0:
                        act.wait_ge(x_loaded[t], 16)
                    else:
                        act.wait_ge(x_ready, 2 * n + t - 1)
                    nc.scalar.activation(xn[:, t, :], x[:, t, :], ACT.Square, accum_out=sumsq[:, t:t + 1])\
                        .then_inc(squares_ready, 1)

            def pre_norm(name):
                norm_squares(name)
                n = NORMS.index(name)
                if n == 0:
                    split(0)
                turn_out(name, lambda k: gains[:, n, k:k + 1])
                if n == 0:
                    split(1)
                split(FIRST[name] + 2)
                if n == 0:
                    set_up()

            def ffn(name):
                n_tiles, conv, f0 = FFNS[name]
                pre_norm(name)

                def tile(f, i, q):
                    gate = bank[4 + f % 4][:, 0:256]
                    act.wait_ge(item_done, i + 1 + 6 * q)
                    tanh_of = gate
                    if conv:
                        tap = P("ffn_conv")[:, 72 * (name == "glu2"):72 * (name == "glu2") + 72]
                        bias = P("ffn_bias")[:, 24 * (name == "glu2"):24 * (name == "glu2") + 24]
                        tap, bias = tap.rearrange("p (f t) -> p f t", t=3), bias
                        nc.scalar.activation(f_gate[:, f % 2, :], gate, ACT.Identity,
                                             scale=at_tile(tap, f, q, 2), bias=at_tile(bias, f, q))\
                            .then_inc(gate_scaled, 1)
                        act.wait_ge(gate_conv, f0 - 44 + f + 1 + 4 * q)
                        tanh_of = f_gate[:, f % 2, :]
                    nc.scalar.activation(f_tanh[:, f % 2, :], tanh_of, ACT.Tanh, scale=0.5).then_inc(gate_tanh, 1)
                    split(i + 3, 2 * q)
                    act.wait_ge(hid_ready, f0 + f + 1 + 4 * q)
                    nc.scalar.activation(hT_hi[:, f % 4, :], f_hid[:, f % 2, :], ACT.Copy).then_inc(hid_hi, 1)

                def down(m, i, q):
                    if m < n_tiles // 2 - 1:
                        split(i + 3, 2 * q)

                ffn_order(act, name, tile, down)

            def at_tile(table, f, q, tap=None):
                if tap is None:
                    return table[:, bass.ds(f + 4 * q, 1)]
                return table[:, bass.ds(f + 4 * q, 1), tap:tap + 1].rearrange("p a b -> p (a b)")

            def results_done(name, t):
                if t == 0:
                    act.wait_ge(y_done, RESULTS.index(name) + 1)
                else:
                    act.wait_ge(item_done, FIRST[name] + dict(COUNTS)[name])

            def post_squares(name):
                for y in range(4):
                    results_done(name, y // 2)
                    nc.scalar.activation(xn[:, y // 2, 512 * (y % 2):512 * (y % 2) + 512], bank[y][:, :], ACT.Square,
                                         accum_out=sumsq[:, y:y + 1]).then_inc(y_squares, 1)

            def copy_block(i, n, block):
                act.wait_ge(item_done, i + 1)
                nc.scalar.activation(proj[:, :, 256 * block:256 * block + 256],
                                     bank[4 + n % 3][:, :].rearrange("p (t c) -> p t c", t=2), ACT.Copy)\
                    .then_inc(copied, 1)

            def copy_heads(layer, b, banks):
                scales, before = HEAD_BANKS[layer]
                act.wait_ge(heads_turned, before + b + 1)
                nc.scalar.activation(heads[:, 2 * b:2 * b + 2, :],
                                     bank[banks[b % len(banks)]][:, :].rearrange("p (j c) -> p j c", j=2),
                                     ACT.Copy, scale=scales[b]).then_inc(heads_copied, 1)

            def mixer_projection():
                for p, b in enumerate(MIX_ORDER):
                    i = FIRST["mix_in"] + p
                    if b < 11:
                        copy_block(i, projections(p), b)
                    split(i + 3)
                    if p == 1:
                        for kv in range(2):
                            act.wait_ge(c_turned, kv + 1)
                            rows = bank[kv][:, :].rearrange("p (g c) -> p g c", g=2)
                            nc.scalar.activation(blockT[0:64, kv, :, :], rows[0:64, :, :], ACT.Copy)
                            nc.scalar.activation(blockT[64:128, kv, :, 0:255], rows[64:128, :, 1:256], ACT.Copy)\
                                .then_inc(c_copied, 1)
                    if p == 2:
                        act.wait_ge(gates_ready, 1)
                        nc.scalar.activation(gates, bank[7][:, 0:64].rearrange("p (t c) -> p t c", t=2)[:, :, 0:24],
                                             ACT.Tanh, scale=0.5).then_inc(gates_tanh, 1)
                    if p in TURN_AT:
                        copy_heads("mix_in", TURN_AT.index(p), [7])
                    if p == 9:
                        act.wait_ge(c_gelu_arg, 1)
                        nc.scalar.activation(hidden2[:, :, 0:30], hidden2[:, :, 0:30], ACT.Tanh,
                                             scale=0.7978845608028654).then_inc(c_tanh, 1)
                    if p == 12:
                        for t in range(2):
                            act.wait_ge(c_masked, t + 1)
                            nc.scalar.activation(cmp_s[:, t], cmp_s[:, t], ACT.Exp).then_inc(c_expo, 1)

            def attention_projection():
                for p in range(6):
                    i = FIRST["att_in"] + p
                    copy_block(i, p, p)
                    if p < 5:
                        act.wait_ge(copied, 11 + p + 1)
                        if p >= 2:
                            act.wait_ge(head_sums, p - 1)
                        nc.scalar.activation(squares_of(p), proj[:, :, 256 * p:256 * p + 256], ACT.Square)\
                            .then_inc(head_squares, 1)
                    split(i + 3)
                    if p >= 2:
                        copy_heads("att_in", p - 2, [3, 7])
                copy_heads("att_in", 4, [3, 7])

            def splits(first, n):
                for i in range(first, first + n):
                    split(i + 3)

            def mix_squared(t):
                act.wait_ge(mix_sum, t + 1)
                nc.scalar.activation(heads_squared(t), xn[:, t, 0:512], ACT.Square).then_inc(mix_squares, 1)

            def attention(layer):
                for n, (t, h0, count) in enumerate(GROUPS[layer]):
                    base, width = GROUPS_BEFORE[layer], 512 // count
                    act.wait_ge(neg_max_ready, base + n + 1)
                    if n >= 2:
                        act.wait_ge(expo_turned, base + n - 1)
                    for c in range(count):
                        cols = slice(width * c, width * c + width)
                        last = nc.scalar.activation(expo[:, n % 2, cols], bank[4 + n % 2][:, cols], ACT.Exp,
                                                    bias=neg_max[:, t, h0 + c:h0 + c + 1],
                                                    accum_out=total[:, t, h0 + c:h0 + c + 1])
                    last.then_inc(expo_ready, 1)
                    if layer == "mix_in" and n == len(GROUPS[layer]) - 5:
                        mix_squared(0)
                    if layer == "att_in":
                        act.wait_ge(sink_args, n + 1)
                        sinks = coef[:, t, 16 + h0:16 + h0 + count]
                        nc.scalar.activation(sinks, sinks, ACT.Exp).then_inc(sink_expo, 1)

            def convolved():
                taps = P("gdn_conv").rearrange("p (f t) -> p f t", t=4)
                for k in range(16):
                    act.wait_ge(item_done, FIRST["gdn_qkv"] + k + 1)
                    if k >= 3:
                        act.wait_ge(g_rows_turned, k - 2)
                    for n in range(2):
                        last = nc.scalar.activation(g_conv[k % 3][:, 256 * n:256 * n + 256],
                                                    bank[4 + k % 3][:, 256 * n:256 * n + 256], ACT.Copy,
                                                    scale=taps[:, 2 * k + n, 3:4])
                    last.then_inc(g_scaled, 1)
                    split(FIRST["gdn_qkv"] + k + 3)
                    act.wait_ge(g_conv_ready, k + 1)
                    if k >= 2:
                        act.wait_ge(g_silu_ready, k - 1)
                    nc.scalar.activation(g_tanh[k % 2], g_conv[k % 3], ACT.Tanh, scale=0.5).then_inc(g_tanh_ready, 1)
                    if k >= 2:
                        rows_out(k - 2)
                    if 2 <= k < 10:
                        squares(k - 2)
                    if k == 2:
                        gates_exp()
                    if k == 5:
                        act.wait_ge(g_sums_read, 1)
                        nc.scalar.activation(decay_exp, decay_sum, ACT.Exp)
                        nc.scalar.activation(decay_rest, decay_rest, ACT.Exp).then_inc(g_exps, 1)
                    if 7 <= k < 15:
                        heads_back(k - 7)
                rows_out(14)
                rows_out(15)

            def rows_out(j):
                act.wait_ge(g_rows_turned, j + 1)
                nc.scalar.activation(qkv[:, :, 256 * j:256 * j + 256],
                                     bank[j % 3][:, :].rearrange("p (t c) -> p t c", t=2), ACT.Copy, scale=0.5)\
                    .then_inc(g_rows_copied, 1)

            def squares(j):
                act.wait_ge(g_rows_copied, j + 1)
                if j >= 2:
                    act.wait_ge(g_variance, j - 1)
                nc.scalar.activation(xn[:, 0, 512 * (j % 2):512 * (j % 2) + 512].rearrange("p (t c) -> p t c", t=2),
                                     qkv[:, :, 256 * j:256 * j + 256], ACT.Square).then_inc(g_squares, 1)

            def heads_back(j):
                act.wait_ge(g_qk_turned, j + 1)
                nc.scalar.activation(qkT[:, 2 * j:2 * j + 2, :],
                                     bank[3 + 4 * (j % 2)][:, :].rearrange("p (j c) -> p j c", j=2), ACT.Copy)\
                    .then_inc(g_qk_copied, 1)

            def gates_exp():
                act.wait_ge(g_soft_args, 1)
                link(nc.scalar.activation(soft[:, :, 0:16], soft[:, :, 0:16], ACT.Exp))
                nc.scalar.activation(soft[:, :, 16:32], ba[:, :, 0:16], ACT.Tanh, scale=0.5)
                nc.scalar.activation(rate, P("a_log"), ACT.Exp)
                nc.scalar.activation(soft[:, :, 0:16], soft[:, :, 0:16], ACT.Ln, bias=1.0).then_inc(g_soft_done, 1)

            def split_half(i, h):
                act.wait_ge(slot_loaded[i % 3], 16 * (i // 3 + 1))
                act.wait_ge(item_done, i - 2)
                at = slice(1024 * h, 1024 * h + 1024)
                last = nc.scalar.activation(w_hi[:, i % 3, at], raw[:, i % 3, at], ACT.Copy)
                if h:
                    last.then_inc(w_hi_done, 1)

            def z_gate(i):
                act.wait_ge(item_done, FIRST["gdn_z"] + i + 1)
                nc.scalar.activation(z_silu[:, i, :], bank[3 + 4 * (i % 2)][:, :], ACT.Tanh, scale=0.5).then_inc(z_tanh, 1)

            def out_squares(b, t):
                act.wait_ge(r_out_read, 2 * b + 2)
                nc.scalar.activation(qkT[:, 8 * t + 2 * b:8 * t + 2 * b + 2, :].rearrange("p a c -> p (a c)"),
                                     qkv[:, t, 2048 + 512 * b:2560 + 512 * b], ACT.Square).then_inc(o_squares, 1)

            def delta(b):
                for t in range(2):
                    act.wait_ge(d_diff, 2 * b + t + 1)
                    nc.scalar.activation(level[t][0], level[t][0], ACT.Exp, scale=-1.0).then_inc(d_exp, 1)
                if b:
                    z_gate(2 * b - 1)
                for t in range(2):
                    act.wait_ge(d_mats_turned, 2 * b + t + 1)
                    nc.scalar.activation(low_T[t], bank[4 * t + 2][:, :], ACT.Copy)
                    nc.scalar.activation(qk_T[t], bank[4 * t][:, :], ACT.Copy).then_inc(d_mats_T, 1)
                for t in range(2):
                    act.wait_ge(d_first_turned, 2 * b + t + 1)
                    nc.scalar.activation(inv[t], bank[4 * t][:, :], ACT.Copy).then_inc(d_first_T, 1)
                for n in range(1, len(LEVELS)):
                    for t in range(2):
                        act.wait_ge(d_prod, 12 * b + 2 * (n - 1) + t + 1)
                        nc.scalar.activation(prod[t], bank[4 * t][:, :], ACT.Copy).then_inc(d_prod_copied, 1)
                    if n in (1, 2) and b:
                        split_half(FIRST["gdn_z"] + 2 * b + 2, n - 1)
                    if n == 3 and b:
                        out_squares(b - 1, 0)
                        out_squares(b - 1, 1)
                    if n in (4, 5):
                        split_half(FIRST["gdn_z"] + 2 * b + 3, n - 4)
                    if n == 5:
                        z_gate(2 * b)
                for t in range(2):
                    act.wait_ge(r_new, 2 * b + t + 1)
                    nc.scalar.activation(level[0][t], bank[2 + 4 * t][:, :], ACT.Copy).then_inc(r_new_copied, 1)
                    if t == 0:
                        act.wait_ge(r_state, b + 1)
                        nc.scalar.activation(level[1][0], bank[0][:, :], ACT.Copy).then_inc(r_state_copied, 1)

            def set_up():
                act.wait_ge(par_loaded, 32)
                nc.scalar.activation(ws_hi[:, :, :], P("small").rearrange("p (k c) -> p k c", c=56), ACT.Copy)\
                    .then_inc(setup_hi, 1)
                act.wait_ge(lam_args, 1)
                nc.scalar.activation(lam[:, 2:4], lam[:, 0:2], ACT.Exp).then_inc(lam_expo, 1)
                act.wait_ge(trig_args, 1)
                nc.scalar.activation(trig[:, 1, :], trig[:, 0, :], ACT.Sin)
                nc.scalar.activation(trig[:, 2, :], trig[:, 0, :], ACT.Sin, scale=0.5).then_inc(trig_done, 1)

            act.wait_ge(par_loaded, 32)
            ffn("ff1")
            post_squares("ff1")
            pre_norm("mix_in")
            mixer_projection()
            attention("mix_in")
            mix_squared(1)
            turn_out("mix_out", nsa_scale)
            splits(FIRST["mix_out"], 3)
            post_squares("mix_out")
            ffn("ff2")
            post_squares("ff2")
            pre_norm("att_in")
            attention_projection()
            attention("att_in")
            turn_out("att_out", lambda k: 1.0)
            splits(FIRST["att_out"], 3)
            ffn("glu1")
            pre_norm("gdn_qkv")
            convolved()
            for b in range(4):
                delta(b)
            out_squares(3, 0)
            out_squares(3, 1)
            z_gate(7)
            split(FIRST["gdn_z"] + 10)
            turn_out("gdn_out0", lambda k: P("gdn_norm"))
            turn_out("gdn_out1", lambda k: P("gdn_norm"))
            splits(FIRST["gdn_out"], 7)
            ffn("glu2")

        @block.gpsimd
        def _(pool):
            steps = [0]

            def link(instruction):
                steps[0] += 1
                instruction.then_inc(pool_step, 1)
                pool.wait_ge(pool_step, steps[0])

            def power(n, value, result):
                pool.wait_ge(variance_ready, n + 1)
                nc.gpsimd.tensor_tensor(result, value, half[:, 0:1].broadcast_to(result.shape), ALU.pow)\
                    .then_inc(rstd_ready, 1)

            def load_post_gain(n):
                if n:
                    pool.wait_ge(x_ready, 2 * n)
                pool.dma_start(post_gain[:, :], ins["post_gains"][n:n + 1, :].broadcast_to((128, D)))\
                    .then_inc(post_gain_loaded, 16)

            link(nc.gpsimd.memset(half, -0.5))
            load_post_gain(0)
            powers = [0]

            def power_of(value, result):
                power(powers[0], value, result)
                powers[0] += 1

            def pre_norm():
                for t in range(2):
                    power_of(rstd[:, t:t + 1], rstd[:, t:t + 1])

            def post_norm():
                pre_norm()
            def norm_heads():
                for p in range(5):
                    pool.wait_ge(head_sums, p + 1)
                    r = head_rstd[:, 8 * p:8 * p + 8]
                    link(nc.gpsimd.tensor_tensor(r, r, half[:, 0:1].broadcast_to(r.shape), ALU.pow))
                    v = proj[:, :, 256 * p:256 * p + 256].rearrange("p t (h d) -> p t h d", d=64)
                    link(nc.gpsimd.tensor_tensor(v, v, spread(r.rearrange("p (t h) -> p t h", t=2), 64, 3), ALU.mult))
                    gain = P("qk_gain")[:, 64 * (p == 4):64 * (p == 4) + 64]
                    nc.gpsimd.tensor_tensor(v, v, spread(spread(gain, 4, 1), 2, 1), ALU.mult)\
                        .then_inc(head_normed, 1)

            def root_heads(b):
                pool.wait_ge(o_variance, b + 1)
                r = r16[:, :, 4 * b:4 * b + 4]
                nc.gpsimd.tensor_tensor(r, r, half[:, 0:1].unsqueeze(2).broadcast_to(r.shape), ALU.pow)\
                    .then_inc(o_rstd, 1)

            def gate_heads(b):
                root_heads(b)
                pool.wait_ge(o_rstd, b + 1)
                v = qkv[:, :, 2048 + 512 * b:2560 + 512 * b].rearrange("p t (h d) -> p t h d", h=4)
                link(nc.gpsimd.tensor_tensor(v, v, spread(r16[:, :, 4 * b:4 * b + 4], 128, 3), ALU.mult))
                pool.wait_ge(z_used, 2 * b + 2)
                for n in range(2):
                    o = qkv[:, :, 2048 + 512 * b + 256 * n:2304 + 512 * b + 256 * n]
                    last = nc.gpsimd.tensor_tensor(o, o, z_silu[:, 2 * b + n, :].rearrange("p (t c) -> p t c", t=2),
                                                   ALU.mult)
                last.then_inc(o_normed, 1)

            pre_norm()
            post_norm()
            pre_norm()
            load_post_gain(1)
            for t in range(2):
                power_of(r16[:, t, 0:4], r16[:, t, 0:4])
            post_norm()
            load_post_gain(2)
            pre_norm()
            post_norm()
            pre_norm()
            norm_heads()
            pre_norm()
            pre_norm()
            for j in range(8):
                pool.wait_ge(g_variance, j + 1)
                r = qk_rstd[:, 4 * j:4 * j + 4]
                link(nc.gpsimd.tensor_tensor(r, r, half[:, 0:1].broadcast_to(r.shape), ALU.pow))
                v = qkv[:, :, 256 * j:256 * j + 256].rearrange("p t (h d) -> p t h d", h=2)
                nc.gpsimd.tensor_tensor(v, v, spread(r.rearrange("p (t h) -> p t h", t=2), 128, 3), ALU.mult)        .then_inc(g_normed, 1)
            for b in range(4):
                for t in range(2):
                    pool.wait_ge(d_exp, 2 * b + t + 1)
                    four = level[t][0].rearrange("p (h d) -> p h d", h=4)
                    nc.gpsimd.tensor_tensor(four, four, spread(C("tril"), 4, 1), ALU.mult).then_inc(d_masked, 1)
                for n in range(len(LEVELS)):
                    for t in range(2):
                        if n == 0:
                            pool.wait_ge(d_mats_T, 2 * b + t + 1)
                        if n == 2:
                            pool.wait_ge(d_first, 2 * b + t + 1)
                        if n > 2:
                            pool.wait_ge(d_prod, 12 * b + 2 * (n - 3) + t + 1)
                        nc.gpsimd.tensor_tensor(level[t][n % 2].rearrange("p (h d) -> p h d", h=4),
                                                low_T[t].rearrange("p (h d) -> p h d", h=4), spread(levels[:, n, :], 4, 1),
                                                ALU.mult).then_inc(d_level, 1)
                if b == 0:
                    pool.wait_ge(g_exps, 1)
                else:
                    pool.wait_ge(r_state, b)
                nc.gpsimd.tensor_tensor(k_decayed.rearrange("p (k m c) -> p k m c", k=2, m=2),
                                        spread(qkv[:, 0, 1024 + 256 * b:1280 + 256 * b].rearrange("p (k c) -> p k c", k=2), 2),
                                        spread(decay_rest[:, 4 * b:4 * b + 4].rearrange("p (k m) -> p k m", k=2), 128, 3),
                                        ALU.mult).then_inc(r_keys, 1)
                if b:
                    gate_heads(b - 1)
            root_heads(3)

            pre_norm()

        @block.vector
        def _(dve):
            chain = [0]

            def link(instruction):
                chain[0] += 1
                instruction.then_inc(dve_step, 1)
                dve.wait_ge(dve_step, chain[0])

            def split(i, r=0):
                if i >= N_ITEMS:
                    return
                dve.wait_ge(w_hi_done, i + 1 + 3 * r)
                nc.vector.tensor_tensor(w_lo[:, i % 3, :], raw[:, i % 3, :], w_hi[:, i % 3, :].bitcast(f32),
                                        ALU.subtract).then_inc(w_lo_done, 1)

            powers = [0]

            def power_of(instruction):
                powers[0] += 1
                instruction.then_inc(variance_ready, 1)
                dve.wait_ge(rstd_ready, powers[0])

            def turn_out(name, scale):
                n = TURNS.index(name)
                hi, lo = (hT_hi, hT_lo) if name == "gdn_out1" else (aT_hi, aT_lo)
                for j in range(4):
                    source = bank[j if name == "att_out" else 4 + j]
                    dve.wait_ge(turned_hi, 4 * n + j + 1)
                    for k in range(2):
                        kk = 2 * j + k
                        last = nc.vector.scalar_tensor_tensor(lo[:, kk, :], source[:, 256 * k:256 * k + 256],
                                                              scale(2 * j + k), hi[:, kk, :].bitcast(f32),
                                                              ALU.mult, ALU.subtract)
                    last.then_inc(turned_lo, 1)

            def pre_norm(name):
                n = NORMS.index(name)
                for t in range(2):
                    dve.wait_ge(squares_ready, 2 * n + t + 1)
                    power_of(nc.vector.tensor_scalar(rstd[:, t:t + 1], sumsq[:, t:t + 1], 1.0 / D, EPS,
                                                     ALU.mult, ALU.add))
                    nc.vector.tensor_scalar(xn[:, t, :], x[:, t, :], rstd[:, t:t + 1], None, ALU.mult)\
                        .then_inc(rows_ready, 1)
                if n == 0:
                    split(0)
                turn_out(name, lambda k: gains[:, n, k:k + 1])
                if n == 0:
                    split(1)
                split(FIRST[name] + 2)
                if n == 0:
                    set_up()

            def post_norm(layer, n, factor):
                dve.wait_ge(post_gain_loaded, 16 * (n + 1))
                for t in range(2):
                    dve.wait_ge(y_squares, 4 * n + 2 * t + 2)
                    r = rstd[:, t:t + 1]
                    link(nc.vector.tensor_tensor(r, sumsq[:, 2 * t:2 * t + 1], sumsq[:, 2 * t + 1:2 * t + 2], ALU.add))
                    power_of(nc.vector.tensor_scalar(r, r, 1.0 / D / factor ** 2, EPS / factor ** 2,
                                                     ALU.mult, ALU.add))
                    for h in range(2):
                        c = slice(512 * h, 512 * h + 512)
                        last = nc.vector.scalar_tensor_tensor(xn[:, t, c], bank[2 * t + h][:, :], r, post_gain[:, c],
                                                              ALU.mult, ALU.mult)
                    link(last)
                    nc.vector.tensor_tensor(x[:, t, :], x[:, t, :], xn[:, t, :], ALU.add).then_inc(x_ready, 1)

            def plain_sum(name):
                for t in range(2):
                    if t == 0:
                        dve.wait_ge(y_done, RESULTS.index(name) + 1)
                    else:
                        dve.wait_ge(item_done, FIRST[name] + dict(COUNTS)[name])
                    nc.vector.tensor_tensor(x[:, t, 0:512], x[:, t, 0:512], bank[2 * t][:, :], ALU.add)
                    nc.vector.tensor_tensor(x[:, t, 512:1024], x[:, t, 512:1024], bank[2 * t + 1][:, :], ALU.add)\
                        .then_inc(x_ready, 1)

            def at_tile(table, f, q, tap):
                return table[:, bass.ds(f + 4 * q, 1), tap:tap + 1].rearrange("p a b -> p (a b)")

            def ffn(name):
                n_tiles, conv, f0 = FFNS[name]
                pre_norm(name)
                tap = P("ffn_conv")[:, 72 * (name == "glu2"):72 * (name == "glu2") + 72]
                tap = tap.rearrange("p (f t) -> p f t", t=3)

                def tile(f, i, q):
                    gate, up = bank[4 + f % 4][:, 0:256], bank[4 + f % 4][:, 256:512]
                    g = f_gate[:, f % 2, :]
                    if conv:
                        dve.wait_ge(gate_scaled, f0 - 44 + f + 1 + 4 * q)
                        c0 = 2 * (f0 - 44 + f)
                        nc.vector.scalar_tensor_tensor(g[:, 1:256], gate[:, 0:255], at_tile(tap, f, q, 1),
                                                       g[:, 1:256], ALU.mult, ALU.add).then_inc(conv_step, 1)
                        dve.wait_ge(conv_step, f0 - 44 + f + 1 + 4 * q)
                        nc.vector.scalar_tensor_tensor(g[:, 2:256], gate[:, 0:254], at_tile(tap, f, q, 0),
                                                       g[:, 2:256], ALU.mult, ALU.add).then_inc(gate_conv, 1)
                        gate = g
                    dve.wait_ge(gate_tanh, f0 + f + 1 + 4 * q)
                    nc.vector.scalar_tensor_tensor(f_tanh[:, f % 2, :], f_tanh[:, f % 2, :], 1.0, gate,
                                                   ALU.add, ALU.mult).then_inc(silu_step, 1)
                    dve.wait_ge(silu_step, f0 + f + 1 + 4 * q)
                    nc.vector.scalar_tensor_tensor(f_hid[:, f % 2, :], f_tanh[:, f % 2, :], 0.5, up,
                                                   ALU.mult, ALU.mult).then_inc(hid_ready, 1)
                    split(i + 3, 2 * q)
                    dve.wait_ge(hid_hi, f0 + f + 1 + 4 * q)
                    nc.vector.tensor_tensor(hT_lo[:, f % 4, :], f_hid[:, f % 2, :],
                                            hT_hi[:, f % 4, :].bitcast(f32), ALU.subtract).then_inc(hid_lo, 1)

                def down(m, i, q):
                    if m < n_tiles // 2 - 1:
                        split(i + 3, 2 * q)

                ffn_order(dve, name, tile, down)

            def rope(b, cos, sin):
                v = proj[:, :, 256 * b:256 * b + 256].rearrange("p t (h d) -> p t h d", d=64)
                x1, x2 = v[:, :, :, 0:8], v[:, :, :, 8:16]
                parts = [rot[:, a, 64 * (b % 3):64 * (b % 3) + 64].rearrange("p (t h d) -> p t h d", t=2, d=8) for a in range(4)]
                cos, sin = spread(cos, 4, 2), spread(sin, 4, 2)
                for to, a, c in zip(parts, (x1, x2, x2, x1), (cos, sin, cos, sin)):
                    last = nc.vector.tensor_tensor(to, a, c, ALU.mult)
                link(last)
                nc.vector.tensor_tensor(x1, parts[0], parts[1], ALU.subtract)
                nc.vector.tensor_tensor(x2, parts[2], parts[3], ALU.add).then_inc(heads_ready, 1)

            def mixer_projection():
                table = C("rope").rearrange("p (f t c) -> p f t c", f=2, t=2)
                for p, b in enumerate(MIX_ORDER):
                    split(FIRST["mix_in"] + p + 3)
                    if b < 7:
                        dve.wait_ge(copied, projections(p) + 1)
                        rope(b, table[:, 0], table[:, 1])
                    if p == 0:
                        dve.wait_ge(copied, 1)
                        for t in range(2):
                            last = nc.vector.tensor_copy(
                                mixed[:, 512 * t:512 * t + 512].rearrange("p (a m d) -> p a m d", a=4, m=2),
                                spread(proj[:, t, 2304:2560].rearrange("p (a d) -> p a d", a=4), 2))
                        last.then_inc(c_twice, 1)
                    if p == 1:
                        dve.wait_ge(small_product, 1)
                        nc.vector.tensor_copy(small_T[0:24, :], bank[7][0:24, 0:SEQ]).then_inc(small_copied, 1)
                    if p == 2:
                        compressed_blocks()
                        dve.wait_ge(gates_tanh, 1)
                        link(nc.vector.tensor_scalar(gates, gates, 0.5, 0.5, ALU.mult, ALU.add))
                    if p in (6, 8):
                        kv = (p - 6) // 2
                        dve.wait_ge(item_done, FIRST["mix_in"] + p + 1)
                        nc.vector.tensor_copy(mixed[0:30, 512 + 256 * kv:768 + 256 * kv], bank[kv][0:30, 0:256])\
                            .then_inc(c_rows, 1)
                    if p == 9:
                        compressed_hidden()
                    if p == 10:
                        link(nc.vector.memset(kc_diag, 0.0))
                        dve.wait_ge(c_products, 1)
                        nc.vector.tensor_copy(v_cmp[0:15, :], bank[1][0:15, 0:128]).then_inc(c_values, 1)
                        nc.vector.tensor_copy(kc_diag[0:64, 0, 0:15], bank[0][0:64, 0:15])
                        nc.vector.tensor_copy(kc_diag[64:128, 1, 0:15], bank[0][64:128, 15:30])
                    if p == 11:
                        dve.wait_ge(c_spread, 1)
                        nc.vector.tensor_tensor(v_diag.rearrange("p (g j) d -> p g j d", g=2),
                                                spread(bank[2][:, 0:128].rearrange("p (g d) -> p g d", g=2), 4),
                                                spread(C("own_head").rearrange("p (g j) -> p g j", g=2), 64, 3),
                                                ALU.mult).then_inc(c_operands, 1)
                    if p == 12:
                        compressed_softmax()
                    if p == 14:
                        dve.wait_ge(c_probs_turned, 1)
                        nc.vector.tensor_copy(c_expT, bank[2][:, 0:256].rearrange("p (t c) -> p t c", t=2))\
                            .then_inc(c_probsT, 1)
                    if p == 14:
                        for t in range(2):
                            dve.wait_ge(c_out, t + 1)
                            nc.vector.tensor_tensor(xn[:, t, 512:1024].rearrange("p (h d) -> p h d", h=8),
                                                    bank[(3, 0)[t]][:, :].rearrange("p (h d) -> p h d", h=8),
                                                    spread(coef[:, t, 0:8], 64), ALU.mult).then_inc(c_out_read, 1)

            def attention_projection():
                for p in range(6):
                    if p:
                        dve.wait_ge(head_normed, p)
                        rope(p - 1, cos_sin[:, 0:2, :], cos_sin[:, 2:4, :])
                    if p < 5:
                        dve.wait_ge(head_squares, p + 1)
                        r = head_rstd[:, 8 * p:8 * p + 8]
                        link(nc.vector.tensor_reduce(r, squares_of(p).rearrange("p t (h d) -> p (t h) d", d=64),
                                                     AX.X, ALU.add))
                        nc.vector.tensor_scalar(r, r, 1.0 / 64, EPS, ALU.mult, ALU.add).then_inc(head_sums, 1)
                    split(FIRST["att_in"] + p + 3)

            def attention(layer):
                groups, base = GROUPS[layer], GROUPS_BEFORE[layer]

                def maximum(n):
                    t, h0, count = groups[n]
                    dve.wait_ge(scores_ready, base + n + 1)
                    to = neg_max[:, t, h0:h0 + count]
                    last = nc.vector.tensor_reduce(to, bank[4 + n % 2][:, :].rearrange("p (h c) -> p h c", h=count),
                                                   AX.X, ALU.max, negate=True)
                    if layer == "att_in":
                        link(last)
                        last = nc.vector.tensor_tensor(to, to, neg_sinks[:, h0:h0 + count], ALU.min)
                    last.then_inc(neg_max_ready, 1)
                    if layer == "att_in":
                        dve.wait_ge(neg_max_ready, base + n + 1)
                        nc.vector.tensor_tensor(coef[:, t, 16 + h0:16 + h0 + count], P("sinks")[:, h0:h0 + count],
                                                to, ALU.add).then_inc(sink_args, 1)

                def normalise(n):
                    t, h0, count = groups[n]
                    dve.wait_ge(sink_expo, n + 1)
                    r = coef[:, t, h0:h0 + count]
                    link(nc.vector.tensor_tensor(r, total[:, t, h0:h0 + count], coef[:, t, 16 + h0:16 + h0 + count],
                                                 ALU.add))
                    link(nc.vector.reciprocal(r, r))
                    e = expo[:, n % 2, :].rearrange("p (h c) -> p h c", h=count)
                    nc.vector.tensor_tensor(e, e, spread(r, 512 // count), ALU.mult).then_inc(expo_normed, 1)

                maximum(0)
                maximum(1)
                if layer == "att_in":
                    normalise(0)
                for n, (t, h0, count) in enumerate(groups):
                    dve.wait_ge(expo_turned, base + n + 1)
                    if n >= 2:
                        dve.wait_ge(pv_done, base + n - 1)
                    nc.vector.tensor_copy(expoT[:, n % 2, :], bank[6 + n % 2][:, :]).then_inc(expoT_ready, 1)
                    if layer == "att_in" and n + 1 < len(groups):
                        normalise(n + 1)
                    if n + 2 < len(groups):
                        maximum(n + 2)
                    if layer == "mix_in" and n == len(groups) // 3:
                        mix_finish(0, base + len(groups) // 3)
                    if layer == "mix_in" and n == len(groups) - 3:
                        mix_norm(0)
                if layer == "mix_in":
                    mix_finish(1, base + len(groups))
                    mix_norm(1)

            def mix_finish(t, groups):
                c = coef[:, t, :]
                link(nc.vector.reciprocal(c[:, 0:24], total[:, t, 0:24]))
                g = gates[:, t, :].rearrange("p (h b) -> p h b", b=3)
                nc.vector.tensor_scalar(c[:, 4:8], c[:, 4:8], lam[:, 5:6], None, ALU.mult)
                nc.vector.tensor_tensor(c[:, 8:16], c[:, 8:16], g[:, :, 1], ALU.mult)
                link(nc.vector.tensor_tensor(c[:, 16:24], c[:, 16:24], g[:, :, 2], ALU.mult))
                dve.wait_ge(pv_done, groups)
                parts = [xn[:, t, 0:512], mixed[:, 0:512], mixed[:, 512:1024], window_part]
                for b, to in enumerate(parts):
                    h = 4 if b < 2 else 8
                    first = 4 * b if b < 2 else 8 * b - 8
                    last = nc.vector.tensor_tensor(to.rearrange("p (h d) -> p h d", h=h),
                                                   bank[b][:, :].rearrange("p (h d) -> p h d", h=h),
                                                   spread(c[:, first:first + h], 512 // h), ALU.mult)
                    if b == 1:
                        link(last)
                        nc.vector.tensor_tensor(xn[:, t, 0:512], xn[:, t, 0:512], mixed[:, 0:512], ALU.add)\
                            .then_inc(mix_sum, 1)
                last.then_inc(out_read, 1)
                dve.wait_ge(out_read, t + 1)
                for part in (mixed[:, 512:1024], window_part):
                    link(nc.vector.tensor_tensor(xn[:, t, 512:1024], xn[:, t, 512:1024], part, ALU.add))

            def mix_norm(t):
                o = xn[:, t, 0:512].rearrange("p (h d) -> p h d", h=4)
                r = r16[:, t, 0:4]
                dve.wait_ge(mix_squares, t + 1)
                link(nc.vector.tensor_reduce(r, heads_squared(t).rearrange("p (h d) -> p h d", h=4), AX.X, ALU.add))
                power_of(nc.vector.tensor_scalar(r, r, 1.0 / 128 / 0.64, EPS / 0.64, ALU.mult, ALU.add))
                nc.vector.tensor_tensor(o, o, spread(r, 128), ALU.mult).then_inc(rows_ready, 1)

            def compressed_blocks():
                pe_terms = P("pe").rearrange("p (v l) -> p v l", v=2)
                for kv in range(2):
                    dve.wait_ge(c_copied, kv + 1)
                    sums = c_sums[:, kv, :].rearrange("p (l c) -> p l c", c=32)
                    for g in range(2):
                        view = blockT[:, kv, g, :].rearrange("p (c l) -> p l c", l=16)[:, 0:16:2, :]
                        for part in range(2):
                            term = spread(pe_terms[:, kv, 8 * part:8 * part + 8], 15)
                            last = nc.vector.tensor_tensor(sums[:, 8 * part:8 * part + 8, 15 * g:15 * g + 15],
                                                           view[:, :, part:part + 15], term, ALU.add)
                    link(last)
                    link(nc.vector.tensor_copy(c_block(hT_hi, kv)[:, :, 0:30], sums[:, :, 0:30]))
                    nc.vector.tensor_tensor(c_block(hT_lo, kv)[:, :, 0:30], sums[:, :, 0:30],
                                            c_block(hT_hi, kv)[:, :, 0:30].bitcast(f32), ALU.subtract)                        .then_inc(c_blocks, 1)

            def compressed_hidden():
                dve.wait_ge(c_rows_turned, 1)
                link(nc.vector.tensor_copy(hidden[:, :, 0:30],
                                           bank[2][:, 0:128].rearrange("p (b c) -> p b c", b=4)[:, :, 0:30]))
                x_, y_ = hidden[:, :, 0:30], hidden2[:, :, 0:30]
                link(nc.vector.tensor_tensor(y_, x_, x_, ALU.mult))
                link(nc.vector.tensor_scalar(y_, y_, 0.044715, 1.0, ALU.mult, ALU.add))
                nc.vector.tensor_tensor(y_, y_, x_, ALU.mult).then_inc(c_gelu_arg, 1)
                dve.wait_ge(c_tanh, 1)
                link(nc.vector.scalar_tensor_tensor(y_, y_, 1.0, x_, ALU.add, ALU.mult))
                nc.vector.tensor_scalar(y_, y_, 0.5, None, ALU.mult).then_inc(c_hidden, 1)

            def compressed_softmax():
                valid = C("cmp_valid").rearrange("p (t c) -> p t c", t=2)
                link(nc.vector.tensor_scalar(c_mask, valid, -NEG, NEG, ALU.mult, ALU.add))
                for t in range(2):
                    s = cmp_s[:, t]
                    dve.wait_ge(c_scores, t + 1)
                    link(nc.vector.tensor_tensor(s, bank[t][:, 0:128].rearrange("p (h c) -> p h c", h=8),
                                                 spread(c_mask[:, t, :], 8, 1), ALU.add))
                    m = neg_max[:, t, 24:32]
                    link(nc.vector.tensor_reduce(m, s, AX.X, ALU.max, negate=True))
                    nc.vector.tensor_tensor(s, s, spread(m, 16), ALU.add).then_inc(c_masked, 1)
                for t in range(2):
                    s = cmp_s[:, t]
                    dve.wait_ge(c_expo, t + 1)
                    link(nc.vector.tensor_reduce(total[:, t, 24:32], s, AX.X, ALU.add))
                    nc.vector.tensor_tensor(s, s, spread(valid[:, t, :], 8, 1), ALU.mult).then_inc(c_probs, 1)
                    link(nc.vector.reciprocal(coef[:, t, 24:32], total[:, t, 24:32]))
                    g = gates[:, t, :].rearrange("p (g j b) -> p g j b", g=2, j=4)
                    c = coef[:, t, 0:8].rearrange("p (g j) -> p g j", g=2)
                    link(nc.vector.tensor_tensor(c, coef[:, t, 24:32].rearrange("p (j g) -> p g j", j=4),
                                                 g[:, :, :, 0], ALU.mult))

            def convolved():
                taps = P("gdn_conv").rearrange("p (f t) -> p f t", t=4)
                for k in range(16):
                    dve.wait_ge(g_scaled, k + 1)
                    for back in (1, 2, 3):
                        for n in range(2):
                            to = g_conv[k % 3][:, 256 * n + back:256 * n + 256]
                            last = nc.vector.scalar_tensor_tensor(to, bank[4 + k % 3][:, 256 * n:256 * n + 256 - back],
                                                                  taps[:, 2 * k + n, 3 - back:4 - back], to,
                                                                  ALU.mult, ALU.add)
                        if back < 3:
                            last.then_inc(g_tap, 1)
                            dve.wait_ge(g_tap, 2 * k + back)
                    last.then_inc(g_conv_ready, 1)
                    split(FIRST["gdn_qkv"] + k + 3)
                    dve.wait_ge(g_tanh_ready, k + 1)
                    nc.vector.scalar_tensor_tensor(g_conv[k % 3], g_tanh[k % 2], 1.0, g_conv[k % 3],
                                                   ALU.add, ALU.mult).then_inc(g_silu_ready, 1)
                    if k == 0:
                        dve.wait_ge(small_product, 2)
                        nc.vector.tensor_copy(small_T[0:32, :], bank[7][0:32, 0:SEQ]).then_inc(small_copied, 1)
                    if k == 1:
                        gates_in()
                    if k == 2:
                        gates_out()
                    if k == 4:
                        dve.wait_ge(g_sums, 1)
                        link(nc.vector.tensor_copy(decay_sum, bank[7][:, 0:32].rearrange("p (t h) -> p t h", t=2)))
                        nc.vector.tensor_tensor(decay_rest, bank[7][:, 32:48], decay_sum[:, 0, :], ALU.subtract)\
                            .then_inc(g_sums_read, 1)
                    if 3 <= k < 11:
                        variances(k - 3)
                dve.wait_ge(g_exps, 1)
                link(nc.vector.tensor_tensor(beta_decay, beta[:, 1, :], decay_exp[:, 1, :], ALU.mult))

            def variances(j):
                dve.wait_ge(g_squares, j + 1)
                r = qk_rstd[:, 4 * j:4 * j + 4]
                link(nc.vector.tensor_reduce(r, xn[:, 0, 512 * (j % 2):512 * (j % 2) + 512]
                                             .rearrange("p (a d) -> p a d", d=128), AX.X, ALU.add))
                nc.vector.tensor_scalar(r, r, EPS, 128.0 if j < 4 else 1.0, ALU.add, ALU.mult).then_inc(g_variance, 1)

            def gates_in():
                dve.wait_ge(gates_ready, 2)
                link(nc.vector.tensor_copy(ba, bank[7][:, 0:64].rearrange("p (t c) -> p t c", t=2)))
                link(nc.vector.tensor_tensor(ba[:, :, 16:32], ba[:, :, 16:32], spread(P("dt_bias"), 2, 1), ALU.add))
                link(nc.vector.tensor_scalar(soft[:, :, 0:16], ba[:, :, 16:32], -1.0, None, ALU.mult))
                nc.vector.tensor_tensor(soft[:, :, 0:16], soft[:, :, 0:16], ba[:, :, 16:32], ALU.min)\
                    .then_inc(g_soft_args, 1)
                link(nc.vector.tensor_scalar(ba[:, :, 16:32], ba[:, :, 16:32], 0.0, None, ALU.max))

            def gates_out():
                dve.wait_ge(g_soft_done, 1)
                nc.vector.tensor_scalar(beta, soft[:, :, 16:32], 0.5, 0.5, ALU.mult, ALU.add)
                link(nc.vector.tensor_tensor(decay, ba[:, :, 16:32], soft[:, :, 0:16], ALU.add))
                nc.vector.scalar_tensor_tensor(decay, decay, -1.0, spread(rate, 2, 1), ALU.mult, ALU.mult)\
                    .then_inc(g_decay, 1)

            def split_half(i, h):
                dve.wait_ge(w_hi_done, i + 1)
                at = slice(1024 * h, 1024 * h + 1024)
                last = nc.vector.tensor_tensor(w_lo[:, i % 3, at], raw[:, i % 3, at], w_hi[:, i % 3, at].bitcast(f32),
                                               ALU.subtract)
                if h:
                    last.then_inc(w_lo_done, 1)

            def z_gate(i):
                dve.wait_ge(z_tanh, i + 1)
                nc.vector.scalar_tensor_tensor(z_silu[:, i, :], z_silu[:, i, :], 1.0, bank[3 + 4 * (i % 2)][:, :],
                                               ALU.add, ALU.mult).then_inc(z_used, 1)

            def out_variances(b):
                for t in range(2):
                    dve.wait_ge(o_squares, 2 * b + t + 1)
                    last = nc.vector.tensor_reduce(
                        r16[:, t, 4 * b:4 * b + 4], qkT[:, 8 * t + 2 * b:8 * t + 2 * b + 2, :].rearrange("p a (h d) -> p (a h) d",
                                                                                              d=128), AX.X, ALU.add)
                link(last)
                nc.vector.tensor_scalar(r16[:, :, 4 * b:4 * b + 4], r16[:, :, 4 * b:4 * b + 4], 4.0 / 128, 4.0 * EPS, ALU.mult, ALU.add)\
                    .then_inc(o_variance, 1)

            def delta(b):
                h = 4 * b
                col = [slice(128 * c, 128 * c + 128) for c in range(4)]

                def four(ap):
                    return ap.rearrange("p (h d) -> p h d", h=4)

                v = [qkv[:, t, 2048 + 512 * b:2560 + 512 * b] for t in range(2)]
                if b == 0:
                    dve.wait_ge(g_qk_copied, 8)
                for t in range(2):
                    dve.wait_ge(d_rows, 2 * b + t + 1)
                    for c in range(4):
                        last = nc.vector.tensor_scalar(level[t][0][:, col[c]], bank[4 * t][:, col[c]],
                                                       decay_sum[:, t, h + c:h + c + 1], 0.0, ALU.subtract, ALU.max)
                    last.then_inc(d_diff, 1)
                for t in range(2):
                    dve.wait_ge(d_masked, 2 * b + t + 1)
                    prods = bank[4 * t + 1]
                    for c in range(4):
                        nc.vector.scalar_tensor_tensor(prod[t][:, col[c]], prods[:, col[c // 2]],
                                                       beta[:, t, h + c:h + c + 1], level[t][0][:, col[c]],
                                                       ALU.mult, ALU.mult)
                    pairs = prods[:, 256:512].rearrange("p (k c) -> p k c", k=2)
                    nc.vector.tensor_tensor(inv[t].rearrange("p (k m c) -> p k m c", k=2, m=2), spread(pairs, 2),
                                            level[t][0].rearrange("p (k m c) -> p k m c", k=2, m=2), ALU.mult)\
                        .then_inc(d_mats, 1)
                for t in range(2):
                    last = nc.vector.tensor_tensor(four(v[t]), four(v[t]), spread(beta[:, t, h:h + 4], 128), ALU.mult)
                last.then_inc(r_inputs, 1)
                if b:
                    z_gate(2 * b - 1)
                for t in range(2):
                    dve.wait_ge(d_level, 14 * b + t + 1)
                    nc.vector.tensor_tensor(four(inv_T[t]), spread(ident, 4, 1), four(level[t][0]), ALU.subtract)\
                        .then_inc(d_first, 1)
                for n in range(1, len(LEVELS)):
                    for t in range(2):
                        if n < len(LEVELS) - 1:
                            dve.wait_ge(d_inv_step, 10 * b + 2 * (n - 1) + t + 1)
                            if n == 1:
                                dve.wait_ge(d_first_T, 2 * b + t + 1)
                            nc.vector.tensor_tensor(inv[t], inv[t], bank[4 * t + 2][:, :], ALU.subtract)\
                                .then_inc(d_inv, 1)
                        dve.wait_ge(d_step, 12 * b + 2 * (n - 1) + t + 1)
                        nc.vector.tensor_tensor(inv_T[t], inv_T[t], bank[4 * t + 1][:, :], ALU.subtract)\
                            .then_inc(d_applied, 1)
                    if n in (2, 3) and b:
                        split_half(FIRST["gdn_z"] + 2 * b + 2, n - 2)
                    if n == 4 and b:
                        out_variances(b - 1)
                    if n == 5:
                        z_gate(2 * b)
                        split_half(FIRST["gdn_z"] + 2 * b + 3, 0)
                split_half(FIRST["gdn_z"] + 2 * b + 3, 1)
                dve.wait_ge(r_out, 2 * b + 1)
                nc.vector.tensor_copy(v[0], bank[1][:, :]).then_inc(r_out_read, 1)
                dve.wait_ge(r_read, b + 1)
                link(nc.vector.tensor_tensor(four(prod[1]), four(bank[4][:, :]), spread(beta_decay[:, h:h + 4], 128),
                                             ALU.mult))
                nc.vector.tensor_tensor(v[1], v[1], prod[1], ALU.subtract).then_inc(r_rhs, 1)
                link(nc.vector.tensor_tensor(four(inv[1]), four(bank[5][:, :]), spread(decay_exp[:, 1, h:h + 4], 128),
                                             ALU.mult))
                dve.wait_ge(r_out, 2 * b + 2)
                nc.vector.tensor_tensor(v[1], inv[1], bank[0][:, :], ALU.add).then_inc(r_out_read, 1)

            def set_up():
                dve.wait_ge(setup_hi, 1)
                nc.vector.tensor_tensor(ws_lo[:, :, :], P("small").rearrange("p (k c) -> p k c", c=56),
                                        ws_hi[:, :, :].bitcast(f32), ALU.subtract).then_inc(setup_done, 1)
                dve.wait_ge(con_loaded, 32)
                link(nc.vector.memset(masks[:, :, :], 0.0))
                nc.vector.tensor_copy(ident_b[:, :], ident)
                nc.vector.tensor_copy(masks[:, 0, :].rearrange("p (h c) -> p h c", h=4), spread(C("causal"), 4, 1))
                for m in (1, 2):
                    rows = masks[:, m, :].rearrange("p (h a c) -> p h a c", h=2, a=2)
                    if m == 2:
                        nc.vector.tensor_copy(rows[:, :, 0, :], spread(C("before"), 2, 1))
                    nc.vector.tensor_copy(rows[:, :, 1, :], spread(C("causal"), 2, 1)).then_inc(setup_done, 1)
                dve.wait_ge(par_loaded, 32)
                pairs = P("lambdas").rearrange("p (a b c) -> p a b c", a=2, b=2)
                link(nc.vector.tensor_tensor(mixed[:, 0:128].rearrange("p (a c) -> p a c", a=2), pairs[:, :, 0, :],
                                             pairs[:, :, 1, :], ALU.mult))
                nc.vector.tensor_reduce(lam[:, 0:2], mixed[:, 0:128].rearrange("p (a c) -> p a c", a=2), AX.X, ALU.add)\
                    .then_inc(lam_args, 1)
                link(nc.vector.tensor_copy(pos, pos_i[:, :]))
                for t in range(2):
                    last = nc.vector.tensor_scalar(ang[:, t, 0:8], C("inv_freq"), pos[:, t:t + 1], None, ALU.mult)
                link(last)
                link(nc.vector.tensor_scalar(trig[:, 3, :].rearrange("p (t c) -> p t c", t=2), ang[:, :, 0:8],
                                             0.15915494309189535, 12582912.0, ALU.mult, ALU.add))
                link(nc.vector.tensor_scalar(trig[:, 3, :], trig[:, 3, :], 12582912.0, None, ALU.subtract))
                rest = trig[:, 0, :]
                link(nc.vector.tensor_copy(rest.rearrange("p (t c) -> p t c", t=2), ang[:, :, 0:8]))
                for part in (6.28125, 0.0019350051879882812, 3.019916e-07):
                    link(nc.vector.scalar_tensor_tensor(rest, trig[:, 3, :], -part, rest, ALU.mult, ALU.add))
                nc.vector.tensor_scalar(rest, rest, 3.1415925, -3.1415925, ALU.min, ALU.max).then_inc(trig_args, 1)
                dve.wait_ge(lam_expo, 1)
                link(nc.vector.tensor_tensor(lam[:, 4:5], lam[:, 2:3], lam[:, 3:4], ALU.subtract))
                nc.vector.tensor_scalar(lam[:, 5:6], lam[:, 4:5], -1.0, -0.2, ALU.mult, ALU.add)
                dve.wait_ge(trig_done, 1)
                nc.vector.tensor_copy(cos_sin[:, 2:4, :].rearrange("p a b -> p (a b)"), trig[:, 1, :])
                link(nc.vector.tensor_tensor(trig[:, 3, :], trig[:, 2, :], trig[:, 2, :], ALU.mult))
                nc.vector.tensor_scalar(cos_sin[:, 0:2, :].rearrange("p a b -> p (a b)"), trig[:, 3, :], -2.0, 1.0,
                                        ALU.mult, ALU.add)
                link(nc.vector.tensor_scalar(neg_sinks, P("sinks"), -1.0, None, ALU.mult))

            dve.wait_ge(con_loaded, 16)
            dve.wait_ge(par_loaded, 32)
            ffn("ff1")
            post_norm("ff1", 0, 0.5)
            pre_norm("mix_in")
            mixer_projection()
            attention("mix_in")
            turn_out("mix_out", nsa_scale)
            for i in range(FIRST["mix_out"], FIRST["mix_out"] + 3):
                split(i + 3)
            post_norm("mix_out", 1, 1.0)
            ffn("ff2")
            post_norm("ff2", 2, 0.5)
            pre_norm("att_in")
            attention_projection()
            attention("att_in")
            turn_out("att_out", lambda k: 1.0)
            for i in range(FIRST["att_out"], FIRST["att_out"] + 3):
                split(i + 3)
            plain_sum("att_out")
            ffn("glu1")
            plain_sum("glu1")
            pre_norm("gdn_qkv")
            convolved()
            for b in range(4):
                delta(b)
            z_gate(7)
            out_variances(3)
            dve.wait_ge(o_normed, 2)
            nc.vector.memset(one_s, 1.0).then_inc(rows_ready, 2)
            split(FIRST["gdn_z"] + 10)
            dve.wait_ge(o_rstd, 4)
            v = qkv[:, :, 3584:4096].rearrange("p t (h d) -> p t h d", h=4)
            link(nc.vector.tensor_tensor(v, v, spread(r16[:, :, 12:16], 128, 3), ALU.mult))
            for half_of in range(2):
                o = qkv[:, :, 3584 + 256 * half_of:3840 + 256 * half_of]
                last = nc.vector.tensor_tensor(o, o, z_silu[:, 6 + half_of, :].rearrange("p (t c) -> p t c", t=2), ALU.mult)
            link(last)
            dve.wait_ge(o_normed, 3)
            nc.vector.memset(one_s, 1.0).then_inc(rows_ready, 2)
            turn_out("gdn_out0", lambda k: P("gdn_norm"))
            turn_out("gdn_out1", lambda k: P("gdn_norm"))
            for i in range(FIRST["gdn_out"], FIRST["gdn_out"] + 7):
                split(i + 3)
            plain_sum("gdn_out")
            ffn("glu2")
            plain_sum("glu2")


def _pack_columns(w, blocks):
    k = w.shape[0] // 128
    return w.reshape(k, 128, w.shape[1] // blocks, blocks).transpose(2, 1, 0, 3)


def _ffn_items(w_gate, w_up, w_down):
    gate = _pack_columns(w_gate, 128)
    up = _pack_columns(w_up, 128)
    n = gate.shape[0]
    tiles = [_np.stack([gate[f], up[f]], 1).reshape(128, ITEM) for f in range(n)]
    down = w_down.reshape(n // 2, 2, 128, D).transpose(0, 2, 1, 3).reshape(n // 2, 128, ITEM)
    order = [tiles[0], tiles[1]]
    for m in range(1, n // 2):
        order += [tiles[2 * m], tiles[2 * m + 1], down[m - 1]]
    return order + [down[n // 2 - 1]]


def _column_items(w):
    out = []
    for block in _pack_columns(w, 256):
        for h in range(block.shape[1] // 8):
            out.append(block[:, 8 * h:8 * h + 8].reshape(128, ITEM))
    return out


def _heads(cols, order, size=64):
    return _np.concatenate([cols[:, size * h:size * h + size] for h in order], 1)


def _column(v, n):
    return v.reshape(n, 128).T


def _stream(a):
    w = a["w_in"][0]
    cut = _np.split(w, _np.cumsum([512, 512, 512, 512] + [128] * 6), axis=1)
    dq, dk, dv, nq, kc, vc, ks, vs, kw, vw, gl = cut
    mix = _np.concatenate([dq, dk, _heads(nq, MIX_Q_ORDER), ks, kw, dv, kc, vc, vs, vw], 1)
    att = a["attn_w_in_2"][0]
    att = _np.concatenate([_heads(att[:, :1024], ATT_Q_ORDER), att[:, 1024:]], 1)
    gdn = a["gdn_w_in_2"][0]
    up0, up1 = a["ffn_w_up_2"]
    items = _ffn_items(a["ff1_w_gate"][0], a["ff1_w_up"][0], a["ff1_w_down"][0])
    blocks = _column_items(mix) + _column_items(a["cmp_k_w1"][0]) + _column_items(a["cmp_v_w1"][0])
    items += [blocks[b] for b in MIX_ORDER]
    items += _column_items(a["w_out"][0])
    items += _ffn_items(a["ff2_w_gate"][0], a["ff2_w_up"][0], a["ff2_w_down"][0])
    items += _column_items(att) + _column_items(a["attn_w_out_2"][0])
    items += _ffn_items(up0[:, :3072], up0[:, 3072:], a["ffn_w_down_2"][0])
    items += _column_items(gdn[:, :6144]) + _column_items(a["gdn_w_out_2"][0])
    items += _ffn_items(up1[:, :3072], up1[:, 3072:], a["ffn_w_down_2"][1])
    small = _np.concatenate([gl, gdn[:, 6144:]], 1).reshape(8, 128, 56).transpose(1, 0, 2)
    return _np.stack(items), small.reshape(128, 448)


def _parameters(a, small):
    def rows(v):
        return _np.broadcast_to(v.reshape(1, -1), (128, v.size))

    def taps(w):
        return w.reshape(w.shape[0], -1, 128).transpose(2, 1, 0).reshape(128, -1)

    def pe(v):
        return v.reshape(16, 128).T

    gains = [a["ff1_norm_pre"][0], a["mix_norm_pre"][0], a["ff2_norm_pre"][0], a["mixer_norm_2"][0],
             a["ffn_norm_2"][0], a["mixer_norm_2"][1], a["ffn_norm_2"][1]]
    w2k = a["cmp_k_w2"][0].reshape(2, 128, 1, 64).transpose(1, 0, 2, 3)
    p = {
        "gains": _np.concatenate([_column(g, 8) for g in gains], 1),
        "subln": a["diff_subln"][0].reshape(128, 1),
        "gdn_norm": a["gdn_norm_2"][0].reshape(128, 1),
        "gdn_conv": taps(a["gdn_conv_2"][0]),
        "ffn_conv": _np.concatenate([taps(a["ffn_conv_2"][0]), taps(a["ffn_conv_2"][1])], 1),
        "ffn_bias": _np.concatenate([_column(a["ffn_conv_b_2"][0], 24), _column(a["ffn_conv_b_2"][1], 24)], 1),
        "pe": _np.concatenate([pe(a["cmp_pe_k"][0]), pe(a["cmp_pe_v"][0])], 1),
        "w2k": _np.broadcast_to(w2k, (128, 2, 2, 64)).reshape(128, 256),
        "w2v": a["cmp_v_w2"][0].reshape(2, 128, 64).transpose(1, 0, 2).reshape(128, 128),
        "lambdas": rows(_np.concatenate([a["lambda_q1"], a["lambda_k1"], a["lambda_q2"], a["lambda_k2"]], 1)),
        "qk_gain": rows(_np.concatenate([a["attn_q_gain_2"], a["attn_k_gain_2"]], 1)),
        "sinks": rows(a["attn_sinks_2"][0, ATT_HEADS]),
        "a_log": rows(a["gdn_a_log_2"]),
        "dt_bias": rows(a["gdn_dt_bias_2"]),
        "small": small,
    }
    assert list(p) == list(PARAMS) and all(p[n].shape == (128, PARAMS[n]) for n in p)
    return _np.concatenate(list(p.values()), 1)


def _constants():
    i, j = _np.arange(128)[:, None], _np.arange(128)[None, :]
    f = lambda m: m.astype(_np.float32)
    block = [(i // s != j // s) & (i // (2 * s) == j // (2 * s)) & (i < j) for s in LEVELS]
    t = _np.arange(256).reshape(2, 128).T[:, :, None]
    valid = (_np.arange(16) < 15) & (_np.arange(16) * 16 + 31 <= t)
    inv = 500000.0 ** (-_np.arange(0, 16, 2, dtype=_np.float32) / 16)
    inv = inv.astype(_np.float32)
    angle = t.astype(_np.float32) * inv
    c = {
        "ident": f(i == j),
        "causal": NEG * f(j > i),
        "before": NEG * f(j <= i),
        "upto": f(i <= j),
        "tril": f(j <= i),
        "levels": _np.concatenate([f(b) for b in block], 1),
        "cmp_valid": f(valid).reshape(128, 32),
        "own_head": f(i // 16 == _np.array([2 * (h % 4) + h // 4 for h in range(8)])[None, :]),
        "spread": f((i == j % 16) & (i < 15)),
        "rope": _np.stack([_np.cos(angle), _np.sin(angle)], 1).reshape(128, 32),
        "inv_freq": _np.broadcast_to(inv, (128, 8)),
        "ones": _np.ones((128, 128)),
    }
    assert list(c) == list(CONSTS) and all(c[n].shape == (128, CONSTS[n]) for n in c)
    return _np.concatenate([v.astype(_np.float32) for v in c.values()], 1)


def kernel(**inputs):
    import concourse.bacc as _bacc
    from concourse.bass_utils import run_bass_kernel_spmd as _run

    a = {k: _np.asarray(v) for k, v in inputs.items()}
    stream, small = _stream(a)
    arrays = {
        "weights": stream,
        "params": _parameters(a, small),
        "consts": _constants(),
        "x": a["x"].reshape(SEQ, D),
        "post_gains": _np.concatenate([a["ff1_norm_post"], a["mix_norm_post"], a["ff2_norm_post"]], 0),
        "positions": a["positions_2"].reshape(2, 128).T,
    }
    arrays = {k: _np.ascontiguousarray(v) for k, v in arrays.items()}
    nc = _bacc.Bacc("TRN2", target_bir_lowering=False, num_devices=1)
    ins = {k: nc.dram_tensor(k, v.shape, mybir.dt.from_np(v.dtype), kind="ExternalInput").ap()
           for k, v in arrays.items()}
    out = nc.dram_tensor("out", (SEQ, D), mybir.dt.float32, kind="ExternalOutput").ap()
    two_blocks(nc, ins, out)
    r = _run(nc, [arrays], core_ids=[0])
    return r.results[0]["out"].reshape(1, SEQ, D)
```
